# Optimizing a Trainium2 kernel written in Bass

```python
import math
import jax, jax.numpy as jnp
from jax import lax
import numpy as np

D_MODEL = 1024
BATCH = 1
SEQ = 256
DEPTH = 1
DEC_BATCH = 8
DEC_SEQ = 8
PAST_LEN = 2048
PAGE_SIZE = 128

MIX_WIDTH = D_MODEL
A_WIDTH = MIX_WIDTH // 2
A_HEADS = 4
A_HEAD_DIM = A_WIDTH // A_HEADS
CHUNK = 128
B_WIDTH = MIX_WIDTH - A_WIDTH
SSD_HEAD_DIM = 64
SSD_HEADS = B_WIDTH // SSD_HEAD_DIM
SSD_GROUPS = 2
HEADS_PER_GROUP = SSD_HEADS // SSD_GROUPS
SSD_STATE = 128
CONV_K = 4
CONV_DIM = B_WIDTH + 2 * SSD_GROUPS * SSD_STATE
IN_DIM = 2 * A_WIDTH + B_WIDTH + CONV_DIM + SSD_HEADS
N_EXPERTS = 32
TOP_K = 4
D_FF = D_MODEL
SWIGLU_LIMIT = 7.0
SWIGLU_ALPHA = 1.702
EXPERT_BLOCK = 128
EPS = 1e-6

kernel_name = 'hymba_gmlp_ssd_moe_adaln_step'

def rmsnorm(x, g):
    xf = x.astype(jnp.float32)
    r = xf * lax.rsqrt(jnp.mean(xf * xf, axis=-1, keepdims=True) + EPS)
    return (r * g.astype(jnp.float32)).astype(x.dtype)

def seg_decay(cs):
    n = cs.shape[-1]
    diff = cs[..., :, None] - cs[..., None, :]
    mask = jnp.tril(jnp.ones((n, n), dtype=bool))
    return jnp.exp(jnp.where(mask, diff, -jnp.inf))

def spatial_mix(v, w_s, b_s):
    b, L, nh, hd = v.shape
    cl = CHUNK if L % CHUNK == 0 else L
    mask = jnp.tril(jnp.ones((cl, cl), dtype=bool))
    w = jnp.where(mask, w_s[:, :cl, :cl], 0.0).astype(v.dtype)
    vc = v.reshape(b, L // cl, cl, nh, hd)
    bias = b_s[:, :cl].T.astype(v.dtype)[None, None, :, :, None]
    s = jnp.einsum('hts,bcshd->bcthd', w, vc) + bias
    return s.reshape(b, L, nh, hd)

def causal_conv(xbc, prev, w, bias):
    L = xbc.shape[1]
    xp = jnp.concatenate([prev.astype(xbc.dtype), xbc], axis=1)
    acc = bias
    for k in range(CONV_K):
        acc = acc + xp[:, k:k + L] * w[k]
    return jax.nn.silu(acc), xp[:, L:]

def ssd(x, dt, a, bm, cm, init_state):
    b, L, h, p = x.shape
    cl = CHUNK if L % CHUNK == 0 else L
    nc = L // cl
    f32 = jnp.float32
    xdt = (x.astype(f32) * dt[..., None]).reshape(b, nc, cl, h, p)
    bh = jnp.repeat(bm.astype(f32), HEADS_PER_GROUP, axis=2).reshape(b, nc, cl, h, -1)
    ch = jnp.repeat(cm.astype(f32), HEADS_PER_GROUP, axis=2).reshape(b, nc, cl, h, -1)
    a_cs = jnp.cumsum((dt * a).reshape(b, nc, cl, h).transpose(0, 3, 1, 2), axis=-1)
    scores = jnp.einsum('bclhn,bcshn->bhcls', ch, bh) * seg_decay(a_cs)
    y_diag = jnp.einsum('bhcls,bcshp->bclhp', scores, xdt)
    decay_to_end = jnp.exp(a_cs[..., -1:] - a_cs)
    chunk_states = jnp.einsum('bclhn,bhcl,bclhp->bchpn', bh, decay_to_end, xdt)
    states = jnp.concatenate([init_state.astype(f32)[:, None], chunk_states], axis=1)
    chunk_cs = jnp.cumsum(jnp.pad(a_cs[..., -1], ((0, 0), (0, 0), (1, 0))), axis=-1)
    states = jnp.einsum('bhzc,bchpn->bzhpn', seg_decay(chunk_cs), states)
    y_off = jnp.einsum('bclhn,bchpn,bhcl->bclhp', ch, states[:, :-1], jnp.exp(a_cs))
    y = (y_diag + y_off).reshape(b, L, h, p)
    return y, states[:, -1]

def parallel_mixers(h, ssm0, conv0, lp):
    b, L, _ = h.shape
    proj = h @ lp['w_in']
    cuts = np.cumsum([A_WIDTH, A_WIDTH, B_WIDTH, CONV_DIM]).tolist()
    u_a, v_a, z, xbc, dt_raw = jnp.split(proj, cuts, axis=-1)
    u_a = jax.nn.gelu(u_a, approximate=False)
    v_a = rmsnorm(jax.nn.gelu(v_a, approximate=False).reshape(b, L, A_HEADS, A_HEAD_DIM),
                  lp['g_v_a'].reshape(A_HEADS, A_HEAD_DIM))
    s_a = spatial_mix(v_a, lp['w_spatial'], lp['b_spatial'])
    out_a = rmsnorm(u_a * s_a.reshape(b, L, A_WIDTH), lp['g_out_a'])
    xbc, conv_new = causal_conv(xbc, conv0, lp['conv_w'], lp['conv_b'])
    xs, bm, cm = jnp.split(xbc, [B_WIDTH, B_WIDTH + SSD_GROUPS * SSD_STATE], axis=-1)
    dt = jax.nn.softplus(dt_raw.astype(jnp.float32) + lp['dt_bias'].astype(jnp.float32))
    a = -jnp.exp(lp['a_log'].astype(jnp.float32))
    xs = xs.reshape(b, L, SSD_HEADS, SSD_HEAD_DIM)
    y, ssm_new = ssd(xs, dt, a, bm.reshape(b, L, SSD_GROUPS, SSD_STATE),
                     cm.reshape(b, L, SSD_GROUPS, SSD_STATE), ssm0)
    y = y + xs.astype(jnp.float32) * lp['d_skip'].astype(jnp.float32)[:, None]
    gated = (y.reshape(b, L, B_WIDTH) * jax.nn.silu(z.astype(jnp.float32))).astype(h.dtype)
    out_b = rmsnorm(gated.reshape(b, L, SSD_GROUPS, B_WIDTH // SSD_GROUPS),
                    lp['g_out_b'].reshape(SSD_GROUPS, B_WIDTH // SSD_GROUPS)).reshape(b, L, B_WIDTH)
    out = jnp.concatenate([out_a, out_b], axis=-1) @ lp['w_out']
    return out, ssm_new.astype(ssm0.dtype), conv_new, v_a.reshape(b, L, A_WIDTH)

def moe(h, lp):
    shape = h.shape
    x = h.reshape(-1, D_MODEL)
    T = x.shape[0]
    logits = (x @ lp['w_router'] + lp['b_router']).astype(jnp.float32)
    top_v, top_i = lax.top_k(logits, TOP_K)
    top_w = jax.nn.softmax(top_v, axis=-1).astype(h.dtype)
    n_assign = T * TOP_K
    flat_e = top_i.reshape(n_assign)
    flat_tok = jnp.arange(n_assign, dtype=jnp.int32) // TOP_K
    flat_w = top_w.reshape(n_assign)
    order = jnp.argsort(flat_e)
    sorted_e = flat_e[order]
    counts = jnp.zeros((N_EXPERTS,), jnp.int32).at[flat_e].add(1)
    starts = jnp.cumsum(counts) - counts
    padded = (counts + EXPERT_BLOCK - 1) // EXPERT_BLOCK * EXPERT_BLOCK
    pad_ends = jnp.cumsum(padded)
    pad_starts = pad_ends - padded
    dest = pad_starts[sorted_e] + jnp.arange(n_assign, dtype=jnp.int32) - starts[sorted_e]
    n_blocks = -(-(n_assign + N_EXPERTS * (EXPERT_BLOCK - 1)) // EXPERT_BLOCK)
    n_rows = n_blocks * EXPERT_BLOCK
    row_tok = jnp.full((n_rows,), T, jnp.int32).at[dest].set(flat_tok[order])
    row_w = jnp.zeros((n_rows,), h.dtype).at[dest].set(flat_w[order])
    block_start = jnp.arange(n_blocks, dtype=jnp.int32) * EXPERT_BLOCK
    block_e = jnp.minimum(jnp.searchsorted(pad_ends, block_start, side='right'), N_EXPERTS - 1)
    x_rows = jnp.concatenate([x, jnp.zeros((1, D_MODEL), x.dtype)], axis=0)[row_tok]
    x_rows = x_rows.reshape(n_blocks, EXPERT_BLOCK, D_MODEL)

    def expert_block(args):
        xb, e = args
        g = jnp.minimum(xb @ lp['w_gate'][e] + lp['b_gate'][e], SWIGLU_LIMIT)
        u = jnp.clip(xb @ lp['w_up'][e] + lp['b_up'][e], -SWIGLU_LIMIT, SWIGLU_LIMIT)
        act = g * jax.nn.sigmoid(SWIGLU_ALPHA * g) * (u + 1.0)
        return act @ lp['w_down'][e] + lp['b_down'][e]

    y_rows = lax.map(expert_block, (x_rows, block_e)).reshape(n_rows, D_MODEL) * row_w[:, None]
    out = jax.ops.segment_sum(y_rows, row_tok, num_segments=T + 1)[:T]
    return out.reshape(shape)

def layer(x, c, ssm0, conv0, lp):
    ada = (jax.nn.silu(c) @ lp['w_ada'] + lp['b_ada'])[:, None, :]
    sh_m, sc_m, gt_m, sh_f, sc_f, gt_f = jnp.split(ada, 6, axis=-1)
    h = rmsnorm(x, lp['g_mix']) * (1.0 + sc_m) + sh_m
    mix, ssm_new, conv_new, v_rows = parallel_mixers(h, ssm0, conv0, lp)
    x = x + gt_m * mix
    h = rmsnorm(x, lp['g_ffn']) * (1.0 + sc_f) + sh_f
    x = x + gt_f * moe(h, lp)
    return x, ssm_new, conv_new, v_rows

def setup_inputs(seed: int = 0) -> dict:
    key = jax.random.key(seed)
    ks = jax.random.split(key, 32)
    f32 = jnp.float32

    def nrm(k, shape, scale):
        return jax.random.normal(k, shape, f32) * scale

    L = DEPTH
    dt0 = jnp.exp(jax.random.uniform(ks[14], (L, SSD_HEADS), f32, minval=math.log(1e-3), maxval=math.log(1e-1)))
    return {
        'x_prompt': nrm(ks[0], (BATCH, SEQ, D_MODEL), 1.0),
        'x_sample': nrm(ks[1], (DEC_BATCH, DEC_SEQ, D_MODEL), 1.0),
        'c_prompt': nrm(ks[2], (BATCH, D_MODEL), 1.0),
        'c_sample': nrm(ks[3], (DEC_BATCH, D_MODEL), 1.0),
        'state_ssm': nrm(ks[4], (L, DEC_BATCH, SSD_HEADS, SSD_HEAD_DIM, SSD_STATE), 0.5),
        'state_conv': nrm(ks[5], (L, DEC_BATCH, CONV_K - 1, CONV_DIM), 1.0),
        'w_ada': nrm(ks[6], (L, D_MODEL, 6 * D_MODEL), 0.5 * D_MODEL ** -0.5),
        'b_ada': nrm(ks[7], (L, 6 * D_MODEL), 0.02),
        'g_mix': 1.0 + nrm(ks[8], (L, D_MODEL), 0.1),
        'w_in': nrm(ks[9], (L, D_MODEL, IN_DIM), D_MODEL ** -0.5),
        'g_v_a': 1.0 + nrm(ks[10], (L, A_WIDTH), 0.1),
        'w_spatial': nrm(ks[11], (L, A_HEADS, CHUNK, CHUNK), CHUNK ** -0.5),
        'b_spatial': 1.0 + nrm(ks[12], (L, A_HEADS, CHUNK), 0.1),
        'g_out_a': 1.0 + nrm(ks[13], (L, A_WIDTH), 0.1),
        'conv_w': nrm(ks[15], (L, CONV_K, CONV_DIM), CONV_K ** -0.5),
        'conv_b': nrm(ks[16], (L, CONV_DIM), 0.02),
        'dt_bias': dt0 + jnp.log(-jnp.expm1(-dt0)),
        'a_log': jnp.log(jax.random.uniform(ks[17], (L, SSD_HEADS), f32, minval=1.0, maxval=16.0)),
        'd_skip': 1.0 + nrm(ks[18], (L, SSD_HEADS), 0.1),
        'g_out_b': 1.0 + nrm(ks[19], (L, B_WIDTH), 0.1),
        'w_out': nrm(ks[20], (L, MIX_WIDTH, D_MODEL), MIX_WIDTH ** -0.5),
        'g_ffn': 1.0 + nrm(ks[21], (L, D_MODEL), 0.1),
        'w_router': nrm(ks[22], (L, D_MODEL, N_EXPERTS), D_MODEL ** -0.5),
        'b_router': nrm(ks[23], (L, N_EXPERTS), 0.01),
        'w_gate': nrm(ks[24], (L, N_EXPERTS, D_MODEL, D_FF), D_MODEL ** -0.5),
        'b_gate': nrm(ks[25], (L, N_EXPERTS, D_FF), 0.02),
        'w_up': nrm(ks[26], (L, N_EXPERTS, D_MODEL, D_FF), D_MODEL ** -0.5),
        'b_up': nrm(ks[27], (L, N_EXPERTS, D_FF), 0.02),
        'w_down': nrm(ks[28], (L, N_EXPERTS, D_FF, D_MODEL), D_FF ** -0.5),
        'b_down': nrm(ks[29], (L, N_EXPERTS, D_MODEL), 0.02),
        'g_final': 1.0 + nrm(ks[30], (D_MODEL,), 0.1),
    }

def reference(x_prompt, x_sample, c_prompt, c_sample, state_ssm, state_conv, w_ada, b_ada, g_mix, w_in,
              g_v_a, w_spatial, b_spatial, g_out_a, conv_w, conv_b, dt_bias, a_log, d_skip, g_out_b, w_out,
              g_ffn, w_router, b_router, w_gate, b_gate, w_up, b_up, w_down, b_down, g_final):
    yp, ys = x_prompt, x_sample
    bp = x_prompt.shape[0]
    ssm_p, conv_p, ssm_s, conv_s, v_s = [], [], [], [], []
    for l in range(DEPTH):
        lp = {'w_ada': w_ada[l], 'b_ada': b_ada[l], 'g_mix': g_mix[l], 'w_in': w_in[l], 'g_v_a': g_v_a[l],
              'w_spatial': w_spatial[l], 'b_spatial': b_spatial[l], 'g_out_a': g_out_a[l],
              'conv_w': conv_w[l], 'conv_b': conv_b[l], 'dt_bias': dt_bias[l], 'a_log': a_log[l],
              'd_skip': d_skip[l], 'g_out_b': g_out_b[l], 'w_out': w_out[l], 'g_ffn': g_ffn[l],
              'w_router': w_router[l], 'b_router': b_router[l], 'w_gate': w_gate[l], 'b_gate': b_gate[l],
              'w_up': w_up[l], 'b_up': b_up[l], 'w_down': w_down[l], 'b_down': b_down[l]}
        ssm0 = jnp.zeros((bp, SSD_HEADS, SSD_HEAD_DIM, SSD_STATE), x_prompt.dtype)
        conv0 = jnp.zeros((bp, CONV_K - 1, CONV_DIM), x_prompt.dtype)
        yp, sp_new, cp_new, _ = layer(yp, c_prompt, ssm0, conv0, lp)
        ys, ss_new, cs_new, vs_new = layer(ys, c_sample, state_ssm[l], state_conv[l], lp)
        ssm_p.append(sp_new)
        conv_p.append(cp_new)
        ssm_s.append(ss_new)
        conv_s.append(cs_new)
        v_s.append(vs_new)
    y_prompt = rmsnorm(yp, g_final)
    y_sample = rmsnorm(ys, g_final)
    return (y_prompt, y_sample, jnp.stack(ssm_p), jnp.stack(conv_p), jnp.stack(ssm_s), jnp.stack(conv_s), jnp.stack(v_s))


_drawn_inputs = setup_inputs


def setup_inputs(seed=0):
    import zlib

    import numpy as np

    out = dict(_drawn_inputs(seed))
    spreads = {}
    factors = {'b_spatial': 2.701,
     'd_skip': 7.954,
     'b_router': 6.504,
     'b_gate': 8.0,
     'b_up': 24.016,
     'b_down': 8.0}
    for name, (base, spread) in spreads.items():
        noise = np.random.default_rng([zlib.crc32(name.encode()), seed]).standard_normal(out[name].shape)
        drawn = base * np.exp(spread * noise) if base else spread * noise
        out[name] = __import__('jax').numpy.asarray(drawn.astype(out[name].dtype))
    for name, factor in factors.items():
        out[name] = (out[name] * factor).astype(out[name].dtype)
    return out
```

```python
from contextlib import ExitStack

import numpy as np

import concourse.bass as bass
from concourse import mybir

ALU = mybir.AluOpType
ACT = mybir.ActivationFunctionType
AX = mybir.AxisListType
F32 = mybir.dt.float32
I32 = mybir.dt.int32
U32 = mybir.dt.uint32

P = 128
D = 1024
KC = D // P
TP = 256
NSEQ = 8
SL = 8
TS = NSEQ * SL
T = TP + TS
TILES = [(0, P), (P, P), (TP, TS)]
NT = len(TILES)
AW = 512
AH = 4
H = 8
HD = 64
G = 2
TAPS = 4
PAD = TAPS - 1
CONVW = PAD + TP + NSEQ * (PAD + SL)
CONVN = CONVW - PAD
SEQ0 = PAD + TP
IN_DIM = 2568
NE = 32
TOPK = 4
CAP = 80
PASSES = -(-T // CAP)
MORE = T * TOPK // (CAP + 1)
EPS = 1e-6
LIMIT = 7.0
ALPHA = 1.702

UNIT = 2048
RING = 16
FS = 6
PER = 12
UNROLL = 4


def layout(spec):
    out, at = {}, 0
    for name, width in spec:
        out[name] = (at, width)
        at += width
    return out, at


VEC, VECW = layout([("c", KC * (1 + NSEQ)), ("b_ada", 48), ("g_mix", KC), ("g_ffn", KC), ("g_final", KC),
                    ("g_cat", KC), ("conv_w", TAPS * KC), ("conv_b", KC), ("b_gate", NE * KC), ("b_up", NE * KC),
                    ("b_down", NE * KC), ("w_router", KC * NE), ("w_dt", KC * H), ("w_sp", AH * P),
                    ("b_sp", AH), ("prev", KC * NSEQ * PAD)])
ROW, ROWW = layout([("g_v", AW), ("dt_bias", H), ("a_log", H), ("d_skip", H), ("b_router", NE)])
CON, CONW = layout([("upto", P), ("after", P), ("ident", P), ("ones", P), ("before", P), ("upto_s", TS),
                    ("after_s", TS), ("seq", NSEQ), ("rep", TS), ("iota", 96), ("thr", PASSES - 1), ("eidx", P)])


def constants():
    k = np.arange(P)[:, None]
    m = np.arange(P)[None, :]
    out = np.zeros((P, CONW), np.float32)

    def put(name, a):
        at = CON[name][0]
        out[:a.shape[0], at:at + a.shape[1]] = a

    ks, ms = k[:TS], m[:, :TS]
    same = ks // SL == ms // SL
    put("upto", (k <= m).astype(np.float32))
    put("after", (k > m).astype(np.float32))
    put("ident", (k == m).astype(np.float32))
    put("ones", np.ones((P, P), np.float32))
    put("before", (k < m).astype(np.float32))
    put("upto_s", ((ks <= ms) & same).astype(np.float32))
    put("after_s", ((ks > ms) & same).astype(np.float32))
    put("seq", (ks // SL == np.arange(NSEQ)[None, :]).astype(np.float32))
    put("rep", (np.arange(SL)[:, None] == ms % SL).astype(np.float32))
    put("iota", np.broadcast_to(np.arange(96, dtype=np.float32), (P, 96)))
    put("thr", np.broadcast_to(CAP * np.arange(1, PASSES, dtype=np.float32), (P, PASSES - 1)))
    put("eidx", np.broadcast_to(np.arange(NE, dtype=np.float32)[:, None], (NE, P)))
    return out


FRONT = ([("ada0", j) for j in range(4)] + [("ada1", j) for j in range(4)] + [("xbc", j) for j in range(4)]
         + [("uv", j) for j in range(4)] + [("z", j) for j in range(2)] + [("ada2", j) for j in range(4)]
         + [("ada3", j) for j in range(4)] + [("out", j) for j in range(4)] + [("ada4", j) for j in range(4)]
         + [("ada5", j) for j in range(4)])
FIRST = {}
for _u, (_m, _j) in enumerate(FRONT):
    FIRST.setdefault(_m, _u)
NF = len(FRONT)
SH_M, SC_M, GT_M, SH_F, SC_F, GT_F = range(6)


class Steps:

    def __init__(self, eng, sem):
        self.eng, self.sem, self.count, self.n = eng, sem, 0, 0

    def __call__(self, ins):
        self.count = self.count + 1
        self.n += 1
        ins.then_inc(self.sem, 1)
        self.eng.wait_ge(self.sem, self.count)


def wait(eng, sem, count):
    if not (isinstance(count, int) and count == 0):
        eng.wait_ge(sem, count)


def turns(engine_loop, body):
    body(0)
    with engine_loop(1, NE // UNROLL) as i:
        body(i)


def build(nc, d, out):
    with ExitStack() as ctx:
        arena = ctx.enter_context(nc.sbuf_tensor("arena", [P, 53208], F32))
        used = [0]

        def view(at, shape, rows=P):
            n = int(np.prod(shape))
            ap = arena[0:rows, at:at + n]
            if len(shape) == 2:
                ap = ap.rearrange("p (a b) -> p a b", a=shape[0])
            if len(shape) == 3:
                ap = ap.rearrange("p (a b c) -> p a b c", a=shape[0], b=shape[1])
            return ap

        def sb(shape):
            at = used[0]
            used[0] += -(-int(np.prod(shape)) // 8) * 8
            assert used[0] <= 53208, used[0]
            return view(at, shape), at

        ring, ring_at = sb([RING, UNIT])
        vec, _ = sb([VECW])
        row, _ = sb([ROWW])
        con, _ = sb([CONW])
        xT, _ = sb([KC, T])
        hT, moe_at = sb([KC, T])
        line, work_at = sb([KC, CONVW])
        catT = hT
        acc, acc_at = sb([KC, T])
        sq = acc
        Lx = view(acc_at, [H, P])
        sel_l = view(acc_at + H * P, [H, P])
        junk, _ = view(acc_at + 2 * H * P, [AW]), 0
        cat, cat_at = sb([NT, D])
        htok = cat
        cacc = view(cat_at, [2, CONVN])
        vsq = view(cat_at, [NT, AW])
        small = {}

        def tiny(name, shape):
            small[name], _ = sb(shape)
            return small[name]

        csil = tiny("csil", [KC, 1 + NSEQ])
        ada = tiny("ada", [6, KC, 1 + NSEQ])
        gain = tiny("gain", [KC, 1 + NSEQ])
        rstd = tiny("rstd", [T])
        dtx = tiny("dtx", [NT, H])
        dtr = tiny("dtr", [NT, H])
        dte = tiny("dte", [NT, H])
        dtu = tiny("dtu", [NT, H])
        dt = tiny("dt", [NT, H])
        dta = tiny("dta", [NT, H])
        ea = tiny("ea", [H])
        dseq = tiny("dseq", [NSEQ, H])
        dec = tiny("dec", [P])
        ssv = tiny("ssv", [NT, AH])
        ss9 = tiny("ss9", [3, NT])
        wblk = tiny("wblk", [AH, TS])
        bsp = tiny("bsp", [NT, AH])
        tmp64 = tiny("tmp64", [TS])
        cnew = tiny("cnew", [KC, PAD * (1 + NSEQ)])
        mdec = view(work_at, [H, P])
        xdt = view(work_at + H * P, [NT, AW])
        at = moe_at
        moe = {"sel": sb([NT, CAP])[0], "selw": sb([NT, CAP])[0]}
        for name, shape in [("g", [KC, CAP]), ("s", [KC, CAP]), ("u", [KC, CAP]), ("a", [KC, CAP]), ("X", [KC, CAP]),
                            ("yT", [KC, CAP]), ("y", [D]), ("selT", [T])]:
            moe[name] = view(at, shape)
            at += int(np.prod(shape))
        assert at <= work_at + KC * CONVW
        logit, rt_at = sb([NT, NE])
        top, _ = sb([NT, 8])
        topi, _ = sb([NT, 8])
        topf, _ = sb([NT, 8])
        topw, _ = sb([NT, 8])
        den, _ = sb([NT])
        picked, _ = sb([NT, NE])
        rank, _ = sb([NE + 1, NT])
        wgt, _ = sb([NE + 1, NT])
        rk_more, _ = sb([NT])
        flag, _ = sb([PASSES - 1])
        place, _ = sb([PASSES - 1])
        oh, _ = sb([PASSES - 1, 16])
        ohb, _ = sb([PASSES - 1, 16])
        more_f, _ = sb([3, 16])
        more_i = sb([3, 16])[0].bitcast(I32)
        onehot = view(acc_at, [NT * TOPK, NE])
        onew = view(acc_at + NT * TOPK * NE, [NT * TOPK, NE])
        up = [ring_at + FS * UNIT]

        def scratch(shape):
            n = int(np.prod(shape))
            at = up[0]
            up[0] += n
            assert up[0] <= ring_at + RING * UNIT
            return view(at, shape)

        xbcT = scratch([KC, T])
        btok = scratch([NT, G * P])
        s0T = scratch([NSEQ, AW])
        cmask = scratch([G, NSEQ * (TS + SL)])
        bmask = scratch([G, NSEQ, P])
        snew = scratch([2, AW])
        st0 = scratch([AW])
        st1 = scratch([AW])
        xw = scratch([NT, AW])
        xs = scratch([NT, AW])
        zs = scratch([NT, AW])
        ug = scratch([NT, AW])
        vg = scratch([NT, AW])
        gm = view(moe_at, [G, P])

        ps = ctx.enter_context(nc.psum_tensor("ps", [P, 8, 512], F32))
        block_sems = {}

        def sem(name):
            if name not in block_sems:
                block_sems[name] = ctx.enter_context(nc.semaphore(name))
            return block_sems[name]

        def vc(name, shape=None, rows=P):
            a, w = VEC[name]
            ap = vec[0:rows, a:a + w]
            return ap if shape is None else ap.rearrange("p (a b) -> p a b", a=shape)

        def cn(name, rows=P, width=None):
            a, w = CON[name]
            return con[0:rows, a:a + (width or w)]

        def rw(name, rows=P):
            a, w = ROW[name]
            return row[0:rows, a:a + w]

        def wide(ap, axis, n):
            shape = list(ap.shape)
            ap = ap.unsqueeze(axis)
            shape.insert(axis, n)
            return ap.to_broadcast(shape)

        conv_w = vc("conv_w", TAPS)
        conv_b = vc("conv_b")
        b_exp = {n: vc(n, NE) for n in ("b_gate", "b_up", "b_down")}
        bada = vc("b_ada", 6)
        w_router = vc("w_router", KC)
        w_dt = vc("w_dt", KC)
        w_sp = vc("w_sp", AH)
        prev = vc("prev", KC * NSEQ)

        def upto(t):
            return cn("upto") if t < 2 else cn("upto_s", TS)

        def after(t):
            return cn("after") if t < 2 else cn("after_s", TS)

        def line_seq(m, first, n):
            return line[:, m, SEQ0:CONVW].rearrange("p (b w) -> p b w", w=PAD + SL)[:, :, first:first + n]

        ld_x, ld_vec, ld_row, ld_con, ld_s0 = (sem(n) for n in ("ld_x", "ld_vec", "ld_row", "ld_con", "ld_s0"))
        front_landed = [sem(f"front_landed{i}") for i in range(FS)]
        front_used = sem("front_used")
        exp_landed = [sem(f"exp_landed{i}") for i in range(RING)]
        exp_used = sem("exp_used")
        x_sq, meansq, var_ready, root_ready, xn_ready = (sem(n) for n in ("x_sq", "meansq", "var_ready", "root_ready", "xn_ready"))
        c_ready, ada_mm, ada_ready, gain_ready = (sem(n) for n in ("c_ready", "ada_mm", "ada_ready", "gain_ready"))
        hp_ready, hs_ready = sem("hp_ready"), sem("hs_ready")
        rep_mm, rep_read = sem("rep_mm"), sem("rep_read")
        line_ready, xbc_mm, xbc_line, conv_begun, conv_done, xbc_ready = (
            sem(n) for n in ("line_ready", "xbc_mm", "xbc_line", "conv_begun", "conv_done", "xbc_ready"))
        dt_mm, dt_abs, dt_exp, dt_one, dt_ln, dta_ready = (
            sem(n) for n in ("dt_mm", "dt_abs", "dt_exp", "dt_one", "dt_ln", "dta_ready"))
        uv_mm, gelu_done, z_mm, z_silu = (sem(n) for n in ("uv_mm", "gelu_done", "z_mm", "z_silu"))
        v_ready, s_mm, s_read, ga_ready, ga_sq = (sem(n) for n in ("v_ready", "s_mm", "s_read", "ga_ready", "ga_sq"))
        xb_tr, xb_tok, decay_mm, decays = (sem(n) for n in ("xb_tr", "xb_tok", "decay_mm", "decays"))
        sl_ready, l_mm, lx_ready, g_mm, gm_ready, m_ready = (
            sem(n) for n in ("sl_ready", "l_mm", "lx_ready", "g_mm", "gm_ready", "m_ready"))
        xdt_ready, xw_ready, skip_ready, cmask_ready, bmask_ready = (
            sem(n) for n in ("xdt_ready", "xw_ready", "skip_ready", "cmask_ready", "bmask_ready"))
        y_mm, y_read, gb_ready, gb_sq, st_mm, st0_ready, st1_ready = (
            sem(n) for n in ("y_mm", "y_read", "gb_ready", "gb_sq", "st_mm", "st0_ready", "st1_ready"))
        sn_mm, sn_copied, sn_added = sem("sn_mm"), sem("sn_copied"), sem("sn_added")
        cat_ready, cat_tr, catT_ready, out_mm, x1_ready, x1_sq = (
            sem(n) for n in ("cat_ready", "cat_tr", "catT_ready", "out_mm", "x1_ready", "x1_sq"))
        h_tr, htok_ready, router_mm, picks_ready, rank_mm, route_ready = (
            sem(n) for n in ("h_tr", "htok_ready", "router_mm", "picks_ready", "rank_mm", "route_ready"))
        soft_in, soft_out, cnt_mm, place_mm, oh_ready, more_mm, more_ready, rank_read, place_read, more_read, flag_ready = (
            sem(n) for n in ("soft_in", "soft_out", "cnt_mm", "place_mm", "oh_ready", "more_mm", "more_ready",
                             "rank_read", "place_read", "more_read", "flag_ready"))
        moe_zero = sem("moe_zero")
        sel_ready, selw_ready, x_mm, x_copied, g_ready, sig_ready, g_read, act_ready, y_ready = (
            sem(n) for n in ("sel_ready", "selw_ready", "x_mm", "x_copied", "g_ready", "sig_ready", "g_read",
                             "act_ready", "y_ready"))
        y_tr, y_tok, selT_tr, selT_ready, comb_mm, comb_added = (
            sem(n) for n in ("y_tr", "y_tok", "selT_tr", "selT_ready", "comb_mm", "comb_added"))
        f_sq_in, f_sq, yfin = sem("f_sq_in"), sem("f_sq"), sem("yfin")
        st_v, st_conv, st_ssmp, st_ssms, st_y = (sem(n) for n in ("st_v", "st_conv", "st_ssmp", "st_ssms", "st_y"))
        pool_zero = sem("pool_zero")
        dve_steps, act_steps, pool_steps = sem("dve_steps"), sem("act_steps"), sem("pool_steps")

        w_in = d["w_in"].rearrange("(c p) n -> p c n", p=P)
        w_ada = d["w_ada"].rearrange("(c p) n -> p c n", p=P)
        w_out = d["w_out"].rearrange("(c p) n -> p c n", p=P)
        w_exp = [d[n].rearrange("e (c p) n -> e p c n", p=P) for n in ("w_gate", "w_up", "w_down")]

        def front_source(m, j):
            if m.startswith("ada"):
                s = int(m[3:])
                return w_ada[:, 2 * j:2 * j + 2, s * D:(s + 1) * D]
            if m == "xbc":
                return w_in[:, 2 * j:2 * j + 2, 3 * AW:3 * AW + D]
            if m == "uv":
                return w_in[:, 2 * j:2 * j + 2, 0:2 * AW]
            if m == "z":
                return w_in[:, 4 * j:4 * j + 4, 2 * AW:3 * AW]
            return w_out[:, 2 * j:2 * j + 2, :]

        def exp_slot(j, k):
            return (FS + PER * j + k) % RING

        block = ctx.enter_context(nc.Block())

        @block.sync
        def _(sp):
            sp.dma_start(xT, d["xT"].rearrange("(c p) t -> p c t", p=P)).then_inc(ld_x, 16)
            sp.dma_start(con, d["con"]).then_inc(ld_con, 16)
            sp.dma_start(vec, d["vec"]).then_inc(ld_vec, 16)
            for u, (m, j) in enumerate(FRONT):
                if u >= FS:
                    sp.wait_ge(front_used, u - FS + 1)
                slot = ring[:, u % FS, :]
                src = front_source(m, j)
                sp.dma_start(slot.rearrange("p (c n) -> p c n", c=src.shape[1]), src).then_inc(front_landed[u % FS], 16)
                if u == FS - 1:
                    sp.dma_start(row, d["row"].broadcast_to([P, ROWW])).then_inc(ld_row, 16)
                    sp.dma_start(s0T, d["s0T"]).then_inc(ld_s0, 16)

            def load_unit(e, k, slot):
                src = w_exp[k // 4][bass.ds(e, 1), :, 2 * (k % 4):2 * (k % 4) + 2, :].rearrange("e p c n -> p (e c) n")
                sp.dma_start(ring[:, slot, :].rearrange("p (c n) -> p c n", c=2), src).then_inc(exp_landed[slot], 16)

            for v in range(PER * UNROLL):
                if v == 0:
                    sp.wait_ge(cat_ready, NT)
                    sp.wait_ge(sn_added, NSEQ)
                    sp.wait_ge(st_v, 16)
                    sp.wait_ge(st_ssmp, 16)
                    sp.wait_ge(st_ssms, 16)
                elif RING - FS <= v < RING:
                    last = max(u for u in range(NF) if u % FS == v - (RING - FS))
                    sp.wait_ge(front_used, last + 1)
                elif v >= RING:
                    sp.wait_ge(exp_used, v - RING + 1)
                load_unit(v // PER, v % PER, (FS + v) % RING)
            with sp.Fori(1, NE // UNROLL) as i:
                for j in range(UNROLL):
                    for k in range(PER):
                        v = PER * j + k
                        sp.wait_ge(exp_used, i * (PER * UNROLL) + (v - RING + 1))
                        load_unit(i * UNROLL + j, k, exp_slot(j, k))

            sp.wait_ge(more_ready, 1)
            with sp.Fori(0, MORE) as i:
                there = sp.value_load(more_i[0:1, 2, bass.ds(i, 1)], min_val=0, max_val=1)
                with sp.If(there == 1):
                    e = sp.value_load(more_i[0:1, 0, bass.ds(i, 1)], min_val=0, max_val=NE - 1)
                    for k in range(PER):
                        sp.wait_ge(exp_used, i * PER + NE * PER)
                        load_unit(e, k, exp_slot(0, k))
            sp.wait_ge(yfin, KC)
            sp.dma_start(out["yT"].rearrange("(c p) t -> p c t", p=P), hT).then_inc(st_y, 16)
            sp.wait_ge(st_y, 16)
            sp.wait_ge(st_conv, 16)

        @block.tensor
        def _(pe):
            def mm(o, l, r, start=True, stop=True):
                return pe.matmul(o, l, r, start=start, stop=stop, skip_group_check=True)

            def landed(u):
                pe.wait_ge(front_landed[u % FS], 16 * (u // FS + 1))

            def unit(u, c=2):
                return ring[:, u % FS, :].rearrange("p (c n) -> p c n", c=c)

            def mean_square(bank):
                for k in range(KC):
                    last = mm(ps[:, bank, 0:T], cn("ones"), sq[:, k, :], k == 0, k == KC - 1)
                last.then_inc(meansq, 1)

            def ada_section(s, bank):
                if s == 0:
                    pe.wait_ge(c_ready, 1)
                for j in range(4):
                    u = FIRST[f"ada{s}"] + j
                    landed(u)
                    for kk in range(2):
                        k = 2 * j + kk
                        for m in range(KC):
                            last = mm(ps[:, bank, m * 9:m * 9 + 9], unit(u)[:, kk, m * P:(m + 1) * P], csil[:, k, :],
                                      k == 0 and m == 0, k == KC - 1)
                    last.then_inc(front_used, 1)
                mm(ps[0:1, bank, 511:512], cn("ones")[:, 0:1], cn("ones")[:, 0:1], False, True).then_inc(ada_mm, 1)

            pe.wait_ge(ld_con, 16)
            pe.wait_ge(ld_vec, 16)
            for h in range(AH):
                mm(ps[0:TS, 3, h * SL:(h + 1) * SL], cn("rep", SL), w_sp[0:SL, h, 0:SL])
            mm(ps[0:TS, 3, 64:64 + AH], cn("rep", SL), vc("b_sp")[0:SL, :]).then_inc(rep_mm, 1)
            pe.wait_ge(x_sq, 1)
            mean_square(0)
            ada_section(SH_M, 1)
            ada_section(SC_M, 2)
            pe.wait_ge(hp_ready, 1)
            pe.wait_ge(hs_ready, 1)
            for j in range(4):
                landed(FIRST["xbc"] + j)
            for i in range(KC):
                m = (i + 4) % KC
                if i >= 2:
                    pe.wait_ge(xbc_line, i - 1)
                for k in range(KC):
                    u = FIRST["xbc"] + k // 2
                    last = mm(ps[:, 6 + i % 2, 0:T], unit(u)[:, k % 2, m * P:(m + 1) * P], hT[:, k, :], k == 0, k == KC - 1)
                    if i == KC - 1 and k % 2 == 1 and k < KC - 1:
                        last.then_inc(front_used, 1)
                    if k == KC - 1:
                        last.then_inc(xbc_mm, 1)
            pe.wait_ge(xbc_line, KC - 1)
            for t, (t0, n) in enumerate(TILES):
                for k in range(KC):
                    last = mm(ps[0:n, 6, t * H:(t + 1) * H], hT[:, k, t0:t0 + n], w_dt[:, k, :], k == 0, k == KC - 1)
                    if t == 0 and k == 0:
                        last.then_inc(front_used, 1)
            last.then_inc(dt_mm, 1)
            pe.wait_ge(xn_ready, 1)
            pe.wait_ge(ada_ready, 2)
            for j in range(4):
                u = FIRST["uv"] + j
                landed(u)
                for kk in range(2):
                    k = 2 * j + kk
                    for half in (1, 0):
                        for t, (t0, n) in enumerate(TILES):
                            last = mm(ps[0:n, 3 * half + t, :], hT[:, k, t0:t0 + n],
                                      unit(u)[:, kk, half * AW:(half + 1) * AW], k == 0, k == KC - 1)
                            if k == KC - 1 and not (half == 0 and t == NT - 1):
                                last.then_inc(uv_mm, 1)
                last.then_inc(front_used, 1)
            pe.wait_ge(dta_ready, 1)
            pe.wait_ge(xbc_line, KC)
            pe.wait_ge(gelu_done, 1)
            for j in range(2):
                u = FIRST["z"] + j
                landed(u)
                for kk in range(4):
                    k = 4 * j + kk
                    for t, (t0, n) in enumerate(TILES):
                        last = mm(ps[0:n, (6, 7, 3)[t], :], hT[:, k, t0:t0 + n], unit(u, 4)[:, kk, :], k == 0, k == KC - 1)
                        if k == KC - 1 and t < NT - 1:
                            last.then_inc(z_mm, 1)
                last.then_inc(front_used, 1)
            pe.wait_ge(gelu_done, 2)
            ada_section(GT_M, 4)
            pe.wait_ge(xbc_ready, KC)
            pe.wait_ge(gelu_done, 6)
            for t, (t0, n) in enumerate(TILES):
                if t:
                    pe.wait_ge(xb_tok, t)
                for m in range(4):
                    pe.transpose(ps[0:n, 1, m * P:(m + 1) * P], xbcT[:, m, t0:t0 + n], cn("ident"))
                for g in range(G):
                    last = pe.transpose(ps[0:n, 2, g * P:(g + 1) * P], xbcT[:, 4 + g, t0:t0 + n], cn("ident"))
                last.then_inc(xb_tr, 1)
            for t, (t0, n) in enumerate(TILES):
                mm(ps[0:n, 0, 2 * t * H:(2 * t + 1) * H], after(t), dta[0:n, t, :])
                mm(ps[0:n, 0, (2 * t + 1) * H:(2 * t + 2) * H], upto(t), dta[0:n, t, :])
            mm(ps[:, 0, 6 * H:7 * H], cn("ones"), dta[:, 1, :])
            mm(ps[:, 0, 64:64 + NSEQ * H].rearrange("p (b h) -> p b h", b=NSEQ), cn("ones", TS), dseq[0:TS]).then_inc(decay_mm, 1)
            pe.wait_ge(z_silu, NT)

            def decay_and_scores(t):
                t0, n = TILES[t]
                pe.wait_ge(sl_ready, t + 1)
                if t:
                    pe.wait_ge(lx_ready, t)
                    pe.wait_ge(gm_ready, t)
                for h in range(H):
                    last = mm(ps[0:n, 6 + h // 4, (h % 4) * P:(h % 4) * P + n], sel_l[0:n, h, 0:n], upto(t))
                last.then_inc(l_mm, 1)
                for g in range(G):
                    last = mm(ps[0:n, 5, g * P:g * P + n], xbcT[:, 4 + g, t0:t0 + n], xbcT[:, 6 + g, t0:t0 + n])
                last.then_inc(g_mm, 1)

            def spatial(t):
                n = TILES[t][1]
                if t == 0:
                    pe.wait_ge(v_ready, 1)
                else:
                    pe.wait_ge(s_read, t)
                for h in range(AH):
                    w = w_sp[:, h, :] if t < 2 else wblk[0:TS, h, :]
                    last = mm(ps[0:n, 3, h * P:(h + 1) * P], w, vg[0:n, t, h * P:(h + 1) * P])
                last.then_inc(s_mm, 1)

            decay_and_scores(0)
            spatial(0)
            decay_and_scores(1)
            spatial(1)
            spatial(2)
            ada_section_wait = 3
            pe.wait_ge(ada_ready, ada_section_wait)
            ada_section(SH_F, 4)

            def y_diag(t):
                n = TILES[t][1]
                pe.wait_ge(m_ready, t + 1)
                for h in range(H):
                    last = mm(ps[0:n, 1, h * HD:(h + 1) * HD], mdec[0:n, h, 0:n], xdt[0:n, t, h * HD:(h + 1) * HD])
                return last

            pe.wait_ge(xdt_ready, 1)
            pe.wait_ge(xb_tok, NT)
            y_diag(0).then_inc(y_mm, 1)
            pe.wait_ge(decays, 1)
            pe.wait_ge(xw_ready, 1)
            for g in range(G):
                last = mm(ps[:, 0, g * 256:(g + 1) * 256], btok[:, 0, g * P:(g + 1) * P], xw[:, 0, g * 256:(g + 1) * 256])
            last.then_inc(st_mm, 1)
            pe.wait_ge(st0_ready, 1)
            for g in range(G):
                mm(ps[:, 2, g * 256:(g + 1) * 256], xbcT[:, 6 + g, P:2 * P], st0[:, g * 256:(g + 1) * 256])
            pe.wait_ge(y_read, 1)
            y_diag(1).then_inc(y_mm, 1)
            for g in range(G):
                last = mm(ps[:, 0, g * 256:(g + 1) * 256], btok[:, 1, g * P:(g + 1) * P], xw[:, 1, g * 256:(g + 1) * 256])
            last.then_inc(st_mm, 1)
            decay_and_scores(2)
            pe.wait_ge(ld_s0, 16)
            pe.wait_ge(cmask_ready, 1)
            pe.wait_ge(y_read, 2)
            for g in range(G):
                for b in range(NSEQ):
                    mm(ps[0:TS, 2, g * 256:(g + 1) * 256], cmask[:, g, b * TS:(b + 1) * TS],
                       s0T[:, b, g * 256:(g + 1) * 256], b == 0, b == NSEQ - 1)
            y_diag(2).then_inc(y_mm, 1)
            pe.wait_ge(bmask_ready, 1)
            pe.wait_ge(gm_ready, NT)
            pe.wait_ge(lx_ready, NT)
            for b in range(NSEQ):
                if b >= 2:
                    pe.wait_ge(sn_copied, b - 1)
                for g in range(G):
                    last = mm(ps[:, 5 + b % 2, g * 256:(g + 1) * 256], bmask[0:TS, g, b, :], xw[0:TS, 2, g * 256:(g + 1) * 256])
                last.then_inc(sn_mm, 1)
            pe.wait_ge(ada_ready, 4)
            pe.wait_ge(s_read, NT)
            for t, (t0, n) in enumerate(TILES):
                pe.wait_ge(cat_ready, t + 1)
                if t:
                    pe.wait_ge(catT_ready, t)
                for m in range(KC):
                    last = pe.transpose(ps[:, 3 + m // 4, (m % 4) * P:(m % 4) * P + n], cat[0:n, t, m * P:(m + 1) * P],
                                        cn("ident", n, n))
                last.then_inc(cat_tr, 1)
            pe.wait_ge(catT_ready, NT)
            pe.wait_ge(sn_copied, NSEQ)
            for j in range(4):
                landed(FIRST["out"] + j)
            for m in range(KC):
                if m >= 2:
                    pe.wait_ge(x1_ready, m - 1)
                for k in range(KC):
                    last = mm(ps[:, 6 + m % 2, 0:T], unit(FIRST["out"] + k // 2)[:, k % 2, m * P:(m + 1) * P], catT[:, k, :],
                              k == 0, k == KC - 1)
                    if m == KC - 1 and k % 2 == 1 and k < KC - 1:
                        last.then_inc(front_used, 1)
                last.then_inc(out_mm, 1)
            pe.wait_ge(st1_ready, 1)
            mm(ps[0:1, 0, 0:1], cn("ones")[:, 0:1], cn("ones")[:, 0:1]).then_inc(front_used, 1)
            ada_section(SC_F, 0)
            pe.wait_ge(y_read, NT)
            ada_section(GT_F, 1)
            pe.wait_ge(x1_sq, KC)
            mean_square(2)
            pe.wait_ge(hp_ready, 2)
            pe.wait_ge(hs_ready, 2)
            for t, (t0, n) in enumerate(TILES):
                for k in range(KC):
                    last = mm(ps[0:n, 7, t * NE:(t + 1) * NE], hT[:, k, t0:t0 + n], w_router[:, k, :], k == 0, k == KC - 1)
            last.then_inc(router_mm, 1)
            for t, (t0, n) in enumerate(TILES):
                if t:
                    pe.wait_ge(htok_ready, t)
                for k in range(KC):
                    last = pe.transpose(ps[0:n, 3 + k // 4, (k % 4) * P:(k % 4 + 1) * P], hT[:, k, t0:t0 + n], cn("ident"))
                last.then_inc(h_tr, 1)
            pe.wait_ge(picks_ready, 1)
            for t, (t0, n) in enumerate(TILES):
                for s in range(t + 1):
                    last = mm(ps[0:n, 2, t * NE:(t + 1) * NE], cn("before" if s == t else "ones", n if s == t else P, n),
                              picked[0:TILES[s][1], s, :], s == 0, s == t)
            last.then_inc(rank_mm, 1)
            for t, (t0, n) in enumerate(TILES):
                last = mm(ps[0:NE, 5, 0:1], picked[0:n, t, :], cn("ones", n, 1), t == 0, t == NT - 1)
            last.then_inc(cnt_mm, 1)
            pe.wait_ge(flag_ready, 1)
            nf = PASSES - 1
            mm(ps[0:NE, 5, 8:8 + nf], cn("before", NE, NE), flag[0:NE, :], True, False)
            for p in range(1, nf):
                last = mm(ps[0:NE, 5, 8 + p:8 + nf], cn("ones", NE, NE), flag[0:NE, 0:nf - p], False, p == nf - 1)
            last.then_inc(place_mm, 1)
            pe.wait_ge(oh_ready, 1)
            for q, (l, r) in enumerate([(cn("eidx", NE), oh), (cn("ones", NE), ohb), (cn("ones", NE), oh)]):
                for p in range(nf):
                    last = mm(ps[:, 5, 32 + 16 * q:48 + 16 * q], l, r[0:NE, p, :], p == 0, p == nf - 1)
            last.then_inc(more_mm, 1)

            X, A = moe["X"], moe["a"]

            def halves(bank, rows=P):
                return [ps[0:rows, bank + m // 4, (m % 4) * CAP:(m % 4 + 1) * CAP] for m in range(KC)]

            def gather(x):
                pe.wait_ge(sel_ready, x + 1)
                o = halves(6)
                for m in range(KC):
                    for t, (t0, n) in enumerate(TILES):
                        last = mm(o[m], htok[0:n, t, m * P:(m + 1) * P], moe["sel"][0:n, t, :], t == 0, t == NT - 1)
                last.then_inc(x_mm, 1)

            def product(bank, rhs, slots, turn):
                o = halves(bank)
                for q in range(4):
                    pe.wait_ge(exp_landed[slots[q]], turn[q])
                    w = ring[:, slots[q], :].rearrange("p (c n) -> p c n", c=2)
                    for kk in range(2):
                        k = 2 * q + kk
                        for m in range(KC):
                            last = mm(o[m], w[:, kk, m * P:(m + 1) * P], rhs[:, k, :], k == 0 and m % 4 == 0, k == KC - 1)
                    if kk == 1:
                        last.then_inc(exp_used, 1)

            def turn_y(y):
                wait(pe, y_ready, y)
                for m in range(KC):
                    last = pe.transpose(ps[0:CAP, m // 4, (m % 4) * P:(m % 4 + 1) * P], moe["yT"][:, m, :], cn("ident"))
                last.then_inc(y_tr, 1)

            def combine(y):
                pe.wait_ge(y_tok, y + 1)
                wait(pe, selT_ready, y)
                wait(pe, comb_added, y * KC)
                for m in range(KC):
                    bank = (3, 6, 7)[m % 3]
                    if m >= 3:
                        pe.wait_ge(comb_added, y * KC + (m - 2))
                    mm(ps[:, bank, 0:T], moe["y"][0:CAP, m * P:(m + 1) * P], moe["selT"][0:CAP, :]).then_inc(comb_mm, 1)

            def turn_sel(n):
                pe.wait_ge(selw_ready, n + 1)
                for t, (t0, r) in enumerate(TILES):
                    last = pe.transpose(ps[0:CAP, 2, t0:t0 + r], moe["selw"][0:r, t, :], cn("ident", r, r))
                last.then_inc(selT_tr, 1)

            pe.wait_ge(more_read, 1)
            pe.wait_ge(htok_ready, NT)
            pe.wait_ge(ada_ready, 6)
            gather(0)

            def expert(n, slots, loads, pipelined):
                y, x = (n, n + 1) if pipelined else (n + 1, n + 1)
                pe.wait_ge(x_copied, x if pipelined else x + 1)
                wait(pe, y_tok, n if pipelined else n + 1)
                product(0, X, slots[0:4], loads[0:4])
                wait(pe, selT_ready, n)
                wait(pe, comb_added, y * KC)
                product(2, X, slots[4:8], loads[4:8])
                if pipelined:
                    pe.wait_ge(g_read, n + 1)
                    turn_y(y)
                    gather(x)
                pe.wait_ge(act_ready, n + 1)
                wait(pe, y_ready, n)
                product(4, A, slots[8:12], loads[8:12])

            def pe_turn(i):
                for j in range(UNROLL):
                    n = i * UNROLL + j
                    slots = [exp_slot(j, k) for k in range(PER)]
                    loads = [i * 48 + 16 * ((PER * j + k) // RING + 1) for k in range(PER)]
                    expert(n, slots, loads, True)
                    pe.wait_ge(x_copied, n + 2)
                    combine(n)
                    turn_sel(n)

            turns(pe.Fori, pe_turn)
            turn_y(NE)
            combine(NE)

            with pe.Fori(0, MORE) as i:
                there = pe.value_load(more_i[0:1, 2, bass.ds(i, 1)], min_val=0, max_val=1)
                with pe.If(there == 1):
                    pe.wait_ge(comb_added, (i + (NE + 1)) * KC)
                    gather(i + (NE + 1))
                    n = i + NE
                    slots = [exp_slot(0, k) for k in range(PER)]
                    loads = [i * 16 + 16 * (NE * PER // RING + 1)] * PER
                    expert(n, slots, loads, False)
                    turn_sel(n)
                    turn_y(i + (NE + 1))
                    combine(i + (NE + 1))
            pe.wait_ge(f_sq, KC)
            mean_square(0)

        @block.scalar
        def _(act):
            A = nc.scalar.activation
            step = Steps(act, act_steps)

            def root(k, ap):
                act.wait_ge(var_ready, k)
                A(ap, ap, ACT.Sqrt).then_inc(root_ready, 1)

            def modulate(k, shift):
                act.wait_ge(xn_ready, k)
                act.wait_ge(gain_ready, k)
                for m in range(KC):
                    last = A(hT[:, m, 0:TP], hT[:, m, 0:TP], ACT.Identity, bias=ada[:, shift, m, 0:1], scale=gain[:, m, 0:1])
                last.then_inc(hp_ready, 1)

            act.wait_ge(ld_vec, 16)
            A(csil, vc("c", KC), ACT.Silu).then_inc(c_ready, 1)
            root(1, rstd)
            modulate(1, SH_M)

            def conv_out(i):
                m = (i + 4) % KC
                act.wait_ge(conv_done, i + 1)
                c = cacc[:, i % 2, :]
                A(xbcT[:, m, 0:TP], c[:, 0:TP], ACT.Silu)
                for b0, nb in ((0, NSEQ - 1), (NSEQ - 1, 1)):
                    at = SEQ0 + b0 * (PAD + SL)
                    if nb > 1:
                        src = c[:, at:at + nb * (PAD + SL)].rearrange("p (b w) -> p b w", w=PAD + SL)[:, :, 0:SL]
                    else:
                        src = c[:, at:at + SL].rearrange("p (b w) -> p b w", b=1)
                    last = A(xbcT[:, m, TP + b0 * SL:TP + (b0 + nb) * SL].rearrange("p (b w) -> p b w", w=SL), src, ACT.Silu)
                last.then_inc(xbc_ready, 1)

            act.wait_ge(line_ready, 1)
            for i in range(KC):
                m = (i + 4) % KC
                act.wait_ge(xbc_mm, i + 1)
                A(line[:, m, PAD:SEQ0], ps[:, 6 + i % 2, 0:TP], ACT.Copy)
                A(line_seq(m, PAD, SL), ps[:, 6 + i % 2, TP:T].rearrange("p (b w) -> p b w", w=SL), ACT.Copy).then_inc(xbc_line, 1)
                act.wait_ge(xbc_line, i + 1)
                if i >= 2:
                    act.wait_ge(xbc_ready, i - 1)
                A(cacc[:, i % 2, :], line[:, m, 0:CONVN], ACT.Identity, bias=conv_b[:, m:m + 1],
                  scale=conv_w[:, 0, m:m + 1]).then_inc(conv_begun, 1)
                if i:
                    conv_out(i - 1)
            conv_out(KC - 1)
            for q, (dst, half) in enumerate([(vg, 1), (ug, 0)]):
                for t, (t0, n) in enumerate(TILES):
                    if q == 0 or t < NT - 1:
                        act.wait_ge(uv_mm, 3 * q + t + 1)
                    else:
                        act.wait_ge(front_used, FIRST["uv"] + 4)
                    A(dst[0:n, t, :], ps[0:n, 3 * half + t, :], ACT.Gelu).then_inc(gelu_done, 1)
            act.wait_ge(ld_row, 16)
            A(ea, rw("a_log"), ACT.Exp)
            act.wait_ge(dt_abs, 1)
            A(dte, dte, ACT.Exp, scale=-1.0).then_inc(dt_exp, 1)
            act.wait_ge(dt_one, 1)
            A(dtx, dtu, ACT.Ln).then_inc(dt_ln, 1)
            root(2, ssv)
            for t, (t0, n) in enumerate(TILES):
                if t < NT - 1:
                    act.wait_ge(z_mm, t + 1)
                else:
                    act.wait_ge(front_used, FIRST["z"] + 2)
                A(zs[0:n, t, :], ps[0:n, (6, 7, 3)[t], :], ACT.Silu).then_inc(z_silu, 1)
            for t, (t0, n) in enumerate(TILES):
                act.wait_ge(xb_tr, t + 1)
                A(xs[0:n, t, :], ps[0:n, 1, :], ACT.Copy)
                A(btok[0:n, t, :], ps[0:n, 2, 0:G * P], ACT.Copy).then_inc(xb_tok, 1)
            act.wait_ge(decay_mm, 1)
            A(dec[:, 0:4 * H], ps[:, 0, 0:4 * H], ACT.Exp)
            A(dec[0:TS, 4 * H:6 * H], ps[0:TS, 0, 4 * H:6 * H], ACT.Exp)
            A(dec[:, 6 * H:7 * H], ps[:, 0, 6 * H:7 * H], ACT.Exp)
            A(dec[:, 64:128], ps[:, 0, 64:128], ACT.Exp).then_inc(decays, 1)

            def decay_exp(t):
                n = TILES[t][1]
                act.wait_ge(l_mm, t + 1)
                if t:
                    act.wait_ge(m_ready, t)
                for q in range(2):
                    last = A(Lx[0:n, 4 * q:4 * q + 4, 0:n],
                             ps[0:n, 6 + q, :].rearrange("p (h l) -> p h l", h=4)[:, :, 0:n], ACT.Exp)
                last.then_inc(lx_ready, 1)

            decay_exp(0)
            decay_exp(1)
            act.wait_ge(st_mm, 1)
            A(st0, ps[:, 0, :], ACT.Copy).then_inc(st0_ready, 1)
            decay_exp(2)
            for t, (t0, n) in enumerate(TILES):
                act.wait_ge(ga_ready, t + 1)
                step(A(junk[0:n, :], cat[0:n, t, 0:AW], ACT.Square, accum_out=ss9[0:n, 0, t:t + 1]))
            for t, (t0, n) in enumerate(TILES):
                act.wait_ge(gb_ready, t + 1)
                for g in range(G):
                    step(A(junk[0:n, 0:256], cat[0:n, t, AW + g * 256:AW + (g + 1) * 256], ACT.Square,
                           accum_out=ss9[0:n, 1 + g, t:t + 1]))
            act.wait_ge(act_steps, step.count)
            A(tmp64[0:1, 0:1], ss9[0:1, 0, 0:1], ACT.Copy).then_inc(gb_sq, 1)
            root(3, ss9)
            for b in range(NSEQ):
                act.wait_ge(sn_mm, b + 1)
                if b >= 2:
                    act.wait_ge(sn_added, b - 1)
                A(snew[:, b % 2, :], ps[:, 5 + b % 2, :], ACT.Copy).then_inc(sn_copied, 1)
            for m in range(KC):
                act.wait_ge(x1_ready, m + 1)
                A(sq[:, m, :], xT[:, m, :], ACT.Square).then_inc(x1_sq, 1)
            root(4, rstd)
            modulate(2, SH_F)
            for t, (t0, n) in enumerate(TILES):
                act.wait_ge(h_tr, t + 1)
                A(htok[0:n, t, :].rearrange("p (a b) -> p a b", a=2), ps[0:n, 3:5, :], ACT.Copy).then_inc(htok_ready, 1)
            act.wait_ge(soft_in, 1)
            A(topw[:, :, 0:TOPK], topw[:, :, 0:TOPK], ACT.Exp).then_inc(soft_out, 1)

            def blocks(bank, rows=P):
                return ps[0:rows, bank:bank + 2, 0:4 * CAP]

            def copy_x(x):
                act.wait_ge(x_mm, x + 1)
                A(moe["X"].rearrange("p (a m) c -> p a (m c)", a=2), blocks(6), ACT.Copy).then_inc(x_copied, 1)

            def sigmoid(n):
                act.wait_ge(g_ready, n + 1)
                A(moe["s"], moe["g"], ACT.Sigmoid, scale=ALPHA).then_inc(sig_ready, 1)

            def copy_y(y):
                act.wait_ge(y_tr, y + 1)
                A(moe["y"][0:CAP].rearrange("p (a b) -> p a b", a=2), ps[0:CAP, 0:2, :], ACT.Copy).then_inc(y_tok, 1)

            def copy_sel(n):
                act.wait_ge(selT_tr, n + 1)
                act.wait_ge(comb_mm, (n + 1) * KC)
                A(moe["selT"][0:CAP, :], ps[0:CAP, 2, 0:T], ACT.Copy).then_inc(selT_ready, 1)

            copy_x(0)

            def act_turn(i):
                for j in range(UNROLL):
                    n = i * UNROLL + j
                    wait(act, act_ready, n)
                    sigmoid(n)
                    copy_y(n)
                    act.wait_ge(exp_used, n * PER + 8)
                    copy_x(n + 1)
                    copy_sel(n)

            turns(act.Fori, act_turn)
            copy_y(NE)
            with act.Fori(0, MORE) as i:
                there = act.value_load(more_i[0:1, 2, bass.ds(i, 1)], min_val=0, max_val=1)
                with act.If(there == 1):
                    copy_x(i + (NE + 1))
                    sigmoid(i + NE)
                    copy_sel(i + NE)
                    copy_y(i + (NE + 1))
            for m in range(KC):
                act.wait_ge(f_sq_in, m + 1)
                A(sq[:, m, :], xT[:, m, :], ACT.Square).then_inc(f_sq, 1)
            root(5, rstd)

        @block.vector
        def _(dve):
            V = nc.vector
            step = Steps(dve, dve_steps)

            def tt(o, a, b, op):
                return V.tensor_tensor(o, a, b, op)

            def inverse_root(k, o, src, n):
                V.tensor_scalar(o, src, 1.0 / n, EPS, ALU.mult, ALU.add).then_inc(var_ready, 1)
                dve.wait_ge(root_ready, k)
                step(V.reciprocal(o, o))

            def ada_rows(s, bank):
                dve.wait_ge(ada_mm, ada_rows.n + 1)
                ada_rows.n += 1
                tt(ada[:, s], ps[:, bank, 0:KC * 9].rearrange("p (m b) -> p m b", m=KC), wide(bada[:, s, :], 2, 9),
                   ALU.add).then_inc(ada_ready, 1)

            ada_rows.n = 0

            def gains(k, s, g):
                dve.wait_ge(ada_ready, {SC_M: 2, SC_F: 5}[s])
                V.scalar_tensor_tensor(gain, ada[:, s], 1.0, wide(vc(g), 2, 9), ALU.add, ALU.mult).then_inc(gain_ready, 1)
                dve.wait_ge(gain_ready, k)

            def by_seq(ap):
                return ap[:, :, TP:T].rearrange("p c (b j) -> p c b j", b=NSEQ)

            def modulate_sample(k, s):
                dve.wait_ge(xn_ready, k)
                step(tt(by_seq(hT), by_seq(hT), wide(gain[:, :, 1:9], 3, SL), ALU.mult))
                tt(by_seq(hT), by_seq(hT), wide(ada[:, s, :, 1:9], 3, SL), ALU.add).then_inc(hs_ready, 1)

            def normed(k, bank):
                dve.wait_ge(meansq, k)
                inverse_root({1: 1, 2: 4}[k], rstd, ps[:, bank, 0:T], D)
                tt(hT, xT, wide(rstd, 1, KC), ALU.mult).then_inc(xn_ready, 1)

            dve.wait_ge(ld_x, 16)
            tt(sq, xT, xT, ALU.mult).then_inc(x_sq, 1)
            step(V.memset(dtx, 0.0))
            step(V.memset(ssv, 0.0))
            step(V.memset(ss9, 0.0))
            step(V.memset(logit, 0.0))
            step(V.memset(rank, -1.0))
            step(V.memset(wgt, 0.0))
            dve.wait_ge(rep_mm, 1)
            dve.wait_ge(ld_con, 16)
            dve.wait_ge(ld_vec, 16)
            step(tt(w_sp, w_sp, wide(cn("upto"), 1, AH), ALU.mult))
            for h in range(AH):
                tt(wblk[0:TS, h, :].rearrange("p (b j) -> p b j", b=NSEQ), wide(ps[0:TS, 3, h * SL:(h + 1) * SL], 1, NSEQ),
                   cn("upto_s", TS).rearrange("p (b j) -> p b j", b=NSEQ), ALU.mult)
            for t in range(2):
                V.tensor_copy(bsp[:, t, :], vc("b_sp"))
            V.tensor_copy(bsp[0:TS, 2, :], ps[0:TS, 3, 64:64 + AH]).then_inc(rep_read, 1)
            normed(1, 0)
            ada_rows(SH_M, 1)
            ada_rows(SC_M, 2)
            gains(1, SC_M, "g_mix")
            modulate_sample(1, SH_M)
            for i in range(KC):
                m = (i + 4) % KC
                dve.wait_ge(conv_begun, i + 1)
                c = cacc[:, i % 2, :]
                for k in range(1, TAPS):
                    ins = V.scalar_tensor_tensor(c, line[:, m, k:k + CONVN], conv_w[:, k, m:m + 1], c, ALU.mult, ALU.add)
                    if k < TAPS - 1:
                        step(ins)
                ins.then_inc(conv_done, 1)
            dve.wait_ge(dt_mm, 1)
            dve.wait_ge(ld_row, 16)
            step(tt(dtx[:, 0:2, :], ps[:, 6, 0:2 * H].rearrange("p (t h) -> p t h", t=2), wide(rw("dt_bias"), 1, 2), ALU.add))
            step(tt(dtx[0:TS, 2, :], ps[0:TS, 6, 2 * H:3 * H], rw("dt_bias", TS), ALU.add))
            step(V.tensor_scalar(dtr, dtx, 0.0, None, ALU.max))
            V.scalar_tensor_tensor(dte, dtx, -1.0, dtx, ALU.mult, ALU.max).then_inc(dt_abs, 1)
            dve.wait_ge(dt_exp, 1)
            V.tensor_scalar(dtu, dte, 1.0, None, ALU.add).then_inc(dt_one, 1)
            dve.wait_ge(dt_one, 1)
            step(V.scalar_tensor_tensor(dt, dtu, -1.0, dte, ALU.add, ALU.subtract))
            step(tt(dt, dtr, dt, ALU.subtract))
            dve.wait_ge(dt_ln, 1)
            step(tt(dt, dt, dtx, ALU.add))
            step(V.scalar_tensor_tensor(dta, dt, -1.0, wide(ea, 1, NT), ALU.mult, ALU.mult))
            tt(dseq[0:TS], wide(dta[0:TS, 2, :], 1, NSEQ), wide(cn("seq", TS), 2, H), ALU.mult).then_inc(dta_ready, 1)
            dve.wait_ge(dta_ready, 1)

            def decay_sel(t):
                n = TILES[t][1]
                if t:
                    dve.wait_ge(l_mm, t)
                tt(sel_l[0:n, :, 0:n], wide(after(t), 1, H), wide(dta[0:n, t, :], 2, n), ALU.mult).then_inc(sl_ready, 1)

            decay_sel(0)
            dve.wait_ge(gelu_done, 3)
            both = slice(0, 2)
            step(tt(vsq[:, both], vg[:, both], vg[:, both], ALU.mult))
            step(tt(vsq[0:TS, 2], vg[0:TS, 2], vg[0:TS, 2], ALU.mult))
            step(V.tensor_reduce(ssv[:, both].rearrange("p t h -> p (t h)"), vsq[:, both].rearrange("p t (h e) -> p (t h) e", h=AH), AX.X, ALU.add))
            step(V.tensor_reduce(ssv[0:TS, 2], vsq[0:TS, 2].rearrange("p (h e) -> p h e", h=AH), AX.X, ALU.add))
            inverse_root(2, ssv, ssv, P)
            for rows, ts, n in ((P, both, 2), (TS, slice(2, 3), 1)):
                v4 = vg[0:rows, ts].rearrange("p t (h e) -> p (t h) e", h=AH)
                step(tt(v4, v4, wide(ssv[0:rows, ts].rearrange("p t h -> p (t h)"), 2, P), ALU.mult))
                ins = tt(vg[0:rows, ts], vg[0:rows, ts], wide(rw("g_v", rows), 1, n), ALU.mult)
                if n == 2:
                    step(ins)
            ins.then_inc(v_ready, 1)

            def scores(t):
                n = TILES[t][1]
                dve.wait_ge(g_mm, t + 1)
                tt(gm[0:n, :, 0:n], ps[0:n, 5, 0:G * P].rearrange("p (g l) -> p g l", g=G)[:, :, 0:n], wide(upto(t), 1, G),
                   ALU.mult).then_inc(gm_ready, 1)
                dve.wait_ge(gm_ready, t + 1)
                dve.wait_ge(lx_ready, t + 1)
                if t:
                    dve.wait_ge(y_mm, t)
                for g in range(G):
                    ins = tt(mdec[0:n, 4 * g:4 * g + 4, 0:n], Lx[0:n, 4 * g:4 * g + 4, 0:n], wide(gm[0:n, g, 0:n], 1, 4), ALU.mult)
                ins.then_inc(m_ready, 1)

            def gate_a(t):
                n = TILES[t][1]
                dve.wait_ge(s_mm, t + 1)
                dst = cat[0:n, t, 0:AW]
                tt(dst.rearrange("p (h e) -> p h e", h=AH), ps[0:n, 3, :].rearrange("p (h e) -> p h e", h=AH),
                   wide(bsp[0:n, t, :], 2, P), ALU.add).then_inc(s_read, 1)
                dve.wait_ge(s_read, t + 1)
                tt(dst, dst, ug[0:n, t, :], ALU.mult).then_inc(ga_ready, 1)

            def heads(ap):
                return ap.rearrange("p (h e) -> p h e", h=H)

            def weight_x(t):
                n = TILES[t][1]
                step(tt(heads(xdt[0:n, t, :]), heads(xs[0:n, t, :]), wide(dt[0:n, t, :], 2, HD), ALU.mult))
                ins = tt(heads(xw[0:n, t, :]), heads(xdt[0:n, t, :]), wide(dec[0:n, 2 * t * H:(2 * t + 1) * H], 2, HD), ALU.mult)
                if t < NT - 1:
                    step(ins)
                else:
                    ins.then_inc(xw_ready, 1)

            dve.wait_ge(gelu_done, 6)
            ada_rows(GT_M, 4)
            gate_a(0)
            dve.wait_ge(xb_tok, NT)
            dve.wait_ge(decays, 1)
            dve.wait_ge(st_conv, 16)
            for t in range(NT):
                weight_x(t)
            V.memset(tmp64[0:1, 0:1], 0.0).then_inc(xdt_ready, 1)
            scores(0)
            decay_sel(1)
            gate_a(1)
            gate_a(2)
            ada_rows(SH_F, 4)

            def y_out(t):
                n = TILES[t][1]
                dve.wait_ge(skip_ready, NT)
                dve.wait_ge(y_mm, t + 1)
                dst = cat[0:n, t, AW:D]
                if t:
                    step(tt(heads(xs[0:n, t, :]), heads(ps[0:n, 2, :]),
                            wide(dec[0:n, (2 * t + 1) * H:(2 * t + 2) * H], 2, HD), ALU.mult))
                    step(tt(dst, dst, xs[0:n, t, :], ALU.add))
                tt(dst, dst, ps[0:n, 1, :], ALU.add).then_inc(y_read, 1)
                dve.wait_ge(y_read, t + 1)
                tt(dst, dst, zs[0:n, t, :], ALU.mult).then_inc(gb_ready, 1)

            scores(1)
            decay_sel(2)
            y_out(0)
            y_out(1)
            scores(2)
            dve.wait_ge(st0_ready, 1)
            step(tt(heads(st1), heads(st0), wide(dec[:, 6 * H:7 * H], 2, HD), ALU.mult))
            dve.wait_ge(st_mm, 2)
            tt(st1, st1, ps[:, 0, :], ALU.add).then_inc(st1_ready, 1)
            y_out(2)
            dve.wait_ge(gb_sq, 1)
            step(V.tensor_scalar(ss9[:, 0, :], ss9[:, 0, :], 0.5, None, ALU.mult))
            inverse_root(3, ss9, ss9, 256)
            for t, (t0, n) in enumerate(TILES):
                V.tensor_scalar(cat[0:n, t, 0:AW], cat[0:n, t, 0:AW], ss9[0:n, 0, t:t + 1], None, ALU.mult)
                for g in range(G):
                    part = cat[0:n, t, AW + g * 256:AW + (g + 1) * 256]
                    ins = V.tensor_scalar(part, part, ss9[0:n, 1 + g, t:t + 1], None, ALU.mult)
                ins.then_inc(cat_ready, 1)
            for t, (t0, n) in enumerate(TILES):
                dve.wait_ge(cat_tr, t + 1)
                for q in range(2):
                    ins = tt(catT[:, 4 * q:4 * q + 4, t0:t0 + n],
                             ps[:, 3 + q, :].rearrange("p (m l) -> p m l", m=4)[:, :, 0:n],
                             wide(vc("g_cat")[:, 4 * q:4 * q + 4], 2, n), ALU.mult)
                ins.then_inc(catT_ready, 1)
            dve.wait_ge(ada_ready, 3)

            def residual(m, src, gate, done):
                step(V.scalar_tensor_tensor(xT[:, m, 0:TP], src[:, 0:TP], ada[:, gate, m, 0:1], xT[:, m, 0:TP], ALU.mult, ALU.add))
                step(tt(tmp64.rearrange("p (b j) -> p b j", b=NSEQ), src[:, TP:T].rearrange("p (b j) -> p b j", b=NSEQ),
                        wide(ada[:, gate, m, 1:9], 2, SL), ALU.mult))
                tt(xT[:, m, TP:T], xT[:, m, TP:T], tmp64, ALU.add).then_inc(done, 1)
                return

            for m in range(KC):
                dve.wait_ge(out_mm, m + 1)
                residual(m, ps[:, 6 + m % 2, 0:T], GT_M, x1_ready)
            ada_rows(SC_F, 0)
            ada_rows(GT_F, 1)
            gains(2, SC_F, "g_ffn")
            dve.wait_ge(x1_ready, KC)
            normed(2, 2)
            modulate_sample(2, SH_F)
            dve.wait_ge(router_mm, 1)
            step(tt(logit[:, 0:2, :], ps[:, 7, 0:2 * NE].rearrange("p (t e) -> p t e", t=2), wide(rw("b_router"), 1, 2), ALU.add))
            step(tt(logit[0:TS, 2, :], ps[0:TS, 7, 2 * NE:3 * NE], rw("b_router", TS), ALU.add))
            for t in range(NT):
                step(V.max(top[:, t, :], logit[:, t, :]))
                step(V.max_index(topi[:, t, :].bitcast(U32), top[:, t, :], logit[:, t, :]))
            step(V.tensor_copy(topf, topi.bitcast(U32)))
            tt(topw[:, :, 0:TOPK], top[:, :, 0:TOPK], top[:, :, 0:1].to_broadcast([P, NT, TOPK]), ALU.subtract).then_inc(soft_in, 1)
            for t in range(NT):
                ins = tt(onehot[:, t * TOPK:(t + 1) * TOPK, :], wide(cn("iota", P, NE), 1, TOPK),
                         wide(topf[:, t, 0:TOPK], 2, NE), ALU.is_equal)
                step(ins)
            picked2 = picked
            V.tensor_reduce(picked2, onehot.rearrange("p (t k) e -> p t e k", t=NT), AX.X, ALU.add).then_inc(picks_ready, 1)
            dve.wait_ge(soft_out, 1)
            step(V.tensor_reduce(den, topw[:, :, 0:TOPK], AX.X, ALU.add))
            step(V.reciprocal(den, den))
            step(tt(topw[:, :, 0:TOPK], topw[:, :, 0:TOPK], wide(den, 2, TOPK), ALU.mult))
            for t in range(NT):
                step(tt(onew[:, t * TOPK:(t + 1) * TOPK, :], onehot[:, t * TOPK:(t + 1) * TOPK, :],
                        wide(topw[:, t, 0:TOPK], 2, NE), ALU.mult))
            step(V.tensor_reduce(wgt[:, 0:NE, :].rearrange("p e t -> p t e"), onew.rearrange("p (t k) e -> p t e k", t=NT), AX.X, ALU.add))
            dve.wait_ge(rank_mm, 1)
            dve.wait_ge(picks_ready, 1)
            for rows, a, b in ((P, 0, 2), (TS, 2, 3)):
                r = rank[0:rows, 0:NE, a:b].rearrange("p e t -> p t e")
                ins = V.scalar_tensor_tensor(r, ps[0:rows, 2, a * NE:b * NE].rearrange("p (t e) -> p t e", e=NE), 1.0,
                                             picked[0:rows, a:b, :], ALU.add, ALU.mult)
                if rows == P:
                    step(ins)
            ins.then_inc(rank_read, 1)
            dve.wait_ge(rank_read, 1)
            step(V.tensor_scalar(rank[:, 0:NE, 0:2], rank[:, 0:NE, 0:2], -1.0, None, ALU.add))
            step(V.tensor_scalar(rank[0:TS, 0:NE, 2:3], rank[0:TS, 0:NE, 2:3], -1.0, None, ALU.add))
            dve.wait_ge(cnt_mm, 1)
            V.tensor_tensor(flag[0:NE, :], ps[0:NE, 5, 0:1].to_broadcast([NE, PASSES - 1]), cn("thr", NE), ALU.is_gt).then_inc(flag_ready, 1)
            dve.wait_ge(place_mm, 1)
            V.tensor_copy(place[0:NE, :], ps[0:NE, 5, 8:8 + PASSES - 1]).then_inc(place_read, 1)
            dve.wait_ge(place_read, 1)
            dve.wait_ge(flag_ready, 1)
            for p in range(PASSES - 1):
                step(V.tensor_scalar(oh[0:NE, p, :], cn("iota", NE, 16), place[0:NE, p:p + 1], flag[0:NE, p:p + 1],
                                     ALU.is_equal, ALU.mult))
            tt(ohb[0:NE], oh[0:NE], wide(cn("thr", NE), 2, 16), ALU.mult).then_inc(oh_ready, 1)
            dve.wait_ge(more_mm, 1)
            V.tensor_copy(more_f, ps[:, 5, 32:80].rearrange("p (q j) -> p q j", q=3)).then_inc(more_read, 1)
            dve.wait_ge(more_read, 1)
            V.tensor_copy(more_i, more_f).then_inc(more_ready, 1)
            step(V.memset(acc, 0.0))
            step(V.memset(moe["yT"], 0.0))
            V.memset(moe["selT"][0:CAP, :], 0.0).then_inc(moe_zero, 1)
            dve.wait_ge(moe_zero, 1)

            Gt, S, U, Aa, yT = moe["g"], moe["s"], moe["u"], moe["a"], moe["yT"]

            def blocks(bank):
                return ps[:, bank:bank + 2, 0:4 * CAP].rearrange("p a (m c) -> p a m c", m=4)

            def split(ap):
                return ap.rearrange("p (a m) c -> p a m c", a=2)

            def bias(name, e):
                return wide(b_exp[name][:, bass.ds(e, 1), :].rearrange("p e (a m) -> p (e a) m", a=2), 3, CAP)

            def select(x, column):
                for t, (t0, r) in enumerate(TILES):
                    ins = V.tensor_scalar(moe["sel"][0:r, t, :], cn("iota", r, CAP), column(t, r), None, ALU.is_equal)
                ins.then_inc(sel_ready, 1)

            def select_weighted(n, column, weight):
                for t, (t0, r) in enumerate(TILES):
                    ins = V.tensor_scalar(moe["selw"][0:r, t, :], cn("iota", r, CAP), column(t, r), weight(t, r),
                                          ALU.is_equal, ALU.mult)
                ins.then_inc(selw_ready, 1)

            def of(table, e):
                return lambda t, r: table[0:r, bass.ds(e, 1), t:t + 1].rearrange("p e t -> p (e t)")

            def gate_part(n, e):
                dve.wait_ge(exp_used, n * PER + 4)
                tt(split(Gt), blocks(0), bias("b_gate", e), ALU.add).then_inc(g_read, 1)
                dve.wait_ge(g_read, n + 1)
                V.tensor_scalar(Gt, Gt, LIMIT, None, ALU.min).then_inc(g_ready, 1)

            def act_part(n, e):
                dve.wait_ge(g_ready, n + 1)
                dve.wait_ge(sig_ready, n + 1)
                step(tt(S, S, Gt, ALU.mult))
                dve.wait_ge(exp_used, n * PER + 8)
                step(tt(split(U), blocks(2), bias("b_up", e), ALU.add))
                step(V.tensor_scalar(U, U, LIMIT, -LIMIT, ALU.min, ALU.max))
                wait(dve, exp_used, n * PER)
                V.scalar_tensor_tensor(Aa, U, 1.0, S, ALU.add, ALU.mult).then_inc(act_ready, 1)

            def down_part(n, e):
                dve.wait_ge(exp_used, n * PER + 12)
                dve.wait_ge(y_tr, n + 1)
                tt(split(yT), blocks(4), bias("b_down", e), ALU.add).then_inc(y_ready, 1)

            def add_up(y):
                for m in range(KC):
                    dve.wait_ge(comb_mm, y * KC + (m + 1))
                    tt(acc[:, m, :], acc[:, m, :], ps[:, (3, 6, 7)[m % 3], 0:T], ALU.add).then_inc(comb_added, 1)

            select(0, of(rank, 0))
            OWN = 3
            start = step.count

            def dve_turn(i):
                for j in range(UNROLL):
                    n = i * UNROLL + j
                    step.count, step.n = start + j * OWN + i * (UNROLL * OWN), 0
                    dve.wait_ge(x_mm, n + 1)
                    select(n + 1, of(rank, n + 1))
                    wait(dve, selT_tr, n)
                    select_weighted(n, of(rank, n), of(wgt, n))
                    gate_part(n, n)
                    act_part(n, n)
                    down_part(n, n)
                    wait(dve, comb_added, n * KC)
                    add_up(n)
                    assert step.n == OWN

            turns(dve.Fori, dve_turn)
            dve.wait_ge(comb_added, NE * KC)
            add_up(NE)
            step.count = start + NE * OWN
            start = step.count
            MORE_OWN = OWN + 1
            with dve.Fori(0, MORE) as i:
                there = dve.value_load(more_i[0:1, 2, bass.ds(i, 1)], min_val=0, max_val=1)
                with dve.If(there == 1):
                    e = dve.value_load(more_i[0:1, 0, bass.ds(i, 1)], min_val=0, max_val=NE - 1)
                    step.count, step.n = start + i * MORE_OWN, 0
                    step(V.tensor_scalar(rk_more, rank[:, bass.ds(e, 1), :].rearrange("p e t -> p (e t)"),
                                         more_f[:, 1, bass.ds(i, 1)], None, ALU.subtract))
                    of_more = lambda t, r: rk_more[0:r, t:t + 1]
                    select(i + (NE + 1), of_more)
                    select_weighted(i + NE, of_more, of(wgt, e))
                    n = i + NE
                    gate_part(n, e)
                    act_part(n, e)
                    dve.wait_ge(exp_used, n * PER + 12)
                    tt(split(yT), blocks(4), bias("b_down", e), ALU.add).then_inc(y_ready, 1)
                    dve.wait_ge(comb_added, (n + 1) * KC)
                    add_up(n + 1)
                    assert step.n == MORE_OWN
            step = Steps(dve, sem("dve_tail_steps"))
            for m in range(KC):
                residual_tail(V, step, tt, m, xT, acc, ada, tmp64, wide, f_sq_in)
            dve.wait_ge(f_sq_in, KC)
            dve.wait_ge(meansq, 3)
            V.tensor_scalar(rstd, ps[:, 0, 0:T], 1.0 / D, EPS, ALU.mult, ALU.add).then_inc(var_ready, 1)
            dve.wait_ge(root_ready, 5)
            step(V.reciprocal(rstd, rstd))
            for m in range(KC):
                V.scalar_tensor_tensor(hT[:, m, :], xT[:, m, :], vc("g_final")[:, m:m + 1], rstd, ALU.mult, ALU.mult).then_inc(yfin, 1)

        @block.gpsimd
        def _(pool):
            Q = nc.gpsimd
            step = Steps(pool, pool_steps)
            step(Q.memset(line[:, :, 0:PAD], 0.0))
            step(Q.memset(cmask, 0.0))
            pool.wait_ge(ld_vec, 16)
            for m in range(KC):
                ins = Q.tensor_copy(line_seq(m, 0, PAD), prev[:, m * NSEQ:(m + 1) * NSEQ, :])
            ins.then_inc(line_ready, 1)
            pool.wait_ge(xbc_line, KC)
            step(Q.tensor_copy(cnew[:, :, 0:PAD], line[:, :, TP:TP + PAD]))
            for m in range(KC):
                step(Q.tensor_copy(cnew[:, m, PAD:].rearrange("p (b w) -> p b w", w=PAD), line_seq(m, SL, PAD)))
            pool.dma_start(out["convT"].rearrange("(c p) t -> p c t", p=P), cnew).then_inc(st_conv, 16)
            pool.wait_ge(xbc_ready, KC)
            for g in range(G):
                diag = cmask[:, g, :].rearrange("p (b w) -> p b w", w=TS + SL)[:, :, 0:SL]
                ins = Q.tensor_copy(diag, xbcT[:, 6 + g, TP:T].rearrange("p (b w) -> p b w", w=SL))
            ins.then_inc(cmask_ready, 1)
            pool.wait_ge(xb_tok, NT)
            pool.wait_ge(v_ready, 1)
            pool.wait_ge(ld_row, 16)
            for t, (t0, n) in enumerate(TILES):
                Q.tensor_tensor(cat[0:n, t, AW:D].rearrange("p (h e) -> p h e", h=H),
                                xs[0:n, t, :].rearrange("p (h e) -> p h e", h=H),
                                wide(rw("d_skip", n), 2, HD), ALU.mult).then_inc(skip_ready, 1)
            for g in range(G):
                ins = Q.tensor_tensor(bmask[0:TS, g], wide(btok[0:TS, 2, g * P:(g + 1) * P], 1, NSEQ),
                                      wide(cn("seq", TS), 2, P), ALU.mult)
            ins.then_inc(bmask_ready, 1)
            pool.dma_start(out["v"], vg[0:TS, 2, :]).then_inc(st_v, 16)
            pool.wait_ge(st1_ready, 1)
            pool.dma_start(out["ssmpT"], st1).then_inc(st_ssmp, 16)
            pool.wait_ge(y_mm, NT)
            pool.wait_ge(decays, 1)
            s0h = s0T.rearrange("p b (h e) -> p (b h) e", e=HD)
            step(Q.tensor_tensor(s0h, s0h, wide(dec[:, 64:128], 2, HD), ALU.mult))
            for b in range(NSEQ):
                pool.wait_ge(sn_copied, b + 1)
                Q.tensor_tensor(s0T[:, b, :], s0T[:, b, :], snew[:, b % 2, :], ALU.add).then_inc(sn_added, 1)
            pool.wait_ge(sn_added, NSEQ)
            pool.dma_start(out["ssmsT"], s0T).then_inc(st_ssms, 16)
            pool.wait_ge(st_ssms, 16)
            pool.wait_ge(st_ssmp, 16)
            pool.wait_ge(st_v, 16)
            pool.wait_ge(st_conv, 16)


def residual_tail(V, step, tt, m, xT, acc, ada, tmp64, wide, done):
    step(V.scalar_tensor_tensor(xT[:, m, 0:TP], acc[:, m, 0:TP], ada[:, GT_F, m, 0:1], xT[:, m, 0:TP], ALU.mult, ALU.add))
    step(tt(tmp64.rearrange("p (b j) -> p b j", b=NSEQ), acc[:, m, TP:T].rearrange("p (b j) -> p b j", b=NSEQ),
            wide(ada[:, GT_F, m, 1:9], 2, SL), ALU.mult))
    tt(xT[:, m, TP:T], xT[:, m, TP:T], tmp64, ALU.add).then_inc(done, 1)


def kernel(**inputs):
    import concourse.bacc as bacc
    from concourse.bass_utils import run_bass_kernel_spmd

    a = {k: np.asarray(v) for k, v in inputs.items()}

    def feat(x):
        x = x.reshape(-1, x.shape[-1] // P, P)
        return x

    def chunk_first(x):
        return feat(x).transpose(2, 1, 0).reshape(P, -1)

    def row_first(x):
        return feat(x).transpose(2, 0, 1).reshape(P, -1)

    x = np.concatenate([a["x_prompt"].reshape(-1, D), a["x_sample"].reshape(-1, D)])
    c = np.concatenate([a["c_prompt"], a["c_sample"]])
    b_sp = a["b_spatial"][0].T
    parts = {
        "c": chunk_first(c), "b_ada": row_first(a["b_ada"]), "g_mix": row_first(a["g_mix"]), "g_ffn": row_first(a["g_ffn"]),
        "g_final": row_first(a["g_final"][None]),
        "g_cat": row_first(np.concatenate([a["g_out_a"], a["g_out_b"]], axis=1)),
        "conv_w": row_first(a["conv_w"][0]), "conv_b": row_first(a["conv_b"]),
        "b_gate": row_first(a["b_gate"][0]), "b_up": row_first(a["b_up"][0]), "b_down": row_first(a["b_down"][0]),
        "w_router": a["w_router"][0].reshape(KC, P, NE).transpose(1, 0, 2).reshape(P, -1),
        "w_dt": a["w_in"][0][:, IN_DIM - H:].reshape(KC, P, H).transpose(1, 0, 2).reshape(P, -1),
        "w_sp": a["w_spatial"][0].transpose(2, 0, 1).reshape(P, -1), "b_sp": b_sp,
        "prev": chunk_first(a["state_conv"][0].reshape(NSEQ * PAD, D)),
    }
    vec = np.concatenate([parts[n] for n in VEC], axis=1)
    row = np.concatenate([a[n].reshape(1, -1) for n in ("g_v_a", "dt_bias", "a_log", "d_skip", "b_router")], axis=1)
    arrays = {
        "xT": x.T, "vec": vec, "row": row, "con": constants(),
        "s0T": a["state_ssm"][0].reshape(NSEQ, AW, P).transpose(2, 0, 1),
        "w_in": a["w_in"][0], "w_ada": a["w_ada"][0], "w_out": a["w_out"][0],
        "w_gate": a["w_gate"][0], "w_up": a["w_up"][0], "w_down": a["w_down"][0],
    }
    arrays = {k: np.ascontiguousarray(v) for k, v in arrays.items()}
    nc = bacc.Bacc("TRN2", target_bir_lowering=False, num_devices=1)
    d = {k: nc.dram_tensor(f"in_{k}", v.shape, F32, kind="ExternalInput").ap() for k, v in arrays.items()}
    shapes = {"yT": (D, T), "convT": (D, PAD * (1 + NSEQ)), "v": (TS, AW), "ssmpT": (P, AW), "ssmsT": (P, NSEQ, AW)}
    out = {k: nc.dram_tensor(f"out_{k}", s, F32, kind="ExternalOutput").ap() for k, s in shapes.items()}
    build(nc, d, out)
    r = run_bass_kernel_spmd(nc, [{f"in_{k}": v for k, v in arrays.items()}], core_ids=[0]).results[0]
    y = r["out_yT"].T
    conv = r["out_convT"].T
    return (
        np.ascontiguousarray(y[:TP]).reshape(1, TP, D),
        np.ascontiguousarray(y[TP:]).reshape(NSEQ, SL, D),
        np.ascontiguousarray(r["out_ssmpT"].T).reshape(1, 1, H, HD, P),
        np.ascontiguousarray(conv[:PAD]).reshape(1, 1, PAD, D),
        np.ascontiguousarray(r["out_ssmsT"].transpose(1, 2, 0)).reshape(1, NSEQ, H, HD, P),
        np.ascontiguousarray(conv[PAD:]).reshape(1, NSEQ, PAD, D),
        np.ascontiguousarray(r["out_v"]).reshape(1, NSEQ, SL, AW),
    )
```

```python
from contextlib import ExitStack

import numpy as np

import concourse.bass as bass
from concourse import mybir

ALU = mybir.AluOpType
ACT = mybir.ActivationFunctionType
AX = mybir.AxisListType
F32 = mybir.dt.float32
I32 = mybir.dt.int32
U32 = mybir.dt.uint32

P = 128
D = 1024
KC = D // P
TP = 256
NSEQ = 8
SL = 8
TS = NSEQ * SL
T = TP + TS
TILES = [(0, P), (P, P), (TP, TS)]
NT = len(TILES)
AW = 512
AH = 4
H = 8
HD = 64
G = 2
TAPS = 4
PAD = TAPS - 1
CONVW = PAD + TP + NSEQ * (PAD + SL)
CONVN = CONVW - PAD
SEQ0 = PAD + TP
IN_DIM = 2568
NE = 32
TOPK = 4
CAP = 64
PASSES = -(-T // CAP)
MORE = T * TOPK // (CAP + 1)
EPS = 1e-6
LIMIT = 7.0
ALPHA = 1.702

UNIT = 2048
RING = 16
FS = 6
PER = 24
UNROLL = 2
PAIRS = NE // 2
MORE_PAIRS = -(-MORE // 2)
LW = 2 * MORE_PAIRS
FAR = 1000.0


def layout(spec):
    out, at = {}, 0
    for name, width in spec:
        out[name] = (at, width)
        at += width
    return out, at


VEC, VECW = layout([("c", KC * (1 + NSEQ)), ("b_ada", 48), ("g_mix", KC), ("g_ffn", KC), ("g_final", KC),
                    ("g_cat", KC), ("conv_w", TAPS * KC), ("conv_b", KC), ("b_exp", D),
                    ("w_router", KC * NE), ("w_dt", KC * H), ("w_sp", AH * P),
                    ("b_sp", AH), ("prev", KC * NSEQ * PAD)])
ROW, ROWW = layout([("g_v", AW), ("dt_bias", H), ("a_log", H), ("d_skip", H), ("b_router", NE)])
CON, CONW = layout([("upto", P), ("after", P), ("ident", P), ("ones", P), ("before", P), ("upto_s", TS),
                    ("after_s", TS), ("seq", NSEQ), ("rep", TS), ("iota", 96), ("thr", PASSES - 1), ("eidx", P)])


def constants():
    k = np.arange(P)[:, None]
    m = np.arange(P)[None, :]
    out = np.zeros((P, CONW), np.float32)

    def put(name, a):
        at = CON[name][0]
        out[:a.shape[0], at:at + a.shape[1]] = a

    ks, ms = k[:TS], m[:, :TS]
    same = ks // SL == ms // SL
    put("upto", (k <= m).astype(np.float32))
    put("after", (k > m).astype(np.float32))
    put("ident", (k == m).astype(np.float32))
    put("ones", np.ones((P, P), np.float32))
    put("before", (k < m).astype(np.float32))
    put("upto_s", ((ks <= ms) & same).astype(np.float32))
    put("after_s", ((ks > ms) & same).astype(np.float32))
    put("seq", (ks // SL == np.arange(NSEQ)[None, :]).astype(np.float32))
    put("rep", (np.arange(SL)[:, None] == ms % SL).astype(np.float32))
    put("iota", np.broadcast_to(np.arange(96, dtype=np.float32), (P, 96)))
    put("thr", np.broadcast_to(CAP * np.arange(1, PASSES, dtype=np.float32), (P, PASSES - 1)))
    put("eidx", np.broadcast_to(np.arange(NE, dtype=np.float32)[:, None], (NE, P)))
    return out


FRONT = ([("ada0", j) for j in range(4)] + [("ada1", j) for j in range(4)] + [("xbc", j) for j in range(4)]
         + [("uv", j) for j in range(4)] + [("z", j) for j in range(2)] + [("ada2", j) for j in range(4)]
         + [("ada3", j) for j in range(4)] + [("out", j) for j in range(4)] + [("ada4", j) for j in range(4)]
         + [("ada5", j) for j in range(4)])
FIRST = {}
for _u, (_m, _j) in enumerate(FRONT):
    FIRST.setdefault(_m, _u)
NF = len(FRONT)
SH_M, SC_M, GT_M, SH_F, SC_F, GT_F = range(6)


class Steps:

    def __init__(self, eng, sem):
        self.eng, self.sem, self.count, self.n = eng, sem, 0, 0

    def __call__(self, ins):
        self.count = self.count + 1
        self.n += 1
        ins.then_inc(self.sem, 1)
        self.eng.wait_ge(self.sem, self.count)


def wait(eng, sem, count):
    if not (isinstance(count, int) and count <= 0):
        eng.wait_ge(sem, count)


def turns(engine_loop, body):
    body(0)
    with engine_loop(1, PAIRS // UNROLL - 1) as i:
        body(i)
    body(PAIRS // UNROLL - 1)


def build(nc, d, out):
    with ExitStack() as ctx:
        arena = ctx.enter_context(nc.sbuf_tensor("arena", [P, 53208], F32))
        used = [0]

        def view(at, shape, rows=P):
            n = int(np.prod(shape))
            ap = arena[0:rows, at:at + n]
            if len(shape) == 2:
                ap = ap.rearrange("p (a b) -> p a b", a=shape[0])
            if len(shape) == 3:
                ap = ap.rearrange("p (a b c) -> p a b c", a=shape[0], b=shape[1])
            return ap

        def sb(shape):
            at = used[0]
            used[0] += -(-int(np.prod(shape)) // 8) * 8
            assert used[0] <= 53208, used[0]
            return view(at, shape), at

        ring, ring_at = sb([RING, UNIT])
        vec, _ = sb([VECW])
        row, _ = sb([ROWW])
        con, _ = sb([CONW])
        xT, _ = sb([KC, T])
        hT, moe_at = sb([KC, T])
        line, work_at = sb([KC, CONVW])
        catT = hT
        acc, acc_at = sb([KC, T])
        sq = acc
        Lx = view(acc_at, [H, P])
        sel_l = view(acc_at + H * P, [H, P])
        junk, _ = view(acc_at + 2 * H * P, [AW]), 0
        cat, cat_at = sb([NT, D])
        htok = cat
        cacc = view(cat_at, [2, CONVN])
        vsq = view(cat_at, [NT, AW])
        small = {}

        def tiny(name, shape):
            small[name], _ = sb(shape)
            return small[name]

        csil = tiny("csil", [KC, 1 + NSEQ])
        ada = tiny("ada", [6, KC, 1 + NSEQ])
        gain = tiny("gain", [KC, 1 + NSEQ])
        rstd = tiny("rstd", [T])
        dtx = tiny("dtx", [NT, H])
        dtr = tiny("dtr", [NT, H])
        dte = tiny("dte", [NT, H])
        dtu = tiny("dtu", [NT, H])
        dt = tiny("dt", [NT, H])
        dta = tiny("dta", [NT, H])
        ea = tiny("ea", [H])
        dseq = tiny("dseq", [NSEQ, H])
        dec = tiny("dec", [P])
        ssv = tiny("ssv", [NT, AH])
        ss9 = tiny("ss9", [3, NT])
        wblk = tiny("wblk", [AH, TS])
        bsp = tiny("bsp", [NT, AH])
        tmp64 = tiny("tmp64", [TS])
        cnew = tiny("cnew", [KC, PAD * (1 + NSEQ)])
        mdec = view(work_at, [H, P])
        xdt = view(work_at + H * P, [NT, AW])
        at = moe_at
        moe = {n: sb([NT, 2 * CAP])[0] for n in ("sel",)}
        for name, shape in [("X", [D]), ("g", [D]), ("s", [D]), ("y", [D]), ("selT", [T]), ("selw", [NT, 2 * CAP]),
                            ("pick", [3, 2 * CAP])]:
            moe[name] = view(at, shape)
            at += int(np.prod(shape))
        assert at <= work_at + KC * CONVW
        logit, rt_at = sb([NT, NE])
        top, _ = sb([NT, 8])
        topi, _ = sb([NT, 8])
        topf, _ = sb([NT, 8])
        topw, _ = sb([NT, 8])
        den, _ = sb([NT])
        picked, _ = sb([NT, NE])
        rank, _ = sb([NE, NT])
        wgt, _ = sb([NE, NT])
        rk_more, _ = sb([2, NT])
        flag, _ = sb([PASSES - 1])
        place, _ = sb([PASSES - 1])
        oh, _ = sb([PASSES - 1, LW])
        ohb, _ = sb([PASSES - 1, LW])
        more_f, _ = sb([3, LW])
        more_i = sb([3, LW])[0].bitcast(I32)
        onehot = view(acc_at, [NT * TOPK, NE])
        onew = view(acc_at + NT * TOPK * NE, [NT * TOPK, NE])
        up = [ring_at + FS * UNIT]

        def scratch(shape):
            n = int(np.prod(shape))
            at = up[0]
            up[0] += n
            assert up[0] <= ring_at + RING * UNIT
            return view(at, shape)

        xbcT = scratch([KC, T])
        btok = scratch([NT, G * P])
        s0T = scratch([NSEQ, AW])
        cmask = scratch([G, NSEQ * (TS + SL)])
        bmask = scratch([G, NSEQ, P])
        snew = scratch([2, AW])
        st0 = scratch([AW])
        st1 = scratch([AW])
        xw = scratch([NT, AW])
        xs = scratch([NT, AW])
        zs = scratch([NT, AW])
        ug = scratch([NT, AW])
        vg = scratch([NT, AW])
        gm = view(moe_at, [G, P])

        ps = ctx.enter_context(nc.psum_tensor("ps", [P, 8, 512], F32))
        block_sems = {}

        def sem(name):
            if name not in block_sems:
                block_sems[name] = ctx.enter_context(nc.semaphore(name))
            return block_sems[name]

        def vc(name, shape=None, rows=P):
            a, w = VEC[name]
            ap = vec[0:rows, a:a + w]
            return ap if shape is None else ap.rearrange("p (a b) -> p a b", a=shape)

        def cn(name, rows=P, width=None):
            a, w = CON[name]
            return con[0:rows, a:a + (width or w)]

        def rw(name, rows=P):
            a, w = ROW[name]
            return row[0:rows, a:a + w]

        def wide(ap, axis, n):
            shape = list(ap.shape)
            ap = ap.unsqueeze(axis)
            shape.insert(axis, n)
            return ap.to_broadcast(shape)

        conv_w = vc("conv_w", TAPS)
        conv_b = vc("conv_b")
        b_exp = vc("b_exp")
        bada = vc("b_ada", 6)
        w_router = vc("w_router", KC)
        w_dt = vc("w_dt", KC)
        w_sp = vc("w_sp", AH)
        prev = vc("prev", KC * NSEQ)

        def upto(t):
            return cn("upto") if t < 2 else cn("upto_s", TS)

        def after(t):
            return cn("after") if t < 2 else cn("after_s", TS)

        def line_seq(m, first, n):
            return line[:, m, SEQ0:CONVW].rearrange("p (b w) -> p b w", w=PAD + SL)[:, :, first:first + n]

        ld_x, ld_vec, ld_row, ld_con, ld_s0 = (sem(n) for n in ("ld_x", "ld_vec", "ld_row", "ld_con", "ld_s0"))
        front_landed = [sem(f"front_landed{i}") for i in range(FS)]
        front_used = sem("front_used")
        exp_landed = [sem(f"exp_landed{i}") for i in range(RING)]
        exp_used = sem("exp_used")
        x_sq, meansq, var_ready, root_ready, xn_ready = (sem(n) for n in ("x_sq", "meansq", "var_ready", "root_ready", "xn_ready"))
        c_ready, ada_mm, ada_ready, gain_ready = (sem(n) for n in ("c_ready", "ada_mm", "ada_ready", "gain_ready"))
        hp_ready, hs_ready = sem("hp_ready"), sem("hs_ready")
        rep_mm, rep_read = sem("rep_mm"), sem("rep_read")
        line_ready, xbc_mm, xbc_line, conv_begun, conv_done, xbc_ready = (
            sem(n) for n in ("line_ready", "xbc_mm", "xbc_line", "conv_begun", "conv_done", "xbc_ready"))
        dt_mm, dt_abs, dt_exp, dt_one, dt_ln, dta_ready = (
            sem(n) for n in ("dt_mm", "dt_abs", "dt_exp", "dt_one", "dt_ln", "dta_ready"))
        uv_mm, gelu_done, z_mm, z_silu = (sem(n) for n in ("uv_mm", "gelu_done", "z_mm", "z_silu"))
        v_ready, s_mm, s_read, ga_ready, ga_sq = (sem(n) for n in ("v_ready", "s_mm", "s_read", "ga_ready", "ga_sq"))
        xb_tr, xb_tok, decay_mm, decays = (sem(n) for n in ("xb_tr", "xb_tok", "decay_mm", "decays"))
        sl_ready, l_mm, lx_ready, g_mm, gm_ready, m_ready = (
            sem(n) for n in ("sl_ready", "l_mm", "lx_ready", "g_mm", "gm_ready", "m_ready"))
        xdt_ready, xw_ready, skip_ready, cmask_ready, bmask_ready = (
            sem(n) for n in ("xdt_ready", "xw_ready", "skip_ready", "cmask_ready", "bmask_ready"))
        y_mm, y_read, gb_ready, gb_sq, st_mm, st0_ready, st1_ready = (
            sem(n) for n in ("y_mm", "y_read", "gb_ready", "gb_sq", "st_mm", "st0_ready", "st1_ready"))
        sn_mm, sn_copied, sn_added = sem("sn_mm"), sem("sn_copied"), sem("sn_added")
        cat_ready, cat_tr, catT_ready, out_mm, x1_ready, x1_sq = (
            sem(n) for n in ("cat_ready", "cat_tr", "catT_ready", "out_mm", "x1_ready", "x1_sq"))
        h_tr, htok_ready, router_mm, picks_ready, rank_mm, route_ready = (
            sem(n) for n in ("h_tr", "htok_ready", "router_mm", "picks_ready", "rank_mm", "route_ready"))
        soft_in, soft_out, cnt_mm, place_mm, oh_ready, more_mm, more_ready, rank_read, place_read, more_read, flag_ready = (
            sem(n) for n in ("soft_in", "soft_out", "cnt_mm", "place_mm", "oh_ready", "more_mm", "more_ready",
                             "rank_read", "place_read", "more_read", "flag_ready"))
        moe_zero = sem("moe_zero")
        sel_ready, selw_ready, pick_ready, x_mm, x_tok, x_tr, x_ready = (
            sem(n) for n in ("sel_ready", "selw_ready", "pick_ready", "x_mm", "x_tok", "x_tr", "x_ready"))
        g_ready, sig_ready, act_ready, a_tr, actT_ready, y_ready, selT_tr, selT_ready, comb_mm, comb_added = (
            sem(n) for n in ("g_ready", "sig_ready", "act_ready", "a_tr", "actT_ready", "y_ready", "selT_tr", "selT_ready",
                             "comb_mm", "comb_added"))
        f_sq_in, f_sq, yfin = sem("f_sq_in"), sem("f_sq"), sem("yfin")
        st_v, st_conv, st_ssmp, st_ssms, st_y = (sem(n) for n in ("st_v", "st_conv", "st_ssmp", "st_ssms", "st_y"))
        pool_zero = sem("pool_zero")
        dve_steps, act_steps, pool_steps = sem("dve_steps"), sem("act_steps"), sem("pool_steps")

        w_in = d["w_in"].rearrange("(c p) n -> p c n", p=P)
        w_ada = d["w_ada"].rearrange("(c p) n -> p c n", p=P)
        w_out = d["w_out"].rearrange("(c p) n -> p c n", p=P)
        w_exp = [d[n].rearrange("e (c p) n -> e p c n", p=P) for n in ("w_gate", "w_up", "w_down")]

        def front_source(m, j):
            if m.startswith("ada"):
                s = int(m[3:])
                return w_ada[:, 2 * j:2 * j + 2, s * D:(s + 1) * D]
            if m == "xbc":
                return w_in[:, 2 * j:2 * j + 2, 3 * AW:3 * AW + D]
            if m == "uv":
                return w_in[:, 2 * j:2 * j + 2, 0:2 * AW]
            if m == "z":
                return w_in[:, 4 * j:4 * j + 4, 2 * AW:3 * AW]
            return w_out[:, 2 * j:2 * j + 2, :]

        def exp_slot(j, k):
            return (FS + PER * j + k) % RING

        def exp_source(k, e):
            m, p = k // 8, k // 2 % 4
            return w_exp[m][bass.ds(e(k % 2), 1), :, 2 * p:2 * p + 2, :].rearrange("e p c n -> p (e c) n")

        block = ctx.enter_context(nc.Block())

        @block.sync
        def _(sp):
            sp.dma_start(xT, d["xT"].rearrange("(c p) t -> p c t", p=P)).then_inc(ld_x, 16)
            sp.dma_start(con, d["con"]).then_inc(ld_con, 16)
            sp.dma_start(vec, d["vec"]).then_inc(ld_vec, 16)
            for u, (m, j) in enumerate(FRONT):
                if u >= FS:
                    sp.wait_ge(front_used, u - FS + 1)
                slot = ring[:, u % FS, :]
                src = front_source(m, j)
                sp.dma_start(slot.rearrange("p (c n) -> p c n", c=src.shape[1]), src).then_inc(front_landed[u % FS], 16)
                if u == FS - 1:
                    sp.dma_start(row, d["row"].broadcast_to([P, ROWW])).then_inc(ld_row, 16)
                    sp.dma_start(s0T, d["s0T"]).then_inc(ld_s0, 16)

            def load_unit(k, e, slot):
                sp.dma_start(ring[:, slot, :].rearrange("p (c n) -> p c n", c=2), exp_source(k, e)).then_inc(exp_landed[slot], 16)

            for v in range(PER * UNROLL):
                if v == 0:
                    sp.wait_ge(cat_ready, NT)
                    sp.wait_ge(sn_added, NSEQ)
                    sp.wait_ge(st_v, 16)
                    sp.wait_ge(st_ssmp, 16)
                    sp.wait_ge(st_ssms, 16)
                elif RING - FS <= v < RING:
                    last = max(u for u in range(NF) if u % FS == v - (RING - FS))
                    sp.wait_ge(front_used, last + 1)
                elif v >= RING:
                    sp.wait_ge(exp_used, v - RING + 1)
                load_unit(v % PER, lambda s: 2 * (v // PER) + s, (FS + v) % RING)
            with sp.Fori(1, PAIRS // UNROLL) as i:
                for j in range(UNROLL):
                    for k in range(PER):
                        sp.wait_ge(exp_used, i * (PER * UNROLL) + (PER * j + k - RING + 1))
                        load_unit(k, lambda s: i * (2 * UNROLL) + (2 * j + s), exp_slot(j, k))

            def more_loads(i):
                there = sp.value_load(more_i[0:1, 2, bass.ds(i * 2, 1)], min_val=0, max_val=1)
                with sp.If(there == 1):
                    es = [sp.value_load(more_i[0:1, 0, bass.ds(i * 2 + s, 1)], min_val=0, max_val=NE - 1) for s in range(2)]
                    for k in range(PER):
                        behind = RING if k >= RING or isinstance(i, int) else (PER - RING if k < PER - RING else PER)
                        sp.wait_ge(exp_used, i * PER + (PAIRS * PER + k - behind + 1))
                        load_unit(k, lambda s: es[s], exp_slot(0, k))

            sp.wait_ge(more_ready, 1)
            more_loads(0)
            with sp.Fori(1, MORE_PAIRS) as i:
                more_loads(i)
            sp.wait_ge(yfin, KC)
            sp.dma_start(out["yT"].rearrange("(c p) t -> p c t", p=P), hT).then_inc(st_y, 16)
            sp.wait_ge(st_y, 16)
            sp.wait_ge(st_conv, 16)

        @block.tensor
        def _(pe):
            def mm(o, l, r, start=True, stop=True):
                return pe.matmul(o, l, r, start=start, stop=stop, skip_group_check=True)

            def landed(u):
                pe.wait_ge(front_landed[u % FS], 16 * (u // FS + 1))

            def unit(u, c=2):
                return ring[:, u % FS, :].rearrange("p (c n) -> p c n", c=c)

            def mean_square(bank):
                for k in range(KC):
                    last = mm(ps[:, bank, 0:T], cn("ones"), sq[:, k, :], k == 0, k == KC - 1)
                last.then_inc(meansq, 1)

            def ada_section(s, bank):
                if s == 0:
                    pe.wait_ge(c_ready, 1)
                for j in range(4):
                    u = FIRST[f"ada{s}"] + j
                    landed(u)
                    for kk in range(2):
                        k = 2 * j + kk
                        for m in range(KC):
                            last = mm(ps[:, bank, m * 9:m * 9 + 9], unit(u)[:, kk, m * P:(m + 1) * P], csil[:, k, :],
                                      k == 0 and m == 0, k == KC - 1)
                    last.then_inc(front_used, 1)
                mm(ps[0:1, bank, 511:512], cn("ones")[:, 0:1], cn("ones")[:, 0:1], False, True).then_inc(ada_mm, 1)

            pe.wait_ge(ld_con, 16)
            pe.wait_ge(ld_vec, 16)
            for h in range(AH):
                mm(ps[0:TS, 3, h * SL:(h + 1) * SL], cn("rep", SL), w_sp[0:SL, h, 0:SL])
            mm(ps[0:TS, 3, 64:64 + AH], cn("rep", SL), vc("b_sp")[0:SL, :]).then_inc(rep_mm, 1)
            pe.wait_ge(x_sq, 1)
            mean_square(0)
            ada_section(SH_M, 1)
            ada_section(SC_M, 2)
            pe.wait_ge(hp_ready, 1)
            pe.wait_ge(hs_ready, 1)
            for j in range(4):
                landed(FIRST["xbc"] + j)
            for i in range(KC):
                m = (i + 4) % KC
                if i >= 2:
                    pe.wait_ge(xbc_line, i - 1)
                for k in range(KC):
                    u = FIRST["xbc"] + k // 2
                    last = mm(ps[:, 6 + i % 2, 0:T], unit(u)[:, k % 2, m * P:(m + 1) * P], hT[:, k, :], k == 0, k == KC - 1)
                    if i == KC - 1 and k % 2 == 1 and k < KC - 1:
                        last.then_inc(front_used, 1)
                    if k == KC - 1:
                        last.then_inc(xbc_mm, 1)
            pe.wait_ge(xbc_line, KC - 1)
            for t, (t0, n) in enumerate(TILES):
                for k in range(KC):
                    last = mm(ps[0:n, 6, t * H:(t + 1) * H], hT[:, k, t0:t0 + n], w_dt[:, k, :], k == 0, k == KC - 1)
                    if t == 0 and k == 0:
                        last.then_inc(front_used, 1)
            last.then_inc(dt_mm, 1)
            pe.wait_ge(xn_ready, 1)
            pe.wait_ge(ada_ready, 2)
            for j in range(4):
                u = FIRST["uv"] + j
                landed(u)
                for kk in range(2):
                    k = 2 * j + kk
                    for half in (1, 0):
                        for t, (t0, n) in enumerate(TILES):
                            last = mm(ps[0:n, 3 * half + t, :], hT[:, k, t0:t0 + n],
                                      unit(u)[:, kk, half * AW:(half + 1) * AW], k == 0, k == KC - 1)
                            if k == KC - 1 and not (half == 0 and t == NT - 1):
                                last.then_inc(uv_mm, 1)
                last.then_inc(front_used, 1)
            pe.wait_ge(dta_ready, 1)
            pe.wait_ge(xbc_line, KC)
            pe.wait_ge(gelu_done, 1)
            for j in range(2):
                u = FIRST["z"] + j
                landed(u)
                for kk in range(4):
                    k = 4 * j + kk
                    for t, (t0, n) in enumerate(TILES):
                        last = mm(ps[0:n, (6, 7, 3)[t], :], hT[:, k, t0:t0 + n], unit(u, 4)[:, kk, :], k == 0, k == KC - 1)
                        if k == KC - 1 and t < NT - 1:
                            last.then_inc(z_mm, 1)
                last.then_inc(front_used, 1)
            pe.wait_ge(gelu_done, 2)
            ada_section(GT_M, 4)
            pe.wait_ge(xbc_ready, KC)
            pe.wait_ge(gelu_done, 6)
            for t, (t0, n) in enumerate(TILES):
                if t:
                    pe.wait_ge(xb_tok, t)
                for m in range(4):
                    pe.transpose(ps[0:n, 1, m * P:(m + 1) * P], xbcT[:, m, t0:t0 + n], cn("ident"))
                for g in range(G):
                    last = pe.transpose(ps[0:n, 2, g * P:(g + 1) * P], xbcT[:, 4 + g, t0:t0 + n], cn("ident"))
                last.then_inc(xb_tr, 1)
            for t, (t0, n) in enumerate(TILES):
                mm(ps[0:n, 0, 2 * t * H:(2 * t + 1) * H], after(t), dta[0:n, t, :])
                mm(ps[0:n, 0, (2 * t + 1) * H:(2 * t + 2) * H], upto(t), dta[0:n, t, :])
            mm(ps[:, 0, 6 * H:7 * H], cn("ones"), dta[:, 1, :])
            mm(ps[:, 0, 64:64 + NSEQ * H].rearrange("p (b h) -> p b h", b=NSEQ), cn("ones", TS), dseq[0:TS]).then_inc(decay_mm, 1)
            pe.wait_ge(z_silu, NT)

            def decay_and_scores(t):
                t0, n = TILES[t]
                pe.wait_ge(sl_ready, t + 1)
                if t:
                    pe.wait_ge(lx_ready, t)
                    pe.wait_ge(gm_ready, t)
                for h in range(H):
                    last = mm(ps[0:n, 6 + h // 4, (h % 4) * P:(h % 4) * P + n], sel_l[0:n, h, 0:n], upto(t))
                last.then_inc(l_mm, 1)
                for g in range(G):
                    last = mm(ps[0:n, 5, g * P:g * P + n], xbcT[:, 4 + g, t0:t0 + n], xbcT[:, 6 + g, t0:t0 + n])
                last.then_inc(g_mm, 1)

            def spatial(t):
                n = TILES[t][1]
                if t == 0:
                    pe.wait_ge(v_ready, 1)
                else:
                    pe.wait_ge(s_read, t)
                for h in range(AH):
                    w = w_sp[:, h, :] if t < 2 else wblk[0:TS, h, :]
                    last = mm(ps[0:n, 3, h * P:(h + 1) * P], w, vg[0:n, t, h * P:(h + 1) * P])
                last.then_inc(s_mm, 1)

            decay_and_scores(0)
            spatial(0)
            decay_and_scores(1)
            spatial(1)
            spatial(2)
            ada_section_wait = 3
            pe.wait_ge(ada_ready, ada_section_wait)
            ada_section(SH_F, 4)

            def y_diag(t):
                n = TILES[t][1]
                pe.wait_ge(m_ready, t + 1)
                for h in range(H):
                    last = mm(ps[0:n, 1, h * HD:(h + 1) * HD], mdec[0:n, h, 0:n], xdt[0:n, t, h * HD:(h + 1) * HD])
                return last

            pe.wait_ge(xdt_ready, 1)
            pe.wait_ge(xb_tok, NT)
            y_diag(0).then_inc(y_mm, 1)
            pe.wait_ge(decays, 1)
            pe.wait_ge(xw_ready, 1)
            for g in range(G):
                last = mm(ps[:, 0, g * 256:(g + 1) * 256], btok[:, 0, g * P:(g + 1) * P], xw[:, 0, g * 256:(g + 1) * 256])
            last.then_inc(st_mm, 1)
            pe.wait_ge(st0_ready, 1)
            for g in range(G):
                mm(ps[:, 2, g * 256:(g + 1) * 256], xbcT[:, 6 + g, P:2 * P], st0[:, g * 256:(g + 1) * 256])
            pe.wait_ge(y_read, 1)
            y_diag(1).then_inc(y_mm, 1)
            for g in range(G):
                last = mm(ps[:, 0, g * 256:(g + 1) * 256], btok[:, 1, g * P:(g + 1) * P], xw[:, 1, g * 256:(g + 1) * 256])
            last.then_inc(st_mm, 1)
            decay_and_scores(2)
            pe.wait_ge(ld_s0, 16)
            pe.wait_ge(cmask_ready, 1)
            pe.wait_ge(y_read, 2)
            for g in range(G):
                for b in range(NSEQ):
                    mm(ps[0:TS, 2, g * 256:(g + 1) * 256], cmask[:, g, b * TS:(b + 1) * TS],
                       s0T[:, b, g * 256:(g + 1) * 256], b == 0, b == NSEQ - 1)
            y_diag(2).then_inc(y_mm, 1)
            pe.wait_ge(bmask_ready, 1)
            pe.wait_ge(gm_ready, NT)
            pe.wait_ge(lx_ready, NT)
            for b in range(NSEQ):
                if b >= 2:
                    pe.wait_ge(sn_copied, b - 1)
                for g in range(G):
                    last = mm(ps[:, 5 + b % 2, g * 256:(g + 1) * 256], bmask[0:TS, g, b, :], xw[0:TS, 2, g * 256:(g + 1) * 256])
                last.then_inc(sn_mm, 1)
            pe.wait_ge(ada_ready, 4)
            pe.wait_ge(s_read, NT)
            for t, (t0, n) in enumerate(TILES):
                pe.wait_ge(cat_ready, t + 1)
                if t:
                    pe.wait_ge(catT_ready, t)
                for m in range(KC):
                    last = pe.transpose(ps[:, 3 + m // 4, (m % 4) * P:(m % 4) * P + n], cat[0:n, t, m * P:(m + 1) * P],
                                        cn("ident", n, n))
                last.then_inc(cat_tr, 1)
            pe.wait_ge(catT_ready, NT)
            pe.wait_ge(sn_copied, NSEQ)
            for j in range(4):
                landed(FIRST["out"] + j)
            for m in range(KC):
                if m >= 2:
                    pe.wait_ge(x1_ready, m - 1)
                for k in range(KC):
                    last = mm(ps[:, 6 + m % 2, 0:T], unit(FIRST["out"] + k // 2)[:, k % 2, m * P:(m + 1) * P], catT[:, k, :],
                              k == 0, k == KC - 1)
                    if m == KC - 1 and k % 2 == 1 and k < KC - 1:
                        last.then_inc(front_used, 1)
                last.then_inc(out_mm, 1)
            pe.wait_ge(st1_ready, 1)
            mm(ps[0:1, 0, 0:1], cn("ones")[:, 0:1], cn("ones")[:, 0:1]).then_inc(front_used, 1)
            ada_section(SC_F, 0)
            pe.wait_ge(y_read, NT)
            ada_section(GT_F, 1)
            pe.wait_ge(x1_sq, KC)
            mean_square(2)
            pe.wait_ge(hp_ready, 2)
            pe.wait_ge(hs_ready, 2)
            for t, (t0, n) in enumerate(TILES):
                for k in range(KC):
                    last = mm(ps[0:n, 7, t * NE:(t + 1) * NE], hT[:, k, t0:t0 + n], w_router[:, k, :], k == 0, k == KC - 1)
            last.then_inc(router_mm, 1)
            for t, (t0, n) in enumerate(TILES):
                if t:
                    pe.wait_ge(htok_ready, t)
                for k in range(KC):
                    last = pe.transpose(ps[0:n, 3 + k // 4, (k % 4) * P:(k % 4 + 1) * P], hT[:, k, t0:t0 + n], cn("ident"))
                last.then_inc(h_tr, 1)
            pe.wait_ge(picks_ready, 1)
            for t, (t0, n) in enumerate(TILES):
                for s in range(t + 1):
                    last = mm(ps[0:n, 2, t * NE:(t + 1) * NE], cn("before" if s == t else "ones", n if s == t else P, n),
                              picked[0:TILES[s][1], s, :], s == 0, s == t)
            last.then_inc(rank_mm, 1)
            for t, (t0, n) in enumerate(TILES):
                last = mm(ps[0:NE, 5, 0:1], picked[0:n, t, :], cn("ones", n, 1), t == 0, t == NT - 1)
            last.then_inc(cnt_mm, 1)
            pe.wait_ge(flag_ready, 1)
            nf = PASSES - 1
            mm(ps[0:NE, 5, 8:8 + nf], cn("before", NE, NE), flag[0:NE, :], True, False)
            for p in range(1, nf):
                last = mm(ps[0:NE, 5, 8 + p:8 + nf], cn("ones", NE, NE), flag[0:NE, 0:nf - p], False, p == nf - 1)
            last.then_inc(place_mm, 1)
            pe.wait_ge(oh_ready, 1)
            for q, (l, r) in enumerate([(cn("eidx", NE), oh), (cn("ones", NE), ohb), (cn("ones", NE), oh)]):
                for p in range(nf):
                    last = mm(ps[:, 5, 32 + LW * q:32 + LW * (q + 1)], l, r[0:NE, p, :], p == 0, p == nf - 1)
            last.then_inc(more_mm, 1)

            X = moe["X"].rearrange("p (k c) -> p k c", k=KC)
            A = moe["g"].rearrange("p (k c) -> p k c", k=KC)

            def gather(q):
                wait(pe, sel_ready, q + 1)
                wait(pe, selT_ready, q - 1)
                for half in range(2):
                    for t, (t0, n) in enumerate(TILES):
                        last = mm(ps[:, 6 + half, :], moe["sel"][0:n, t, :], htok[0:n, t, half * AW:(half + 1) * AW],
                                  t == 0, t == NT - 1)
                last.then_inc(x_mm, 1)

            def turn(src, done):
                for k in range(KC):
                    last = pe.transpose(ps[:, k // 4, (k % 4) * P:(k % 4 + 1) * P], src[:, k, :], cn("ident"))
                last.then_inc(done, 1)

            def turn_x(q):
                pe.wait_ge(x_tok, q + 1)
                wait(pe, actT_ready, q)
                turn(X, x_tr)

            def product(m, bank, rows, loads, slots):
                for half in range(2):
                    mm(ps[:, bank + half, :], moe["pick"][:, m, :], b_exp[:, half * AW:(half + 1) * AW], True, False)
                for p in range(4):
                    for s in range(2):
                        pe.wait_ge(exp_landed[slots[2 * p + s]], loads[2 * p + s])
                    w = [ring[:, slots[2 * p + s], :].rearrange("p (c n) -> p c n", c=2) for s in range(2)]
                    for kk in range(2):
                        for half in range(2):
                            for s in range(2):
                                c = slice(s * CAP, (s + 1) * CAP)
                                last = mm(ps[c, bank + half, :], rows[:, 2 * p + kk, c], w[s][:, kk, half * AW:(half + 1) * AW],
                                          False, p == 3 and kk == 1)
                                if kk == 1 and half == 1:
                                    last.then_inc(exp_used, 1)

            def combine(q):
                pe.wait_ge(y_ready, q + 1)
                pe.wait_ge(selT_ready, q + 1)
                for m in range(KC):
                    wait(pe, comb_added, q * KC + max(0, m - 2))
                    mm(ps[:, (2, 3, 6)[m % 3], 0:T], moe["y"][:, m * P:(m + 1) * P], moe["selT"]).then_inc(comb_mm, 1)

            def turn_sel(q):
                pe.wait_ge(selw_ready, q + 1)
                for t, (t0, r) in enumerate(TILES):
                    last = pe.transpose(ps[:, 7, t0:t0 + r], moe["selw"][0:r, t, :], cn("ident", r, r))
                last.then_inc(selT_tr, 1)

            def pair(q, slots, loads, serial=False):
                first, last = isinstance(q, int) and q == 0, isinstance(q, int) and q == PAIRS - 1
                if serial:
                    wait(pe, comb_added, q * KC)
                    gather(q)
                    turn_x(q)
                pe.wait_ge(x_ready, q + 1)
                pe.wait_ge(pick_ready, q + 1)
                product(0, 0, X, loads[0:8], slots[0:8])
                if not first:
                    wait(pe, comb_added, (q - (0 if serial else 1)) * KC)
                product(1, 2, X, loads[8:16], slots[8:16])
                if not serial and not last:
                    gather(q + 1)
                pe.wait_ge(act_ready, q + 1)
                turn(A, a_tr)
                if not serial and not last:
                    pe.wait_ge(x_tok, q + 2)
                if not serial and not first:
                    combine(q - 1)
                if not serial and not last:
                    turn_x(q + 1)
                turn_sel(q)
                pe.wait_ge(actT_ready, q + 1)
                wait(pe, y_ready, q)
                product(2, 4, A, loads[16:24], slots[16:24])

            pe.wait_ge(more_read, 1)
            pe.wait_ge(htok_ready, NT)
            pe.wait_ge(ada_ready, 6)
            gather(0)
            turn_x(0)

            def pe_turn(i):
                for j in range(UNROLL):
                    loads = [i * 48 + 16 * ((PER * j + k) // RING + 1) for k in range(PER)]
                    pair(i * UNROLL + j, [exp_slot(j, k) for k in range(PER)], loads)

            turns(pe.Fori, pe_turn)
            combine(PAIRS - 1)

            with pe.Fori(0, MORE_PAIRS) as i:
                there = pe.value_load(more_i[0:1, 2, bass.ds(i * 2, 1)], min_val=0, max_val=1)
                with pe.If(there == 1):
                    loads = [i * (32 if k % RING < PER - RING else 16) + 16 * (PAIRS * PER // RING + k // RING + 1)
                             for k in range(PER)]
                    pair(i + PAIRS, [exp_slot(0, k) for k in range(PER)], loads, True)
                    combine(i + PAIRS)
            pe.wait_ge(f_sq, KC)
            mean_square(0)

        @block.scalar
        def _(act):
            A = nc.scalar.activation
            step = Steps(act, act_steps)

            def root(k, ap):
                act.wait_ge(var_ready, k)
                A(ap, ap, ACT.Sqrt).then_inc(root_ready, 1)

            def modulate(k, shift):
                act.wait_ge(xn_ready, k)
                act.wait_ge(gain_ready, k)
                for m in range(KC):
                    last = A(hT[:, m, 0:TP], hT[:, m, 0:TP], ACT.Identity, bias=ada[:, shift, m, 0:1], scale=gain[:, m, 0:1])
                last.then_inc(hp_ready, 1)

            act.wait_ge(ld_vec, 16)
            A(csil, vc("c", KC), ACT.Silu).then_inc(c_ready, 1)
            root(1, rstd)
            modulate(1, SH_M)

            def conv_out(i):
                m = (i + 4) % KC
                act.wait_ge(conv_done, i + 1)
                c = cacc[:, i % 2, :]
                A(xbcT[:, m, 0:TP], c[:, 0:TP], ACT.Silu)
                for b0, nb in ((0, NSEQ - 1), (NSEQ - 1, 1)):
                    at = SEQ0 + b0 * (PAD + SL)
                    if nb > 1:
                        src = c[:, at:at + nb * (PAD + SL)].rearrange("p (b w) -> p b w", w=PAD + SL)[:, :, 0:SL]
                    else:
                        src = c[:, at:at + SL].rearrange("p (b w) -> p b w", b=1)
                    last = A(xbcT[:, m, TP + b0 * SL:TP + (b0 + nb) * SL].rearrange("p (b w) -> p b w", w=SL), src, ACT.Silu)
                last.then_inc(xbc_ready, 1)

            act.wait_ge(line_ready, 1)
            for i in range(KC):
                m = (i + 4) % KC
                act.wait_ge(xbc_mm, i + 1)
                A(line[:, m, PAD:SEQ0], ps[:, 6 + i % 2, 0:TP], ACT.Copy)
                A(line_seq(m, PAD, SL), ps[:, 6 + i % 2, TP:T].rearrange("p (b w) -> p b w", w=SL), ACT.Copy).then_inc(xbc_line, 1)
                act.wait_ge(xbc_line, i + 1)
                if i >= 2:
                    act.wait_ge(xbc_ready, i - 1)
                A(cacc[:, i % 2, :], line[:, m, 0:CONVN], ACT.Identity, bias=conv_b[:, m:m + 1],
                  scale=conv_w[:, 0, m:m + 1]).then_inc(conv_begun, 1)
                if i:
                    conv_out(i - 1)
            conv_out(KC - 1)
            for q, (dst, half) in enumerate([(vg, 1), (ug, 0)]):
                for t, (t0, n) in enumerate(TILES):
                    if q == 0 or t < NT - 1:
                        act.wait_ge(uv_mm, 3 * q + t + 1)
                    else:
                        act.wait_ge(front_used, FIRST["uv"] + 4)
                    A(dst[0:n, t, :], ps[0:n, 3 * half + t, :], ACT.Gelu).then_inc(gelu_done, 1)
            act.wait_ge(ld_row, 16)
            A(ea, rw("a_log"), ACT.Exp)
            act.wait_ge(dt_abs, 1)
            A(dte, dte, ACT.Exp, scale=-1.0).then_inc(dt_exp, 1)
            act.wait_ge(dt_one, 1)
            A(dtx, dtu, ACT.Ln).then_inc(dt_ln, 1)
            root(2, ssv)
            for t, (t0, n) in enumerate(TILES):
                if t < NT - 1:
                    act.wait_ge(z_mm, t + 1)
                else:
                    act.wait_ge(front_used, FIRST["z"] + 2)
                A(zs[0:n, t, :], ps[0:n, (6, 7, 3)[t], :], ACT.Silu).then_inc(z_silu, 1)
            for t, (t0, n) in enumerate(TILES):
                act.wait_ge(xb_tr, t + 1)
                A(xs[0:n, t, :], ps[0:n, 1, :], ACT.Copy)
                A(btok[0:n, t, :], ps[0:n, 2, 0:G * P], ACT.Copy).then_inc(xb_tok, 1)
            act.wait_ge(decay_mm, 1)
            A(dec[:, 0:4 * H], ps[:, 0, 0:4 * H], ACT.Exp)
            A(dec[0:TS, 4 * H:6 * H], ps[0:TS, 0, 4 * H:6 * H], ACT.Exp)
            A(dec[:, 6 * H:7 * H], ps[:, 0, 6 * H:7 * H], ACT.Exp)
            A(dec[:, 64:128], ps[:, 0, 64:128], ACT.Exp).then_inc(decays, 1)

            def decay_exp(t):
                n = TILES[t][1]
                act.wait_ge(l_mm, t + 1)
                if t:
                    act.wait_ge(m_ready, t)
                for q in range(2):
                    last = A(Lx[0:n, 4 * q:4 * q + 4, 0:n],
                             ps[0:n, 6 + q, :].rearrange("p (h l) -> p h l", h=4)[:, :, 0:n], ACT.Exp)
                last.then_inc(lx_ready, 1)

            decay_exp(0)
            decay_exp(1)
            act.wait_ge(st_mm, 1)
            A(st0, ps[:, 0, :], ACT.Copy).then_inc(st0_ready, 1)
            decay_exp(2)
            for t, (t0, n) in enumerate(TILES):
                act.wait_ge(ga_ready, t + 1)
                step(A(junk[0:n, :], cat[0:n, t, 0:AW], ACT.Square, accum_out=ss9[0:n, 0, t:t + 1]))
            for t, (t0, n) in enumerate(TILES):
                act.wait_ge(gb_ready, t + 1)
                for g in range(G):
                    step(A(junk[0:n, 0:256], cat[0:n, t, AW + g * 256:AW + (g + 1) * 256], ACT.Square,
                           accum_out=ss9[0:n, 1 + g, t:t + 1]))
            act.wait_ge(act_steps, step.count)
            A(tmp64[0:1, 0:1], ss9[0:1, 0, 0:1], ACT.Copy).then_inc(gb_sq, 1)
            root(3, ss9)
            for b in range(NSEQ):
                act.wait_ge(sn_mm, b + 1)
                if b >= 2:
                    act.wait_ge(sn_added, b - 1)
                A(snew[:, b % 2, :], ps[:, 5 + b % 2, :], ACT.Copy).then_inc(sn_copied, 1)
            for m in range(KC):
                act.wait_ge(x1_ready, m + 1)
                A(sq[:, m, :], xT[:, m, :], ACT.Square).then_inc(x1_sq, 1)
            root(4, rstd)
            modulate(2, SH_F)
            for t, (t0, n) in enumerate(TILES):
                act.wait_ge(h_tr, t + 1)
                A(htok[0:n, t, :].rearrange("p (a b) -> p a b", a=2), ps[0:n, 3:5, :], ACT.Copy).then_inc(htok_ready, 1)
            act.wait_ge(soft_in, 1)
            A(topw[:, :, 0:TOPK], topw[:, :, 0:TOPK], ACT.Exp).then_inc(soft_out, 1)

            def from_banks(bank, name, done):
                A(moe[name].rearrange("p (a b) -> p a b", a=2), ps[:, bank:bank + 2, :], ACT.Copy).then_inc(done, 1)

            def copy_x(q):
                act.wait_ge(x_mm, q + 1)
                from_banks(6, "X", x_tok)

            def copy_xT(q):
                act.wait_ge(x_tr, q + 1)
                from_banks(0, "X", x_ready)

            def sigmoid(q):
                act.wait_ge(g_ready, q + 1)
                A(moe["s"], moe["g"], ACT.Sigmoid, scale=ALPHA).then_inc(sig_ready, 1)

            def copy_act(q):
                act.wait_ge(a_tr, q + 1)
                from_banks(0, "g", actT_ready)

            def copy_sel(q):
                act.wait_ge(selT_tr, q + 1)
                A(moe["selT"], ps[:, 7, 0:T], ACT.Copy).then_inc(selT_ready, 1)

            def copy_y(q):
                act.wait_ge(exp_used, q * PER + PER)
                from_banks(4, "y", y_ready)

            copy_x(0)
            copy_xT(0)

            def act_turn(i):
                for j in range(UNROLL):
                    q = i * UNROLL + j
                    last = isinstance(q, int) and q == PAIRS - 1
                    sigmoid(q)
                    if not last:
                        copy_x(q + 1)
                    copy_act(q)
                    if not last:
                        copy_xT(q + 1)
                    copy_sel(q)
                    copy_y(q)

            turns(act.Fori, act_turn)
            with act.Fori(0, MORE_PAIRS) as i:
                there = act.value_load(more_i[0:1, 2, bass.ds(i * 2, 1)], min_val=0, max_val=1)
                with act.If(there == 1):
                    for copy in (copy_x, copy_xT, sigmoid, copy_act, copy_sel, copy_y):
                        copy(i + PAIRS)
            for m in range(KC):
                act.wait_ge(f_sq_in, m + 1)
                A(sq[:, m, :], xT[:, m, :], ACT.Square).then_inc(f_sq, 1)
            root(5, rstd)

        @block.vector
        def _(dve):
            V = nc.vector
            step = Steps(dve, dve_steps)

            def tt(o, a, b, op):
                return V.tensor_tensor(o, a, b, op)

            def inverse_root(k, o, src, n):
                V.tensor_scalar(o, src, 1.0 / n, EPS, ALU.mult, ALU.add).then_inc(var_ready, 1)
                dve.wait_ge(root_ready, k)
                step(V.reciprocal(o, o))

            def ada_rows(s, bank):
                dve.wait_ge(ada_mm, ada_rows.n + 1)
                ada_rows.n += 1
                tt(ada[:, s], ps[:, bank, 0:KC * 9].rearrange("p (m b) -> p m b", m=KC), wide(bada[:, s, :], 2, 9),
                   ALU.add).then_inc(ada_ready, 1)

            ada_rows.n = 0

            def gains(k, s, g):
                dve.wait_ge(ada_ready, {SC_M: 2, SC_F: 5}[s])
                V.scalar_tensor_tensor(gain, ada[:, s], 1.0, wide(vc(g), 2, 9), ALU.add, ALU.mult).then_inc(gain_ready, 1)
                dve.wait_ge(gain_ready, k)

            def by_seq(ap):
                return ap[:, :, TP:T].rearrange("p c (b j) -> p c b j", b=NSEQ)

            def modulate_sample(k, s):
                dve.wait_ge(xn_ready, k)
                step(tt(by_seq(hT), by_seq(hT), wide(gain[:, :, 1:9], 3, SL), ALU.mult))
                tt(by_seq(hT), by_seq(hT), wide(ada[:, s, :, 1:9], 3, SL), ALU.add).then_inc(hs_ready, 1)

            def normed(k, bank):
                dve.wait_ge(meansq, k)
                inverse_root({1: 1, 2: 4}[k], rstd, ps[:, bank, 0:T], D)
                tt(hT, xT, wide(rstd, 1, KC), ALU.mult).then_inc(xn_ready, 1)

            dve.wait_ge(ld_x, 16)
            tt(sq, xT, xT, ALU.mult).then_inc(x_sq, 1)
            step(V.memset(dtx, 0.0))
            step(V.memset(ssv, 0.0))
            step(V.memset(ss9, 0.0))
            step(V.memset(logit, 0.0))
            step(V.memset(rank, -1.0))
            step(V.memset(wgt, 0.0))
            dve.wait_ge(rep_mm, 1)
            dve.wait_ge(ld_con, 16)
            dve.wait_ge(ld_vec, 16)
            step(tt(w_sp, w_sp, wide(cn("upto"), 1, AH), ALU.mult))
            for h in range(AH):
                tt(wblk[0:TS, h, :].rearrange("p (b j) -> p b j", b=NSEQ), wide(ps[0:TS, 3, h * SL:(h + 1) * SL], 1, NSEQ),
                   cn("upto_s", TS).rearrange("p (b j) -> p b j", b=NSEQ), ALU.mult)
            for t in range(2):
                V.tensor_copy(bsp[:, t, :], vc("b_sp"))
            V.tensor_copy(bsp[0:TS, 2, :], ps[0:TS, 3, 64:64 + AH]).then_inc(rep_read, 1)
            normed(1, 0)
            ada_rows(SH_M, 1)
            ada_rows(SC_M, 2)
            gains(1, SC_M, "g_mix")
            modulate_sample(1, SH_M)
            for i in range(KC):
                m = (i + 4) % KC
                dve.wait_ge(conv_begun, i + 1)
                c = cacc[:, i % 2, :]
                for k in range(1, TAPS):
                    ins = V.scalar_tensor_tensor(c, line[:, m, k:k + CONVN], conv_w[:, k, m:m + 1], c, ALU.mult, ALU.add)
                    if k < TAPS - 1:
                        step(ins)
                ins.then_inc(conv_done, 1)
            dve.wait_ge(dt_mm, 1)
            dve.wait_ge(ld_row, 16)
            step(tt(dtx[:, 0:2, :], ps[:, 6, 0:2 * H].rearrange("p (t h) -> p t h", t=2), wide(rw("dt_bias"), 1, 2), ALU.add))
            step(tt(dtx[0:TS, 2, :], ps[0:TS, 6, 2 * H:3 * H], rw("dt_bias", TS), ALU.add))
            step(V.tensor_scalar(dtr, dtx, 0.0, None, ALU.max))
            V.scalar_tensor_tensor(dte, dtx, -1.0, dtx, ALU.mult, ALU.max).then_inc(dt_abs, 1)
            dve.wait_ge(dt_exp, 1)
            V.tensor_scalar(dtu, dte, 1.0, None, ALU.add).then_inc(dt_one, 1)
            dve.wait_ge(dt_one, 1)
            step(V.scalar_tensor_tensor(dt, dtu, -1.0, dte, ALU.add, ALU.subtract))
            step(tt(dt, dtr, dt, ALU.subtract))
            dve.wait_ge(dt_ln, 1)
            step(tt(dt, dt, dtx, ALU.add))
            step(V.scalar_tensor_tensor(dta, dt, -1.0, wide(ea, 1, NT), ALU.mult, ALU.mult))
            tt(dseq[0:TS], wide(dta[0:TS, 2, :], 1, NSEQ), wide(cn("seq", TS), 2, H), ALU.mult).then_inc(dta_ready, 1)
            dve.wait_ge(dta_ready, 1)

            def decay_sel(t):
                n = TILES[t][1]
                if t:
                    dve.wait_ge(l_mm, t)
                tt(sel_l[0:n, :, 0:n], wide(after(t), 1, H), wide(dta[0:n, t, :], 2, n), ALU.mult).then_inc(sl_ready, 1)

            decay_sel(0)
            dve.wait_ge(gelu_done, 3)
            both = slice(0, 2)
            step(tt(vsq[:, both], vg[:, both], vg[:, both], ALU.mult))
            step(tt(vsq[0:TS, 2], vg[0:TS, 2], vg[0:TS, 2], ALU.mult))
            step(V.tensor_reduce(ssv[:, both].rearrange("p t h -> p (t h)"), vsq[:, both].rearrange("p t (h e) -> p (t h) e", h=AH), AX.X, ALU.add))
            step(V.tensor_reduce(ssv[0:TS, 2], vsq[0:TS, 2].rearrange("p (h e) -> p h e", h=AH), AX.X, ALU.add))
            inverse_root(2, ssv, ssv, P)
            for rows, ts, n in ((P, both, 2), (TS, slice(2, 3), 1)):
                v4 = vg[0:rows, ts].rearrange("p t (h e) -> p (t h) e", h=AH)
                step(tt(v4, v4, wide(ssv[0:rows, ts].rearrange("p t h -> p (t h)"), 2, P), ALU.mult))
                ins = tt(vg[0:rows, ts], vg[0:rows, ts], wide(rw("g_v", rows), 1, n), ALU.mult)
                if n == 2:
                    step(ins)
            ins.then_inc(v_ready, 1)

            def scores(t):
                n = TILES[t][1]
                dve.wait_ge(g_mm, t + 1)
                tt(gm[0:n, :, 0:n], ps[0:n, 5, 0:G * P].rearrange("p (g l) -> p g l", g=G)[:, :, 0:n], wide(upto(t), 1, G),
                   ALU.mult).then_inc(gm_ready, 1)
                dve.wait_ge(gm_ready, t + 1)
                dve.wait_ge(lx_ready, t + 1)
                if t:
                    dve.wait_ge(y_mm, t)
                for g in range(G):
                    ins = tt(mdec[0:n, 4 * g:4 * g + 4, 0:n], Lx[0:n, 4 * g:4 * g + 4, 0:n], wide(gm[0:n, g, 0:n], 1, 4), ALU.mult)
                ins.then_inc(m_ready, 1)

            def gate_a(t):
                n = TILES[t][1]
                dve.wait_ge(s_mm, t + 1)
                dst = cat[0:n, t, 0:AW]
                tt(dst.rearrange("p (h e) -> p h e", h=AH), ps[0:n, 3, :].rearrange("p (h e) -> p h e", h=AH),
                   wide(bsp[0:n, t, :], 2, P), ALU.add).then_inc(s_read, 1)
                dve.wait_ge(s_read, t + 1)
                tt(dst, dst, ug[0:n, t, :], ALU.mult).then_inc(ga_ready, 1)

            def heads(ap):
                return ap.rearrange("p (h e) -> p h e", h=H)

            def weight_x(t):
                n = TILES[t][1]
                step(tt(heads(xdt[0:n, t, :]), heads(xs[0:n, t, :]), wide(dt[0:n, t, :], 2, HD), ALU.mult))
                ins = tt(heads(xw[0:n, t, :]), heads(xdt[0:n, t, :]), wide(dec[0:n, 2 * t * H:(2 * t + 1) * H], 2, HD), ALU.mult)
                if t < NT - 1:
                    step(ins)
                else:
                    ins.then_inc(xw_ready, 1)

            dve.wait_ge(gelu_done, 6)
            ada_rows(GT_M, 4)
            gate_a(0)
            dve.wait_ge(xb_tok, NT)
            dve.wait_ge(decays, 1)
            dve.wait_ge(st_conv, 16)
            for t in range(NT):
                weight_x(t)
            V.memset(tmp64[0:1, 0:1], 0.0).then_inc(xdt_ready, 1)
            scores(0)
            decay_sel(1)
            gate_a(1)
            gate_a(2)
            ada_rows(SH_F, 4)

            def y_out(t):
                n = TILES[t][1]
                dve.wait_ge(skip_ready, NT)
                dve.wait_ge(y_mm, t + 1)
                dst = cat[0:n, t, AW:D]
                if t:
                    step(tt(heads(xs[0:n, t, :]), heads(ps[0:n, 2, :]),
                            wide(dec[0:n, (2 * t + 1) * H:(2 * t + 2) * H], 2, HD), ALU.mult))
                    step(tt(dst, dst, xs[0:n, t, :], ALU.add))
                tt(dst, dst, ps[0:n, 1, :], ALU.add).then_inc(y_read, 1)
                dve.wait_ge(y_read, t + 1)
                tt(dst, dst, zs[0:n, t, :], ALU.mult).then_inc(gb_ready, 1)

            scores(1)
            decay_sel(2)
            y_out(0)
            y_out(1)
            scores(2)
            dve.wait_ge(st0_ready, 1)
            step(tt(heads(st1), heads(st0), wide(dec[:, 6 * H:7 * H], 2, HD), ALU.mult))
            dve.wait_ge(st_mm, 2)
            tt(st1, st1, ps[:, 0, :], ALU.add).then_inc(st1_ready, 1)
            y_out(2)
            dve.wait_ge(gb_sq, 1)
            step(V.tensor_scalar(ss9[:, 0, :], ss9[:, 0, :], 0.5, None, ALU.mult))
            inverse_root(3, ss9, ss9, 256)
            for t, (t0, n) in enumerate(TILES):
                V.tensor_scalar(cat[0:n, t, 0:AW], cat[0:n, t, 0:AW], ss9[0:n, 0, t:t + 1], None, ALU.mult)
                for g in range(G):
                    part = cat[0:n, t, AW + g * 256:AW + (g + 1) * 256]
                    ins = V.tensor_scalar(part, part, ss9[0:n, 1 + g, t:t + 1], None, ALU.mult)
                ins.then_inc(cat_ready, 1)
            for t, (t0, n) in enumerate(TILES):
                dve.wait_ge(cat_tr, t + 1)
                for q in range(2):
                    ins = tt(catT[:, 4 * q:4 * q + 4, t0:t0 + n],
                             ps[:, 3 + q, :].rearrange("p (m l) -> p m l", m=4)[:, :, 0:n],
                             wide(vc("g_cat")[:, 4 * q:4 * q + 4], 2, n), ALU.mult)
                ins.then_inc(catT_ready, 1)
            dve.wait_ge(ada_ready, 3)

            def residual(m, src, gate, done):
                step(V.scalar_tensor_tensor(xT[:, m, 0:TP], src[:, 0:TP], ada[:, gate, m, 0:1], xT[:, m, 0:TP], ALU.mult, ALU.add))
                step(tt(tmp64.rearrange("p (b j) -> p b j", b=NSEQ), src[:, TP:T].rearrange("p (b j) -> p b j", b=NSEQ),
                        wide(ada[:, gate, m, 1:9], 2, SL), ALU.mult))
                tt(xT[:, m, TP:T], xT[:, m, TP:T], tmp64, ALU.add).then_inc(done, 1)
                return

            for m in range(KC):
                dve.wait_ge(out_mm, m + 1)
                residual(m, ps[:, 6 + m % 2, 0:T], GT_M, x1_ready)
            ada_rows(SC_F, 0)
            ada_rows(GT_F, 1)
            gains(2, SC_F, "g_ffn")
            dve.wait_ge(x1_ready, KC)
            normed(2, 2)
            modulate_sample(2, SH_F)
            dve.wait_ge(router_mm, 1)
            step(tt(logit[:, 0:2, :], ps[:, 7, 0:2 * NE].rearrange("p (t e) -> p t e", t=2), wide(rw("b_router"), 1, 2), ALU.add))
            step(tt(logit[0:TS, 2, :], ps[0:TS, 7, 2 * NE:3 * NE], rw("b_router", TS), ALU.add))
            for t in range(NT):
                step(V.max(top[:, t, :], logit[:, t, :]))
                step(V.max_index(topi[:, t, :].bitcast(U32), top[:, t, :], logit[:, t, :]))
            step(V.tensor_copy(topf, topi.bitcast(U32)))
            tt(topw[:, :, 0:TOPK], top[:, :, 0:TOPK], top[:, :, 0:1].to_broadcast([P, NT, TOPK]), ALU.subtract).then_inc(soft_in, 1)
            for t in range(NT):
                ins = tt(onehot[:, t * TOPK:(t + 1) * TOPK, :], wide(cn("iota", P, NE), 1, TOPK),
                         wide(topf[:, t, 0:TOPK], 2, NE), ALU.is_equal)
                step(ins)
            picked2 = picked
            V.tensor_reduce(picked2, onehot.rearrange("p (t k) e -> p t e k", t=NT), AX.X, ALU.add).then_inc(picks_ready, 1)
            dve.wait_ge(soft_out, 1)
            step(V.tensor_reduce(den, topw[:, :, 0:TOPK], AX.X, ALU.add))
            step(V.reciprocal(den, den))
            step(tt(topw[:, :, 0:TOPK], topw[:, :, 0:TOPK], wide(den, 2, TOPK), ALU.mult))
            for t in range(NT):
                step(tt(onew[:, t * TOPK:(t + 1) * TOPK, :], onehot[:, t * TOPK:(t + 1) * TOPK, :],
                        wide(topw[:, t, 0:TOPK], 2, NE), ALU.mult))
            step(V.tensor_reduce(wgt[:, 0:NE, :].rearrange("p e t -> p t e"), onew.rearrange("p (t k) e -> p t e k", t=NT), AX.X, ALU.add))
            dve.wait_ge(rank_mm, 1)
            dve.wait_ge(picks_ready, 1)
            for rows, a, b in ((P, 0, 2), (TS, 2, 3)):
                r = rank[0:rows, 0:NE, a:b].rearrange("p e t -> p t e")
                ins = V.scalar_tensor_tensor(r, ps[0:rows, 2, a * NE:b * NE].rearrange("p (t e) -> p t e", e=NE), 1.0,
                                             picked[0:rows, a:b, :], ALU.add, ALU.mult)
                if rows == P:
                    step(ins)
            ins.then_inc(rank_read, 1)
            dve.wait_ge(rank_read, 1)
            step(V.tensor_scalar(rank[:, 0:NE, 0:2], rank[:, 0:NE, 0:2], -1.0, None, ALU.add))
            step(V.tensor_scalar(rank[0:TS, 0:NE, 2:3], rank[0:TS, 0:NE, 2:3], -1.0, None, ALU.add))
            dve.wait_ge(cnt_mm, 1)
            V.tensor_tensor(flag[0:NE, :], ps[0:NE, 5, 0:1].to_broadcast([NE, PASSES - 1]), cn("thr", NE), ALU.is_gt).then_inc(flag_ready, 1)
            dve.wait_ge(place_mm, 1)
            V.tensor_copy(place[0:NE, :], ps[0:NE, 5, 8:8 + PASSES - 1]).then_inc(place_read, 1)
            dve.wait_ge(place_read, 1)
            dve.wait_ge(flag_ready, 1)
            for p in range(PASSES - 1):
                step(V.tensor_scalar(oh[0:NE, p, :], cn("iota", NE, LW), place[0:NE, p:p + 1], flag[0:NE, p:p + 1],
                                     ALU.is_equal, ALU.mult))
            tt(ohb[0:NE], oh[0:NE], wide(cn("thr", NE), 2, LW), ALU.mult).then_inc(oh_ready, 1)
            dve.wait_ge(more_mm, 1)
            V.tensor_copy(more_f, ps[:, 5, 32:32 + 3 * LW].rearrange("p (q j) -> p q j", q=3)).then_inc(more_read, 1)
            dve.wait_ge(more_read, 1)
            step(V.scalar_tensor_tensor(more_f[:, 1, :], more_f[:, 2, :], -FAR, more_f[:, 1, :], ALU.mult, ALU.add))
            step(V.tensor_scalar(more_f[:, 1, :], more_f[:, 1, :], FAR, None, ALU.add))
            V.tensor_copy(more_i, more_f).then_inc(more_ready, 1)
            V.memset(acc, 0.0).then_inc(moe_zero, 1)
            dve.wait_ge(moe_zero, 1)

            def blocks(bank):
                return ps[:, bank:bank + 2, :]

            def halves(name):
                return moe[name].rearrange("p (a b) -> p a b", a=2)

            def of(table, q):
                return lambda s, t, r: table[0:r, bass.ds(q * 2 + s, 1), t:t + 1].rearrange("p e t -> p (e t)")

            def select(q, place_of):
                for t, (t0, r) in enumerate(TILES):
                    for s in range(2):
                        ins = V.tensor_scalar(moe["sel"][0:r, t, s * CAP:(s + 1) * CAP], cn("iota", r, CAP),
                                              place_of(s, t, r), None, ALU.is_equal)
                ins.then_inc(sel_ready, 1)

            def select_weighted(q, place_of, weight_of):
                for t, (t0, r) in enumerate(TILES):
                    for s in range(2):
                        ins = V.tensor_scalar(moe["selw"][0:r, t, s * CAP:(s + 1) * CAP], cn("iota", r, CAP),
                                              place_of(s, t, r), weight_of(s, t, r), ALU.is_equal, ALU.mult)
                ins.then_inc(selw_ready, 1)

            def pick_bias(experts):
                for m in range(3):
                    for s in range(2):
                        ins = V.tensor_copy(moe["pick"][:, m, s * CAP:(s + 1) * CAP],
                                            cn("ident")[:, bass.ds(experts(s) + NE * m, 1)].to_broadcast([P, CAP]))
                ins.then_inc(pick_ready, 1)

            def activate(q):
                g, s = moe["g"], moe["s"]
                dve.wait_ge(exp_used, q * PER + 8)
                V.tensor_scalar(halves("g"), blocks(0), LIMIT, None, ALU.min).then_inc(g_ready, 1)
                dve.wait_ge(sig_ready, q + 1)
                step(tt(g, g, s, ALU.mult))
                dve.wait_ge(exp_used, q * PER + 16)
                step(V.tensor_scalar(halves("s"), blocks(2), LIMIT, -LIMIT, ALU.min, ALU.max))
                V.scalar_tensor_tensor(g, s, 1.0, g, ALU.add, ALU.mult).then_inc(act_ready, 1)

            def add_up(q):
                for m in range(KC):
                    dve.wait_ge(comb_mm, q * KC + (m + 1))
                    tt(acc[:, m, :], acc[:, m, :], ps[:, (2, 3, 6)[m % 3], 0:T], ALU.add).then_inc(comb_added, 1)

            OWN = 2
            select(0, of(rank, 0))
            dve.wait_ge(h_tr, NT)
            dve.wait_ge(router_mm, 1)
            pick_bias(lambda s: s)
            start = step.count

            def dve_turn(i):
                for j in range(UNROLL):
                    q = i * UNROLL + j
                    first, last = isinstance(q, int) and q == 0, isinstance(q, int) and q == PAIRS - 1
                    step.count, step.n = start + j * OWN + i * (UNROLL * OWN), 0
                    if not last:
                        dve.wait_ge(x_mm, q + 1)
                        select(q + 1, of(rank, q + 1))
                    wait(dve, selT_tr, q)
                    select_weighted(q, of(rank, q), of(wgt, q))
                    activate(q)
                    if not first:
                        add_up(q - 1)
                    if not last:
                        dve.wait_ge(exp_used, q * PER + 17)
                        pick_bias(lambda s: (q + 1) * 2 + s)
                    assert step.n == OWN

            turns(dve.Fori, dve_turn)
            add_up(PAIRS - 1)
            start = start + PAIRS * OWN
            MORE_OWN = OWN + 2
            with dve.Fori(0, MORE_PAIRS) as i:
                there = dve.value_load(more_i[0:1, 2, bass.ds(i * 2, 1)], min_val=0, max_val=1)
                with dve.If(there == 1):
                    es = [dve.value_load(more_i[0:1, 0, bass.ds(i * 2 + s, 1)], min_val=0, max_val=NE - 1) for s in range(2)]
                    step.count, step.n = start + i * MORE_OWN, 0
                    q = i + PAIRS
                    for s in range(2):
                        step(V.tensor_scalar(rk_more[:, s, :], rank[:, bass.ds(es[s], 1), :].rearrange("p e t -> p (e t)"),
                                             more_f[:, 1, bass.ds(i * 2 + s, 1)], None, ALU.subtract))
                    of_more = lambda s, t, r: rk_more[0:r, s, t:t + 1]
                    dve.wait_ge(comb_mm, q * KC)
                    select(q, of_more)
                    select_weighted(q, of_more,
                                    lambda s, t, r: wgt[0:r, bass.ds(es[s], 1), t:t + 1].rearrange("p e t -> p (e t)"))
                    pick_bias(lambda s: es[s])
                    activate(q)
                    add_up(q)
                    assert step.n == MORE_OWN
            step = Steps(dve, sem("dve_tail_steps"))
            for m in range(KC):
                residual_tail(V, step, tt, m, xT, acc, ada, tmp64, wide, f_sq_in)
            dve.wait_ge(f_sq_in, KC)
            dve.wait_ge(meansq, 3)
            V.tensor_scalar(rstd, ps[:, 0, 0:T], 1.0 / D, EPS, ALU.mult, ALU.add).then_inc(var_ready, 1)
            dve.wait_ge(root_ready, 5)
            step(V.reciprocal(rstd, rstd))
            for m in range(KC):
                V.scalar_tensor_tensor(hT[:, m, :], xT[:, m, :], vc("g_final")[:, m:m + 1], rstd, ALU.mult, ALU.mult).then_inc(yfin, 1)

        @block.gpsimd
        def _(pool):
            Q = nc.gpsimd
            step = Steps(pool, pool_steps)
            step(Q.memset(line[:, :, 0:PAD], 0.0))
            step(Q.memset(cmask, 0.0))
            pool.wait_ge(ld_vec, 16)
            for m in range(KC):
                ins = Q.tensor_copy(line_seq(m, 0, PAD), prev[:, m * NSEQ:(m + 1) * NSEQ, :])
            ins.then_inc(line_ready, 1)
            pool.wait_ge(xbc_line, KC)
            step(Q.tensor_copy(cnew[:, :, 0:PAD], line[:, :, TP:TP + PAD]))
            for m in range(KC):
                step(Q.tensor_copy(cnew[:, m, PAD:].rearrange("p (b w) -> p b w", w=PAD), line_seq(m, SL, PAD)))
            pool.dma_start(out["convT"].rearrange("(c p) t -> p c t", p=P), cnew).then_inc(st_conv, 16)
            pool.wait_ge(xbc_ready, KC)
            for g in range(G):
                diag = cmask[:, g, :].rearrange("p (b w) -> p b w", w=TS + SL)[:, :, 0:SL]
                ins = Q.tensor_copy(diag, xbcT[:, 6 + g, TP:T].rearrange("p (b w) -> p b w", w=SL))
            ins.then_inc(cmask_ready, 1)
            pool.wait_ge(xb_tok, NT)
            pool.wait_ge(v_ready, 1)
            pool.wait_ge(ld_row, 16)
            for t, (t0, n) in enumerate(TILES):
                Q.tensor_tensor(cat[0:n, t, AW:D].rearrange("p (h e) -> p h e", h=H),
                                xs[0:n, t, :].rearrange("p (h e) -> p h e", h=H),
                                wide(rw("d_skip", n), 2, HD), ALU.mult).then_inc(skip_ready, 1)
            for g in range(G):
                ins = Q.tensor_tensor(bmask[0:TS, g], wide(btok[0:TS, 2, g * P:(g + 1) * P], 1, NSEQ),
                                      wide(cn("seq", TS), 2, P), ALU.mult)
            ins.then_inc(bmask_ready, 1)
            pool.dma_start(out["v"], vg[0:TS, 2, :]).then_inc(st_v, 16)
            pool.wait_ge(st1_ready, 1)
            pool.dma_start(out["ssmpT"], st1).then_inc(st_ssmp, 16)
            pool.wait_ge(y_mm, NT)
            pool.wait_ge(decays, 1)
            s0h = s0T.rearrange("p b (h e) -> p (b h) e", e=HD)
            step(Q.tensor_tensor(s0h, s0h, wide(dec[:, 64:128], 2, HD), ALU.mult))
            for b in range(NSEQ):
                pool.wait_ge(sn_copied, b + 1)
                Q.tensor_tensor(s0T[:, b, :], s0T[:, b, :], snew[:, b % 2, :], ALU.add).then_inc(sn_added, 1)
            pool.wait_ge(sn_added, NSEQ)
            pool.dma_start(out["ssmsT"], s0T).then_inc(st_ssms, 16)
            pool.wait_ge(st_ssms, 16)
            pool.wait_ge(st_ssmp, 16)
            pool.wait_ge(st_v, 16)
            pool.wait_ge(st_conv, 16)


def residual_tail(V, step, tt, m, xT, acc, ada, tmp64, wide, done):
    step(V.scalar_tensor_tensor(xT[:, m, 0:TP], acc[:, m, 0:TP], ada[:, GT_F, m, 0:1], xT[:, m, 0:TP], ALU.mult, ALU.add))
    step(tt(tmp64.rearrange("p (b j) -> p b j", b=NSEQ), acc[:, m, TP:T].rearrange("p (b j) -> p b j", b=NSEQ),
            wide(ada[:, GT_F, m, 1:9], 2, SL), ALU.mult))
    tt(xT[:, m, TP:T], xT[:, m, TP:T], tmp64, ALU.add).then_inc(done, 1)


def kernel(**inputs):
    import concourse.bacc as bacc
    from concourse.bass_utils import run_bass_kernel_spmd

    a = {k: np.asarray(v) for k, v in inputs.items()}

    def feat(x):
        x = x.reshape(-1, x.shape[-1] // P, P)
        return x

    def chunk_first(x):
        return feat(x).transpose(2, 1, 0).reshape(P, -1)

    def row_first(x):
        return feat(x).transpose(2, 0, 1).reshape(P, -1)

    x = np.concatenate([a["x_prompt"].reshape(-1, D), a["x_sample"].reshape(-1, D)])
    c = np.concatenate([a["c_prompt"], a["c_sample"]])
    b_sp = a["b_spatial"][0].T
    parts = {
        "c": chunk_first(c), "b_ada": row_first(a["b_ada"]), "g_mix": row_first(a["g_mix"]), "g_ffn": row_first(a["g_ffn"]),
        "g_final": row_first(a["g_final"][None]),
        "g_cat": row_first(np.concatenate([a["g_out_a"], a["g_out_b"]], axis=1)),
        "conv_w": row_first(a["conv_w"][0]), "conv_b": row_first(a["conv_b"]),
        "b_exp": np.concatenate([a["b_gate"][0], a["b_up"][0], a["b_down"][0], np.zeros((P - 3 * NE, D), np.float32)]),
        "w_router": a["w_router"][0].reshape(KC, P, NE).transpose(1, 0, 2).reshape(P, -1),
        "w_dt": a["w_in"][0][:, IN_DIM - H:].reshape(KC, P, H).transpose(1, 0, 2).reshape(P, -1),
        "w_sp": a["w_spatial"][0].transpose(2, 0, 1).reshape(P, -1), "b_sp": b_sp,
        "prev": chunk_first(a["state_conv"][0].reshape(NSEQ * PAD, D)),
    }
    vec = np.concatenate([parts[n] for n in VEC], axis=1)
    row = np.concatenate([a[n].reshape(1, -1) for n in ("g_v_a", "dt_bias", "a_log", "d_skip", "b_router")], axis=1)
    arrays = {
        "xT": x.T, "vec": vec, "row": row, "con": constants(),
        "s0T": a["state_ssm"][0].reshape(NSEQ, AW, P).transpose(2, 0, 1),
        "w_in": a["w_in"][0], "w_ada": a["w_ada"][0], "w_out": a["w_out"][0],
        "w_gate": a["w_gate"][0], "w_up": a["w_up"][0], "w_down": a["w_down"][0],
    }
    arrays = {k: np.ascontiguousarray(v) for k, v in arrays.items()}
    nc = bacc.Bacc("TRN2", target_bir_lowering=False, num_devices=1)
    d = {k: nc.dram_tensor(f"in_{k}", v.shape, F32, kind="ExternalInput").ap() for k, v in arrays.items()}
    shapes = {"yT": (D, T), "convT": (D, PAD * (1 + NSEQ)), "v": (TS, AW), "ssmpT": (P, AW), "ssmsT": (P, NSEQ, AW)}
    out = {k: nc.dram_tensor(f"out_{k}", s, F32, kind="ExternalOutput").ap() for k, s in shapes.items()}
    build(nc, d, out)
    r = run_bass_kernel_spmd(nc, [{f"in_{k}": v for k, v in arrays.items()}], core_ids=[0]).results[0]
    y = r["out_yT"].T
    conv = r["out_convT"].T
    return (
        np.ascontiguousarray(y[:TP]).reshape(1, TP, D),
        np.ascontiguousarray(y[TP:]).reshape(NSEQ, SL, D),
        np.ascontiguousarray(r["out_ssmpT"].T).reshape(1, 1, H, HD, P),
        np.ascontiguousarray(conv[:PAD]).reshape(1, 1, PAD, D),
        np.ascontiguousarray(r["out_ssmsT"].transpose(1, 2, 0)).reshape(1, NSEQ, H, HD, P),
        np.ascontiguousarray(conv[PAD:]).reshape(1, NSEQ, PAD, D),
        np.ascontiguousarray(r["out_v"]).reshape(1, NSEQ, SL, AW),
    )
```

```python
from contextlib import ExitStack

import numpy as np

import concourse.bass as bass
from concourse import mybir

ALU = mybir.AluOpType
ACT = mybir.ActivationFunctionType
AX = mybir.AxisListType
F32 = mybir.dt.float32
I32 = mybir.dt.int32
U32 = mybir.dt.uint32

P = 128
D = 1024
KC = D // P
TP = 256
NSEQ = 8
SL = 8
TS = NSEQ * SL
T = TP + TS
TILES = [(0, P), (P, P), (TP, TS)]
NT = len(TILES)
ORDER = (2, 0, 1)
AW = 512
AH = 4
H = 8
HD = 64
G = 2
TAPS = 4
PAD = TAPS - 1
CONVW = PAD + TP + NSEQ * (PAD + SL)
CONVN = CONVW - PAD
SEQ0 = PAD + TP
IN_DIM = 2568
NE = 32
TOPK = 4
CAP = 64
PASSES = -(-T // CAP)
MORE = T * TOPK // (CAP + 1)
EPS = 1e-6
LIMIT = 7.0
ALPHA = 1.702

UNIT = 2048
RING = 16
FS = 6
PER = 24
UNROLL = 2
PAIRS = NE // 2
MORE_PAIRS = -(-MORE // 2)
LW = 2 * MORE_PAIRS
ARENA = 53208
FAR = 1000.0


def layout(spec):
    out, at = {}, 0
    for name, width in spec:
        out[name] = (at, width)
        at += width
    return out, at


VEC, VECW = layout([("c", KC * (1 + NSEQ)), ("b_ada", 48), ("g_mix", KC), ("g_ffn", KC), ("g_final", KC),
                    ("g_cat", KC), ("conv_w", TAPS * KC), ("conv_b", KC), ("w_dt", KC * H),
                    ("prev", KC * NSEQ * PAD), ("w_sp", AH * P), ("b_sp", AH), ("w_router", KC * NE), ("b_exp", D)])
VECA = VEC["w_sp"][0]
ROW, ROWW = layout([("g_v", AW), ("dt_bias", H), ("a_log", H), ("d_skip", H), ("b_router", NE)])
CON, CONW = layout([("upto", P), ("after", P), ("ident", P), ("ones", P), ("before", P), ("upto_s", TS),
                    ("after_s", TS), ("seq", NSEQ), ("rep", TS), ("iota", CAP), ("thr", PASSES - 1), ("eidx", P), ("gather9", 2 * (1 + NSEQ)), ("gather32", NE)])


def constants():
    k = np.arange(P)[:, None]
    m = np.arange(P)[None, :]
    out = np.zeros((P, CONW), np.float32)

    def put(name, a):
        at = CON[name][0]
        out[:a.shape[0], at:at + a.shape[1]] = a

    ks, ms = k[:TS], m[:, :TS]
    same = ks // SL == ms // SL
    put("upto", (k <= m).astype(np.float32))
    put("after", (k > m).astype(np.float32))
    put("ident", (k == m).astype(np.float32))
    put("ones", np.ones((P, P), np.float32))
    put("before", (k < m).astype(np.float32))
    put("upto_s", ((ks <= ms) & same).astype(np.float32))
    put("after_s", ((ks > ms) & same).astype(np.float32))
    put("seq", (ks // SL == np.arange(NSEQ)[None, :]).astype(np.float32))
    put("rep", (np.arange(SL)[:, None] == ms % SL).astype(np.float32))
    put("iota", np.broadcast_to(np.arange(CAP, dtype=np.float32), (P, CAP)))
    put("thr", np.broadcast_to(CAP * np.arange(1, PASSES, dtype=np.float32), (P, PASSES - 1)))
    put("eidx", np.broadcast_to(np.arange(NE, dtype=np.float32)[:, None], (NE, P)))
    which = np.arange(P)
    for half in range(2):
        for s in range(1 + NSEQ):
            out[(which % 32 == s) & (which // 32 % 2 == half), CON["gather9"][0] + half * (1 + NSEQ) + s] = 1.0
    put("gather32", (which[:, None] % NE == np.arange(NE)[None, :]).astype(np.float32))
    return out


FRONT = ([("ada0", j) for j in range(4)] + [("ada1", j) for j in range(4)] + [("xbc", j) for j in range(4)]
         + [("uv", j) for j in range(4)] + [("z", j) for j in range(2)] + [("ada2", j) for j in range(4)]
         + [("ada3", j) for j in range(4)] + [("ada4", j) for j in range(4)] + [("ada5", j) for j in range(4)]
         + [("out", j) for j in range(4)])
FIRST = {}
for _u, (_m, _j) in enumerate(FRONT):
    FIRST.setdefault(_m, _u)
NF = len(FRONT)
SH_M, SC_M, GT_M, SH_F, SC_F, GT_F = range(6)
SPATIAL = (5, 3, 5)
XB = ((1, 2), (0, 6), (1, 2))
CATB = (3, 1, 3)
HTOK = (3, 5, 0)


class Steps:

    def __init__(self, eng, sem):
        self.eng, self.sem, self.count, self.n = eng, sem, 0, 0

    def __call__(self, ins):
        self.count = self.count + 1
        self.n += 1
        ins.then_inc(self.sem, 1)
        self.eng.wait_ge(self.sem, self.count)


def wait(eng, sem, count):
    if not (isinstance(count, int) and count <= 0):
        eng.wait_ge(sem, count)


def turns(engine_loop, body):
    body(0)
    with engine_loop(1, PAIRS // UNROLL - 1) as i:
        body(i)
    body(PAIRS // UNROLL - 1)


def further_pairs(engine, there, body):
    with engine.If(there(engine, 0) == 1):
        body(0)
    with engine.If(there(engine, 1) == 1):
        with engine.Fori(1, MORE_PAIRS) as i:
            with engine.If(there(engine, i) == 1):
                body(i)


def build(nc, d, out):
    with ExitStack() as ctx:
        arena = ctx.enter_context(nc.sbuf_tensor("arena", [P, ARENA], F32))
        used = [0]

        def view(at, shape, rows=P):
            n = int(np.prod(shape))
            ap = arena[0:rows, at:at + n]
            if len(shape) == 2:
                ap = ap.rearrange("p (a b) -> p a b", a=shape[0])
            if len(shape) == 3:
                ap = ap.rearrange("p (a b c) -> p a b c", a=shape[0], b=shape[1])
            return ap

        def sb(shape):
            at = used[0]
            used[0] += -(-int(np.prod(shape)) // 8) * 8
            assert used[0] <= ARENA, used[0]
            return view(at, shape), at

        ring, ring_at = sb([RING, UNIT])
        vec, _ = sb([VECW])
        row, _ = sb([ROWW])
        con, _ = sb([CONW])
        xT, _ = sb([KC, T])
        hT, moe_at = sb([KC, T])
        line, work_at = sb([KC, CONVW])
        catT = hT
        acc, acc_at = sb([KC, T])
        sq = acc
        Lx = view(acc_at, [H, P])
        sel_l = [view(acc_at + H * P, [H, P]), view(moe_at + G * P, [H, P]), view(moe_at + G * P + H * P, [H, P])]
        junk = view(acc_at + 2 * H * P, [AW])
        cat, cat_at = sb([NT, D])
        htok = cat
        cacc = view(cat_at, [2, CONVN])
        vsq = view(cat_at, [NT, AW])

        def tiny(shape):
            return sb(shape)[0]

        csil = tiny([KC, 32])
        ada = tiny([6, KC, 1 + NSEQ])
        gain = tiny([KC, 1 + NSEQ])
        rstd = tiny([T])
        dtx = tiny([NT, H])
        dtr = tiny([NT, H])
        dte = tiny([NT, H])
        dtu = tiny([NT, H])
        dt = tiny([NT, H])
        dta = tiny([NT, H])
        ea = tiny([H])
        dseq = tiny([NSEQ, H])
        dec = tiny([P])
        ssv = tiny([NT, AH])
        ss9 = tiny([3, NT])
        wblk = tiny([AH, TS])
        bsp = tiny([NT, AH])
        tmp64 = tiny([TS])
        cnew = view(acc_at, [KC, PAD * (1 + NSEQ)])
        mdec = view(work_at, [H, P])
        logT = view(work_at, [T])
        xdt = view(work_at + H * P, [NT, AW])
        at = moe_at
        sel, sel_at = sb([NT, 2 * CAP])
        moe = {"sel": sel}
        adat = view(sel_at, [2, AW])
        for name, shape in [("X", [D]), ("g", [D]), ("s", [D]), ("y", [D]), ("selT", [T]), ("selw", [NT, 2 * CAP]),
                            ("pick", [3, 2 * CAP])]:
            moe[name] = view(at, shape)
            at += int(np.prod(shape))
        assert at <= work_at + KC * CONVW
        logit, _ = sb([NT, NE])
        top, _ = sb([NT, 8])
        topi, _ = sb([NT, 8])
        topf, _ = sb([NT, 8])
        topw, _ = sb([NT, 8])
        den, _ = sb([NT])
        picked, _ = sb([NT, NE])
        rank, _ = sb([NE, NT])
        wgt, _ = sb([NE, NT])
        rk_more, _ = sb([2, NT])
        flag, _ = sb([PASSES - 1])
        place, _ = sb([PASSES - 1])
        oh, _ = sb([PASSES - 1, LW])
        ohb, _ = sb([PASSES - 1, LW])
        more_f, _ = sb([3, LW])
        more_i = sb([3, LW])[0].bitcast(I32)
        onehot = view(acc_at, [NT * TOPK, NE])
        onew = view(acc_at + NT * TOPK * NE, [NT * TOPK, NE])
        sb([max(0, sel_at + 2 * AW - used[0])])
        up = [ring_at + FS * UNIT]

        def scratch(shape):
            n = int(np.prod(shape))
            at = up[0]
            up[0] += n
            assert up[0] <= ring_at + RING * UNIT
            return view(at, shape)

        xs = scratch([NT, AW])
        zs = scratch([NT, AW])
        ug = scratch([NT, AW])
        vg = scratch([NT, AW])
        gates_end = up[0]
        st0 = scratch([AW])
        xbcT = scratch([KC, T])
        btok = scratch([NT, G * P])
        cmask = scratch([G, NSEQ * (TS + SL)])
        scores_end = up[0]
        bmask = scratch([G, NSEQ, P])
        xw = scratch([NT, AW])
        st1 = scratch([AW])
        snew = scratch([2, AW])
        s0T = scratch([NSEQ, AW])
        gm = view(moe_at, [G, P])

        ps = ctx.enter_context(nc.psum_tensor("ps", [P, 8, 512], F32))
        block_sems = {}

        def sem(name):
            if name not in block_sems:
                block_sems[name] = ctx.enter_context(nc.semaphore(name))
            return block_sems[name]

        def vc(name, shape=None, rows=P):
            a, w = VEC[name]
            ap = vec[0:rows, a:a + w]
            return ap if shape is None else ap.rearrange("p (a b) -> p a b", a=shape)

        def cn(name, rows=P, width=None):
            a, w = CON[name]
            return con[0:rows, a:a + (width or w)]

        def rw(name, rows=P):
            a, w = ROW[name]
            return row[0:rows, a:a + w]

        def wide(ap, axis, n):
            shape = list(ap.shape)
            ap = ap.unsqueeze(axis)
            shape.insert(axis, n)
            return ap.to_broadcast(shape)

        conv_w = vc("conv_w", TAPS)
        conv_b = vc("conv_b")
        b_exp = vc("b_exp")
        bada = vc("b_ada", 6)
        w_router = vc("w_router", KC)
        w_dt = vc("w_dt", KC)
        w_sp = vc("w_sp", AH)
        prev = vc("prev", KC * NSEQ)

        def upto(t):
            return cn("upto") if t < 2 else cn("upto_s", TS)

        def after(t):
            return cn("after") if t < 2 else cn("after_s", TS)

        def line_seq(m, first, n):
            return line[:, m, SEQ0:CONVW].rearrange("p (b w) -> p b w", w=PAD + SL)[:, :, first:first + n]

        ld_x, ld_vec, ld_vec2, ld_row, ld_con, ld_s0 = (
            sem(n) for n in ("ld_x", "ld_vec", "ld_vec2", "ld_row", "ld_con", "ld_s0"))
        front_landed = [sem(f"front_landed{i}") for i in range(FS)]
        front_used = sem("front_used")
        exp_landed = [sem(f"exp_landed{i}") for i in range(RING)]
        exp_used = sem("exp_used")
        x_sq, meansq, var_ready, root_ready, xn_ready = (sem(n) for n in ("x_sq", "meansq", "var_ready", "root_ready", "xn_ready"))
        c_zero, c_ready, ada_mm, adat_ready, ada_tr, ada_ready, gain_ready = (
            sem(n) for n in ("c_zero", "c_ready", "ada_mm", "adat_ready", "ada_tr", "ada_ready", "gain_ready"))
        hp_ready, hs_ready = sem("hp_ready"), sem("hs_ready")
        rep_mm, rep_read = sem("rep_mm"), sem("rep_read")
        line_ready, xbc_mm, xbc_line, conv_begun, conv_done, xbc_ready = (
            sem(n) for n in ("line_ready", "xbc_mm", "xbc_line", "conv_begun", "conv_done", "xbc_ready"))
        dt_mm, dt_abs, dt_exp, dt_one, dt_ln, dta_ready = (
            sem(n) for n in ("dt_mm", "dt_abs", "dt_exp", "dt_one", "dt_ln", "dta_ready"))
        uv_mm, gelu_done, z_mm, z_silu = (sem(n) for n in ("uv_mm", "gelu_done", "z_mm", "z_silu"))
        v_ready, s_mm, s_read, ga_ready = (sem(n) for n in ("v_ready", "s_mm", "s_read", "ga_ready"))
        xb_tr, xb_tok, decay_mm, decays = (sem(n) for n in ("xb_tr", "xb_tok", "decay_mm", "decays"))
        sl_ready, l_mm, lx_ready, g_mm, gm_ready, m_ready = (
            sem(n) for n in ("sl_ready", "l_mm", "lx_ready", "g_mm", "gm_ready", "m_ready"))
        xdt_ready, xw_ready, skip_ready, cmask_ready, bmask_ready = (
            sem(n) for n in ("xdt_ready", "xw_ready", "skip_ready", "cmask_ready", "bmask_ready"))
        y_mm, y_read, gb_ready, gb_sq, st_mm, st0_ready, st1_ready = (
            sem(n) for n in ("y_mm", "y_read", "gb_ready", "gb_sq", "st_mm", "st0_ready", "st1_ready"))
        sn_mm, sn_copied, sn_added = sem("sn_mm"), sem("sn_copied"), sem("sn_added")
        cat_ready, cat_tr, catT_ready, out_mm, x1_ready, x1_sq = (
            sem(n) for n in ("cat_ready", "cat_tr", "catT_ready", "out_mm", "x1_ready", "x1_sq"))
        h_tr, htok_ready, router_mm, picks_ready, rank_mm = (
            sem(n) for n in ("h_tr", "htok_ready", "router_mm", "picks_ready", "rank_mm"))
        sq_added = sem("sq_added")
        logit_mm, logT_ready = sem("logit_mm"), sem("logT_ready")
        soft_in, soft_out, cnt_mm, place_mm, oh_ready, more_mm, more_ready, rank_read, place_read, more_read, flag_ready = (
            sem(n) for n in ("soft_in", "soft_out", "cnt_mm", "place_mm", "oh_ready", "more_mm", "more_ready",
                             "rank_read", "place_read", "more_read", "flag_ready"))
        moe_zero = sem("moe_zero")
        sel_ready, selw_ready, pick_ready, x_mm, x_ready = (
            sem(n) for n in ("sel_ready", "selw_ready", "pick_ready", "x_mm", "x_ready"))
        g_ready, sig_ready, act_ready, a_tr, actT_ready, y_ready, selT_tr, selT_ready, comb_mm, comb_added = (
            sem(n) for n in ("g_ready", "sig_ready", "act_ready", "a_tr", "actT_ready", "y_ready", "selT_tr", "selT_ready",
                             "comb_mm", "comb_added"))
        f_sq_in, f_sq, yfin = sem("f_sq_in"), sem("f_sq"), sem("yfin")
        st_v, st_conv, st_ssmp, st_ssms, st_y = (sem(n) for n in ("st_v", "st_conv", "st_ssmp", "st_ssms", "st_y"))
        dve_steps, act_steps, pool_steps = sem("dve_steps"), sem("act_steps"), sem("pool_steps")

        w_in = d["w_in"].rearrange("(c p) n -> p c n", p=P)
        w_ada = d["w_ada"].rearrange("(c p) n -> p c n", p=P)
        w_out = d["w_out"].rearrange("(c p) n -> p c n", p=P)
        w_exp = [d[n].rearrange("e (c p) n -> e p c n", p=P) for n in ("w_gate", "w_up", "w_down")]

        def front_source(m, j):
            if m.startswith("ada"):
                s = int(m[3:])
                return w_ada[:, 2 * j:2 * j + 2, s * D:(s + 1) * D]
            if m == "xbc":
                return w_in[:, 2 * j:2 * j + 2, 3 * AW:3 * AW + D]
            if m == "uv":
                return w_in[:, 2 * j:2 * j + 2, 0:2 * AW]
            if m == "z":
                return w_in[:, 4 * j:4 * j + 4, 2 * AW:3 * AW]
            return w_out[:, 2 * j:2 * j + 2, :]

        def exp_slot(j, k):
            return (FS + PER * j + k) % RING

        def exp_source(k, e):
            m, p = k // 8, k // 2 % 4
            return w_exp[m][bass.ds(e(k % 2), 1), :, 2 * p:2 * p + 2, :].rearrange("e p c n -> p (e c) n")

        def there(eng, i):
            return eng.value_load(more_i[0:1, 2, bass.ds(i * 2, 1)], min_val=0, max_val=1)

        def listed(eng, i):
            return [eng.value_load(more_i[0:1, 0, bass.ds(i * 2 + s, 1)], min_val=0, max_val=NE - 1) for s in range(2)]

        block = ctx.enter_context(nc.Block())

        @block.sync
        def _(sp):
            sp.dma_start(xT, d["xT"].rearrange("(c p) t -> p c t", p=P)).then_inc(ld_x, 16)
            sp.dma_start(con, d["con"]).then_inc(ld_con, 16)
            sp.dma_start(vec[:, 0:VECA], d["vec"][:, 0:VECA]).then_inc(ld_vec, 16)

            def load_front(u):
                m, j = FRONT[u]
                if u >= FS:
                    sp.wait_ge(front_used, u - FS + 1)
                slot = ring[:, u % FS, :]
                src = front_source(m, j)
                sp.dma_start(slot.rearrange("p (c n) -> p c n", c=src.shape[1]), src).then_inc(front_landed[u % FS], 16)

            def load_unit(k, e, slot):
                sp.dma_start(ring[:, slot, :].rearrange("p (c n) -> p c n", c=2), exp_source(k, e)).then_inc(exp_landed[slot], 16)

            def load_first(v):
                load_unit(v % PER, lambda s: 2 * (v // PER) + s, (FS + v) % RING)

            for u in range(NF):
                load_front(u)
                if u == FIRST["uv"]:
                    sp.dma_start(row, d["row"].broadcast_to([P, ROWW])).then_inc(ld_row, 16)
                    sp.dma_start(vec[:, VECA:], d["vec"][:, VECA:]).then_inc(ld_vec2, 16)
                if u == FIRST["ada2"]:
                    sp.dma_start(s0T, d["s0T"]).then_inc(ld_s0, 16)
            for v in range(RING - FS):
                begins, ends = ring_at + (FS + v) * UNIT, ring_at + (FS + v + 1) * UNIT
                if v == 0:
                    sp.wait_ge(gb_ready, NT)
                    sp.wait_ge(st_v, 16)
                if begins < scores_end and ends > gates_end:
                    sp.wait_ge(y_mm, NT)
                    sp.wait_ge(bmask_ready, 1)
                if ends > scores_end:
                    sp.wait_ge(st_ssmp, 16)
                    sp.wait_ge(st_ssms, 16)
                load_first(v)
            for v in range(RING - FS, PER * UNROLL):
                if v < RING:
                    last = max(u for u in range(NF) if u % FS == v - (RING - FS))
                    if last == NF - 1:
                        sp.wait_ge(out_mm, KC)
                    else:
                        sp.wait_ge(front_used, last + 1)
                else:
                    sp.wait_ge(exp_used, v - RING + 1)
                load_first(v)
            with sp.Fori(1, PAIRS // UNROLL) as i:
                for j in range(UNROLL):
                    for k in range(PER):
                        sp.wait_ge(exp_used, i * (PER * UNROLL) + (PER * j + k - RING + 1))
                        load_unit(k, lambda s: i * (2 * UNROLL) + (2 * j + s), exp_slot(j, k))

            def more_loads(i):
                es = listed(sp, i)
                for k in range(PER):
                    behind = RING if k >= RING or isinstance(i, int) else (PER - RING if k < PER - RING else PER)
                    sp.wait_ge(exp_used, i * PER + (PAIRS * PER + k - behind + 1))
                    load_unit(k, lambda s: es[s], exp_slot(0, k))

            sp.wait_ge(more_ready, 1)
            further_pairs(sp, there, more_loads)
            for q in range(0, KC, 2):
                sp.wait_ge(yfin, q + 2)
                sp.dma_start(out["yT"].rearrange("(c p) t -> p c t", p=P)[:, q:q + 2], hT[:, q:q + 2]).then_inc(st_y, 16)
            sp.wait_ge(st_y, 16 * (KC // 2))
            sp.wait_ge(st_conv, 16)

        @block.tensor
        def _(pe):
            def mm(o, l, r, start=True, stop=True):
                return pe.matmul(o, l, r, start=start, stop=stop, skip_group_check=True)

            def landed(u):
                pe.wait_ge(front_landed[u % FS], 16 * (u // FS + 1))

            def unit(u, c=2):
                return ring[:, u % FS, :].rearrange("p (c n) -> p c n", c=c)

            def mean_square(bank):
                for k in range(KC):
                    last = mm(ps[:, bank, 0:T], cn("ones"), sq[:, k, :], k == 0, k == KC - 1)
                last.then_inc(meansq, 1)

            def ada_sums(s, bank):
                if s == 0:
                    pe.wait_ge(c_ready, 1)
                for j in range(4):
                    u = FIRST[f"ada{s}"] + j
                    landed(u)
                    for kk in range(2):
                        for half in range(2):
                            g = 32 * (2 * kk + half)
                            last = mm(ps[g:g + 32, bank, :], csil[:, 2 * j + kk, :], unit(u)[:, kk, half * AW:(half + 1) * AW],
                                      j == 0, j == 3)
                    last.then_inc(front_used if j < 3 else ada_mm, 1)

            def ada_turn(n, s, bank):
                pe.wait_ge(adat_ready, n + 1)
                for m in range(KC):
                    c = (m % 4) * P
                    last = mm(ps[:, bank, m * 9:m * 9 + 9], adat[:, n % 2, c:c + P],
                              cn("gather9")[:, (m // 4) * 9:(m // 4) * 9 + 9])
                    if m == 0:
                        last.then_inc(front_used, 1)
                last.then_inc(ada_tr, 1)

            pe.wait_ge(ld_con, 16)
            pe.wait_ge(ld_vec, 16)
            pe.wait_ge(x_sq, 1)
            mean_square(0)
            ada_sums(SH_M, 1)
            ada_sums(SC_M, 2)
            ada_turn(0, SH_M, 1)
            ada_turn(1, SC_M, 2)
            for j in range(4):
                landed(FIRST["xbc"] + j)
            for i in range(KC):
                m = (i + 4) % KC
                if i >= 2:
                    pe.wait_ge(xbc_line, i - 1)
                for k in range(KC):
                    if i == 0:
                        pe.wait_ge(hp_ready, k + 1)
                        pe.wait_ge(hs_ready, k // 4 + 1)
                    u = FIRST["xbc"] + k // 2
                    last = mm(ps[:, 6 + i % 2, 0:T], unit(u)[:, k % 2, m * P:(m + 1) * P], hT[:, k, :], k == 0, k == KC - 1)
                    if i == KC - 1 and k % 2 == 1 and k < KC - 1:
                        last.then_inc(front_used, 1)
                    if k == KC - 1:
                        last.then_inc(xbc_mm, 1)
            pe.wait_ge(xbc_line, KC - 1)
            for t, (t0, n) in enumerate(TILES):
                for k in range(KC):
                    last = mm(ps[0:n, 6, t * H:(t + 1) * H], hT[:, k, t0:t0 + n], w_dt[:, k, :], k == 0, k == KC - 1)
                    if t == 0 and k == 0:
                        last.then_inc(front_used, 1)
            last.then_inc(dt_mm, 1)
            pe.wait_ge(ld_vec2, 16)
            pe.wait_ge(xbc_line, KC)
            for h in range(AH):
                mm(ps[0:TS, 7, h * SL:(h + 1) * SL], cn("rep", SL), w_sp[0:SL, h, 0:SL])
            mm(ps[0:TS, 7, 64:64 + AH], cn("rep", SL), vc("b_sp")[0:SL, :]).then_inc(rep_mm, 1)
            pe.wait_ge(ada_ready, 2)
            for j in range(4):
                u = FIRST["uv"] + j
                landed(u)
                for kk in range(2):
                    k = 2 * j + kk
                    for half, t in ((1, 0), (1, 1), (1, 2), (0, 2), (0, 0), (0, 1)):
                        t0, n = TILES[t]
                        at = TS if (half, t) == (0, 2) else 0
                        last = mm(ps[at:at + n, 3 * half + t, :], hT[:, k, t0:t0 + n],
                                  unit(u)[:, kk, half * AW:(half + 1) * AW], k == 0, k == KC - 1)
                        if k == KC - 1 and (half, t) != (0, 1):
                            last.then_inc(uv_mm, 1)
                last.then_inc(front_used, 1)
            pe.wait_ge(dta_ready, 1)
            pe.wait_ge(rep_read, 1)
            pe.wait_ge(gelu_done, 1)
            for j in range(2):
                u = FIRST["z"] + j
                landed(u)
                for kk in range(4):
                    k = 4 * j + kk
                    for t in range(2):
                        last = mm(ps[:, 6 + t, :], hT[:, k, t * P:(t + 1) * P], unit(u, 4)[:, kk, :], k == 0, k == KC - 1)
                        if k == KC - 1:
                            last.then_inc(z_mm, 1)
                    for q in range(2):
                        c = slice(q * 256, (q + 1) * 256)
                        last = mm(ps[q * TS:(q + 1) * TS, 3, c], hT[:, k, TP:T], unit(u, 4)[:, kk, c], k == 0, k == KC - 1)
                last.then_inc(front_used, 1)
            pe.wait_ge(gelu_done, 2)
            ada_sums(GT_M, 4)

            def spatial(t):
                n = TILES[t][1]
                if t == 0:
                    pe.wait_ge(v_ready, 1)
                if t == 1:
                    pe.wait_ge(z_silu, NT)
                if t == 2:
                    pe.wait_ge(s_read, 1)
                for h in range(AH):
                    w = w_sp[:, h, :] if t < 2 else wblk[0:TS, h, :]
                    last = mm(ps[0:n, SPATIAL[t], h * P:(h + 1) * P], w, vg[0:n, t, h * P:(h + 1) * P])
                last.then_inc(s_mm, 1)

            pe.wait_ge(xbc_ready, KC)
            pe.wait_ge(gelu_done, 6)
            for t, (t0, n) in enumerate(TILES):
                if t == 1:
                    pe.wait_ge(z_silu, 1)
                    spatial(0)
                    spatial(1)
                if t == 2:
                    pe.wait_ge(xb_tok, 1)
                for m in range(4):
                    pe.transpose(ps[0:n, XB[t][0], m * P:(m + 1) * P], xbcT[:, m, t0:t0 + n], cn("ident"))
                for g in range(G):
                    last = pe.transpose(ps[0:n, XB[t][1], g * P:(g + 1) * P], xbcT[:, 4 + g, t0:t0 + n], cn("ident"))
                last.then_inc(xb_tr, 1)
            spatial(2)
            pe.wait_ge(xb_tok, 2)
            for t, (t0, n) in enumerate(TILES):
                mm(ps[0:n, 0, 2 * t * H:(2 * t + 1) * H], after(t), dta[0:n, t, :])
                mm(ps[0:n, 0, (2 * t + 1) * H:(2 * t + 2) * H], upto(t), dta[0:n, t, :])
            mm(ps[:, 0, 6 * H:7 * H], cn("ones"), dta[:, 1, :])
            mm(ps[:, 0, 64:64 + NSEQ * H].rearrange("p (b h) -> p b h", b=NSEQ), cn("ones", TS), dseq[0:TS]).then_inc(decay_mm, 1)
            ada_turn(2, GT_M, 4)

            def decay_and_scores(i):
                t = ORDER[i]
                t0, n = TILES[t]
                pe.wait_ge(sl_ready, i + 1)
                if i:
                    pe.wait_ge(lx_ready, i)
                    pe.wait_ge(gm_ready, i)
                for h in range(H):
                    last = mm(ps[0:n, 6 + h // 4, (h % 4) * P:(h % 4) * P + n], sel_l[i][0:n, h, 0:n], upto(t))
                last.then_inc(l_mm, 1)
                if i == 0:
                    pe.wait_ge(s_read, NT)
                for g in range(G):
                    last = mm(ps[0:n, 5, g * P:g * P + n], xbcT[:, 4 + g, t0:t0 + n], xbcT[:, 6 + g, t0:t0 + n])
                last.then_inc(g_mm, 1)

            def y_diag(i):
                t = ORDER[i]
                n = TILES[t][1]
                pe.wait_ge(xdt_ready, i + 1)
                pe.wait_ge(m_ready, i + 1)
                for h in range(H):
                    last = mm(ps[0:n, 1, h * HD:(h + 1) * HD], mdec[0:n, h, 0:n], xdt[0:n, t, h * HD:(h + 1) * HD])
                last.then_inc(y_mm, 1)

            def end_state(t):
                for g in range(G):
                    last = mm(ps[:, 0, g * 256:(g + 1) * 256], btok[:, t, g * P:(g + 1) * P], xw[:, t, g * 256:(g + 1) * 256])
                last.then_inc(st_mm, 1)

            decay_and_scores(0)
            pe.wait_ge(ada_ready, 3)
            ada_sums(SH_F, 4)
            pe.wait_ge(ld_s0, 16)
            pe.wait_ge(cmask_ready, 1)
            pe.wait_ge(xb_tok, NT)
            half_seq = NSEQ // 2
            for g in range(G):
                for i in range(NSEQ):
                    b = i % 2 * half_seq + i // 2
                    at = i % 2 * half_seq * SL
                    mm(ps[at:at + half_seq * SL, 2, g * 256:(g + 1) * 256],
                       cmask[:, g, b * TS + at:b * TS + at + half_seq * SL],
                       s0T[:, b, g * 256:(g + 1) * 256], i < 2, i >= NSEQ - 2)
            ada_turn(3, SH_F, 4)
            decay_and_scores(1)
            y_diag(0)
            pe.wait_ge(decays, 1)
            pe.wait_ge(xw_ready, NT)
            end_state(0)
            decay_and_scores(2)
            pe.wait_ge(ada_ready, 4)
            ada_sums(SC_F, 4)
            pe.wait_ge(y_read, 1)
            y_diag(1)
            pe.wait_ge(st0_ready, 1)
            for g in range(G):
                mm(ps[:, 2, g * 256:(g + 1) * 256], xbcT[:, 6 + g, P:2 * P], st0[:, g * 256:(g + 1) * 256])
            end_state(1)
            ada_turn(4, SC_F, 4)
            pe.wait_ge(y_read, 2)
            y_diag(2)
            pe.wait_ge(gm_ready, NT)
            pe.wait_ge(lx_ready, NT)
            ada_sums(GT_F, 7)

            def add_state(b):
                if b >= 2:
                    pe.wait_ge(sn_copied, b - 1)
                for g in range(G):
                    last = mm(ps[:, 5 + b % 2, g * 256:(g + 1) * 256], bmask[0:TS, g, b, :], xw[0:TS, 2, g * 256:(g + 1) * 256])
                last.then_inc(sn_mm, 1)

            def turn_cat(t):
                n = TILES[t][1]
                pe.wait_ge(cat_ready, t + 1)
                if t == 2:
                    pe.wait_ge(catT_ready, 1)
                for m in range(KC):
                    last = pe.transpose(ps[:, CATB[t] + m // 4, (m % 4) * P:(m % 4) * P + n], cat[0:n, t, m * P:(m + 1) * P],
                                        cn("ident", n, n))
                last.then_inc(cat_tr, 1)

            pe.wait_ge(bmask_ready, 1)
            add_state(0)
            add_state(1)
            ada_turn(5, GT_F, 7)
            pe.wait_ge(ada_ready, 5)
            turn_cat(0)
            add_state(2)
            pe.wait_ge(y_read, NT)
            turn_cat(1)
            add_state(3)
            turn_cat(2)
            for b in range(4, NSEQ):
                add_state(b)
            pe.wait_ge(ada_ready, 6)
            pe.wait_ge(catT_ready, NT)
            pe.wait_ge(sn_copied, NSEQ)

            for j in range(4):
                landed(FIRST["out"] + j)
            for m in range(KC):
                if m >= 2:
                    pe.wait_ge(x1_ready, m - 1)
                for k in range(KC):
                    last = mm(ps[:, 6 + m % 2, 0:T], unit(FIRST["out"] + k // 2)[:, k % 2, m * P:(m + 1) * P], catT[:, k, :],
                              k == 0, k == KC - 1)
                    if m == KC - 1 and k % 2 == 1 and k < KC - 1:
                        last.then_inc(front_used, 1)
                last.then_inc(out_mm, 1)
            pe.wait_ge(sq_added, KC - 1)
            mm(ps[:, 2, 0:T], cn("ones"), sq[:, 0, :]).then_inc(meansq, 1)
            for k in range(KC):
                pe.wait_ge(hp_ready, KC + k + 1)
                pe.wait_ge(hs_ready, 2 + k // 4 + 1)
                g = NE * (k % 4)
                last = mm(ps[g:g + NE, 7, 0:T], w_router[:, k, :], hT[:, k, :], k < 4, k >= 4)
            last.then_inc(logit_mm, 1)
            for t, (t0, n) in enumerate(TILES):
                for k in range(KC):
                    last = pe.transpose(ps[0:n, HTOK[t] + k // 4, (k % 4) * P:(k % 4 + 1) * P], hT[:, k, t0:t0 + n], cn("ident"))
                last.then_inc(h_tr, 1)
                if t == 0:
                    pe.wait_ge(logT_ready, 1)
                    for s, (s0, r) in enumerate(TILES):
                        last = mm(ps[0:r, 7, s * NE:(s + 1) * NE], logT[:, s0:s0 + r], cn("gather32"))
                    last.then_inc(router_mm, 1)
            pe.wait_ge(picks_ready, 1)
            for t, (t0, n) in enumerate(TILES):
                for s in range(t + 1):
                    last = mm(ps[0:n, 2, t * NE:(t + 1) * NE], cn("before" if s == t else "ones", n if s == t else P, n),
                              picked[0:TILES[s][1], s, :], s == 0, s == t)
            last.then_inc(rank_mm, 1)
            X = moe["X"].rearrange("p (k c) -> p k c", k=KC)
            A = moe["g"].rearrange("p (k c) -> p k c", k=KC)

            def gather(q):
                wait(pe, sel_ready, q + 1)
                wait(pe, selT_ready, q - 1)
                for k in range(KC):
                    for t, (t0, n) in enumerate(TILES):
                        last = mm(ps[:, 6 + k // 4, (k % 4) * P:(k % 4 + 1) * P], htok[0:n, t, k * P:(k + 1) * P],
                                  moe["sel"][0:n, t, :], t == 0, t == NT - 1)
                last.then_inc(x_mm, 1)

            def turn_act():
                for k in range(KC):
                    last = pe.transpose(ps[:, k // 4, (k % 4) * P:(k % 4 + 1) * P], A[:, k, :], cn("ident"))
                last.then_inc(a_tr, 1)

            def product(m, bank, rows, loads, slots):
                for half in range(2):
                    mm(ps[:, bank + half, :], moe["pick"][:, m, :], b_exp[:, half * AW:(half + 1) * AW], True, False)
                for p in range(4):
                    for s in range(2):
                        pe.wait_ge(exp_landed[slots[2 * p + s]], loads[2 * p + s])
                    w = [ring[:, slots[2 * p + s], :].rearrange("p (c n) -> p c n", c=2) for s in range(2)]
                    for kk in range(2):
                        for half in range(2):
                            for s in range(2):
                                c = slice(s * CAP, (s + 1) * CAP)
                                last = mm(ps[c, bank + half, :], rows[:, 2 * p + kk, c], w[s][:, kk, half * AW:(half + 1) * AW],
                                          False, p == 3 and kk == 1)
                                if kk == 1 and half == 1:
                                    last.then_inc(exp_used, 1)

            def combine(q):
                pe.wait_ge(y_ready, q + 1)
                pe.wait_ge(selT_ready, q + 1)
                for m in range(KC):
                    wait(pe, comb_added, q * KC + max(0, m - 2))
                    mm(ps[:, (2, 3, 6)[m % 3], 0:T], moe["y"][:, m * P:(m + 1) * P], moe["selT"]).then_inc(comb_mm, 1)

            def turn_sel(q):
                pe.wait_ge(selw_ready, q + 1)
                for t, (t0, r) in enumerate(TILES):
                    last = pe.transpose(ps[:, 7, t0:t0 + r], moe["selw"][0:r, t, :], cn("ident", r, r))
                last.then_inc(selT_tr, 1)

            def pair(q, slots, loads, serial=False):
                first = isinstance(q, int) and q == 0
                if serial and not isinstance(q, int):
                    wait(pe, comb_added, q * KC)
                    gather(q)
                pe.wait_ge(x_ready, q + 1)
                pe.wait_ge(pick_ready, q + 1)
                product(0, 0, X, loads[0:8], slots[0:8])
                if first:
                    further_blocks()
                if not first:
                    wait(pe, comb_added, (q - (0 if serial else 1)) * KC)
                product(1, 2, X, loads[8:16], slots[8:16])
                if not serial:
                    gather(q + 1)
                pe.wait_ge(act_ready, q + 1)
                turn_act()
                if not serial:
                    pe.wait_ge(x_ready, q + 2)
                if not serial and not first:
                    combine(q - 1)
                turn_sel(q)
                pe.wait_ge(actT_ready, q + 1)
                wait(pe, y_ready, q)
                if first:
                    pe.wait_ge(more_read, 1)
                product(2, 4, A, loads[16:24], slots[16:24])

            nf = PASSES - 1

            def further_blocks():
                pe.wait_ge(oh_ready, 1)
                for q, (l, r) in enumerate([(cn("eidx", NE), oh), (cn("ones", NE), ohb), (cn("ones", NE), oh)]):
                    for p in range(nf):
                        last = mm(ps[:, 5, 32 + LW * q:32 + LW * (q + 1)], l, r[0:NE, p, :], p == 0, p == nf - 1)
                last.then_inc(more_mm, 1)

            pe.wait_ge(htok_ready, NT)
            gather(0)
            for t, (t0, n) in enumerate(TILES):
                last = mm(ps[0:NE, 5, 0:1], picked[0:n, t, :], cn("ones", n, 1), t == 0, t == NT - 1)
            last.then_inc(cnt_mm, 1)
            pe.wait_ge(flag_ready, 1)
            mm(ps[0:NE, 5, 8:8 + nf], cn("before", NE, NE), flag[0:NE, :], True, False)
            for p in range(1, nf):
                last = mm(ps[0:NE, 5, 8 + p:8 + nf], cn("ones", NE, NE), flag[0:NE, 0:nf - p], False, p == nf - 1)
            last.then_inc(place_mm, 1)

            def pe_turn(i):
                for j in range(UNROLL):
                    loads = [i * 48 + 16 * ((PER * j + k) // RING + 1) for k in range(PER)]
                    pair(i * UNROLL + j, [exp_slot(j, k) for k in range(PER)], loads)

            turns(pe.Fori, pe_turn)
            combine(PAIRS - 1)
            pe.wait_ge(more_ready, 1)

            def more_pair(i):
                loads = [i * (32 if k % RING < PER - RING else 16) + 16 * (PAIRS * PER // RING + k // RING + 1)
                         for k in range(PER)]
                pair(i + PAIRS, [exp_slot(0, k) for k in range(PER)], loads, True)
                combine(i + PAIRS)

            further_pairs(pe, there, more_pair)
            for m in range(KC):
                pe.wait_ge(f_sq, m + 1)
                last = mm(ps[:, 0, 0:T], cn("ones"), sq[:, m, :], m == 0, m == KC - 1)
            last.then_inc(meansq, 1)

        @block.scalar
        def _(act):
            A = nc.scalar.activation
            step = Steps(act, act_steps)

            def root(k, ap):
                act.wait_ge(var_ready, k)
                A(ap, ap, ACT.Sqrt).then_inc(root_ready, 1)

            def modulate(k, shift):
                act.wait_ge(gain_ready, k)
                for m in range(KC):
                    act.wait_ge(xn_ready, 2 * (k - 1) + m // 4 + 1)
                    A(hT[:, m, 0:TP], hT[:, m, 0:TP], ACT.Identity, bias=ada[:, shift, m, 0:1],
                      scale=gain[:, m, 0:1]).then_inc(hp_ready, 1)

            act.wait_ge(ld_vec, 16)
            act.wait_ge(c_zero, 1)
            A(csil[:, :, 0:9], vc("c", KC), ACT.Silu).then_inc(c_ready, 1)
            root(1, rstd)

            def copy_ada(n, bank):
                act.wait_ge(ada_mm, n + 1)
                if n >= 2:
                    act.wait_ge(ada_tr, n - 1)
                A(adat[:, n % 2, :], ps[:, bank, :], ACT.Copy).then_inc(adat_ready, 1)

            copy_ada(0, 1)
            copy_ada(1, 2)
            modulate(1, SH_M)

            def conv_out(i):
                m = (i + 4) % KC
                act.wait_ge(conv_done, i + 1)
                c = cacc[:, i % 2, :]
                A(xbcT[:, m, 0:TP], c[:, 0:TP], ACT.Silu)
                for b0, nb in ((0, NSEQ - 1), (NSEQ - 1, 1)):
                    at = SEQ0 + b0 * (PAD + SL)
                    if nb > 1:
                        src = c[:, at:at + nb * (PAD + SL)].rearrange("p (b w) -> p b w", w=PAD + SL)[:, :, 0:SL]
                    else:
                        src = c[:, at:at + SL].rearrange("p (b w) -> p b w", b=1)
                    last = A(xbcT[:, m, TP + b0 * SL:TP + (b0 + nb) * SL].rearrange("p (b w) -> p b w", w=SL), src, ACT.Silu)
                last.then_inc(xbc_ready, 1)

            act.wait_ge(line_ready, 1)
            for i in range(KC):
                m = (i + 4) % KC
                act.wait_ge(xbc_mm, i + 1)
                A(line[:, m, PAD:SEQ0], ps[:, 6 + i % 2, 0:TP], ACT.Copy)
                A(line_seq(m, PAD, SL), ps[:, 6 + i % 2, TP:T].rearrange("p (b w) -> p b w", w=SL), ACT.Copy).then_inc(xbc_line, 1)
                act.wait_ge(xbc_line, i + 1)
                if i >= 2:
                    act.wait_ge(xbc_ready, i - 1)
                A(cacc[:, i % 2, :], line[:, m, 0:CONVN], ACT.Identity, bias=conv_b[:, m:m + 1],
                  scale=conv_w[:, 0, m:m + 1]).then_inc(conv_begun, 1)
                if i:
                    conv_out(i - 1)
            conv_out(KC - 1)
            act.wait_ge(ld_row, 16)
            A(ea, rw("a_log"), ACT.Exp)
            act.wait_ge(dt_abs, 1)
            A(dte, dte, ACT.Exp, scale=-1.0).then_inc(dt_exp, 1)
            act.wait_ge(dt_one, 1)
            A(dtx, dtu, ACT.Ln).then_inc(dt_ln, 1)
            for i, (dst, half, t) in enumerate([(vg, 1, 0), (vg, 1, 1), (vg, 1, 2), (ug, 0, 2), (ug, 0, 0), (ug, 0, 1)]):
                n = TILES[t][1]
                at = TS if (half, t) == (0, 2) else 0
                if i < 5:
                    act.wait_ge(uv_mm, i + 1)
                else:
                    act.wait_ge(front_used, FIRST["uv"] + 4)
                A(dst[0:n, t, :], ps[at:at + n, 3 * half + t, :], ACT.Gelu).then_inc(gelu_done, 1)
            root(2, ssv)
            for t, (t0, n) in enumerate(TILES):
                if t < NT - 1:
                    act.wait_ge(z_mm, t + 1)
                    A(zs[:, t, :], ps[:, 6 + t, :], ACT.Silu).then_inc(z_silu, 1)
                else:
                    act.wait_ge(front_used, FIRST["z"] + 2)
                    A(zs[0:TS, t, 0:256], ps[0:TS, 3, 0:256], ACT.Silu)
                    A(zs[0:TS, t, 256:512], ps[TS:2 * TS, 3, 256:512], ACT.Silu).then_inc(z_silu, 1)
            copy_ada(2, 4)
            for t, (t0, n) in enumerate(TILES):
                act.wait_ge(xb_tr, t + 1)
                A(xs[0:n, t, :], ps[0:n, XB[t][0], :], ACT.Copy)
                A(btok[0:n, t, :], ps[0:n, XB[t][1], 0:G * P], ACT.Copy).then_inc(xb_tok, 1)
            act.wait_ge(decay_mm, 1)
            A(dec[:, 0:4 * H], ps[:, 0, 0:4 * H], ACT.Exp)
            A(dec[0:TS, 4 * H:6 * H], ps[0:TS, 0, 4 * H:6 * H], ACT.Exp)
            A(dec[:, 6 * H:7 * H], ps[:, 0, 6 * H:7 * H], ACT.Exp)
            A(dec[:, 64:128], ps[:, 0, 64:128], ACT.Exp).then_inc(decays, 1)

            def decay_exp(i):
                n = TILES[ORDER[i]][1]
                act.wait_ge(l_mm, i + 1)
                if i:
                    act.wait_ge(m_ready, i)
                for q in range(2):
                    last = A(Lx[0:n, 4 * q:4 * q + 4, 0:n],
                             ps[0:n, 6 + q, :].rearrange("p (h l) -> p h l", h=4)[:, :, 0:n], ACT.Exp)
                last.then_inc(lx_ready, 1)

            act.wait_ge(st_conv, 16)
            decay_exp(0)
            copy_ada(3, 4)
            decay_exp(1)
            act.wait_ge(st_mm, 1)
            A(st0, ps[:, 0, :], ACT.Copy).then_inc(st0_ready, 1)
            decay_exp(2)
            for t, (t0, n) in enumerate(TILES):
                act.wait_ge(ga_ready, t + 1)
                step(A(junk[0:n, :], cat[0:n, t, 0:AW], ACT.Square, accum_out=ss9[0:n, 0, t:t + 1]))
            copy_ada(4, 4)
            for i, t in enumerate(ORDER):
                n = TILES[t][1]
                act.wait_ge(gb_ready, i + 1)
                for g in range(G):
                    step(A(junk[0:n, 0:256], cat[0:n, t, AW + g * 256:AW + (g + 1) * 256], ACT.Square,
                           accum_out=ss9[0:n, 1 + g, t:t + 1]))
            A(tmp64[0:1, 0:1], ss9[0:1, 0, 0:1], ACT.Copy).then_inc(gb_sq, 1)
            root(3, ss9)
            copy_ada(5, 7)
            for b in range(NSEQ):
                act.wait_ge(sn_mm, b + 1)
                if b >= 2:
                    act.wait_ge(sn_added, b - 1)
                A(snew[:, b % 2, :], ps[:, 5 + b % 2, :], ACT.Copy).then_inc(sn_copied, 1)
            for m in range(KC):
                act.wait_ge(x1_ready, m + 1)
                A(sq[:, m, :], xT[:, m, :], ACT.Square).then_inc(x1_sq, 1)
            root(4, rstd)
            modulate(2, SH_F)
            act.wait_ge(logit_mm, 1)
            A(logT, ps[:, 7, 0:T], ACT.Copy).then_inc(logT_ready, 1)
            for t, (t0, n) in enumerate(TILES):
                act.wait_ge(h_tr, t + 1)
                A(htok[0:n, t, :].rearrange("p (a b) -> p a b", a=2), ps[0:n, HTOK[t]:HTOK[t] + 2, :], ACT.Copy).then_inc(htok_ready, 1)
            act.wait_ge(soft_in, 1)
            A(topw[:, :, 0:TOPK], topw[:, :, 0:TOPK], ACT.Exp).then_inc(soft_out, 1)

            def from_banks(bank, name, done):
                A(moe[name].rearrange("p (a b) -> p a b", a=2), ps[:, bank:bank + 2, :], ACT.Copy).then_inc(done, 1)

            def copy_x(q):
                act.wait_ge(x_mm, q + 1)
                from_banks(6, "X", x_ready)

            def sigmoid(q):
                act.wait_ge(g_ready, q + 1)
                A(moe["s"], moe["g"], ACT.Sigmoid, scale=ALPHA).then_inc(sig_ready, 1)

            def copy_act(q):
                act.wait_ge(a_tr, q + 1)
                from_banks(0, "g", actT_ready)

            def copy_sel(q):
                act.wait_ge(selT_tr, q + 1)
                A(moe["selT"], ps[:, 7, 0:T], ACT.Copy).then_inc(selT_ready, 1)

            def copy_y(q):
                act.wait_ge(exp_used, q * PER + PER)
                from_banks(4, "y", y_ready)

            copy_x(0)

            def act_turn(i):
                for j in range(UNROLL):
                    q = i * UNROLL + j
                    sigmoid(q)
                    copy_x(q + 1)
                    copy_act(q)
                    copy_sel(q)
                    copy_y(q)

            turns(act.Fori, act_turn)
            act.wait_ge(more_ready, 1)

            def more_pair(i):
                if not isinstance(i, int):
                    copy_x(i + PAIRS)
                for copy in (sigmoid, copy_act, copy_sel, copy_y):
                    copy(i + PAIRS)

            further_pairs(act, there, more_pair)
            for m in range(KC):
                act.wait_ge(f_sq_in, max(1, m))
                A(sq[:, m, :], xT[:, m, :], ACT.Square).then_inc(f_sq, 1)
            root(5, rstd)

        @block.vector
        def _(dve):
            V = nc.vector
            step = Steps(dve, dve_steps)

            def tt(o, a, b, op):
                return V.tensor_tensor(o, a, b, op)

            def inverse_root(k, o, src, n):
                V.tensor_scalar(o, src, 1.0 / n, EPS, ALU.mult, ALU.add).then_inc(var_ready, 1)
                dve.wait_ge(root_ready, k)
                step(V.reciprocal(o, o))

            def ada_rows(s, bank):
                dve.wait_ge(ada_tr, ada_rows.n + 1)
                ada_rows.n += 1
                tt(ada[:, s], ps[:, bank, 0:KC * 9].rearrange("p (m b) -> p m b", m=KC), wide(bada[:, s, :], 2, 9),
                   ALU.add).then_inc(ada_ready, 1)

            ada_rows.n = 0

            def gains(k, s, g):
                dve.wait_ge(ada_ready, {SC_M: 2, SC_F: 5}[s])
                V.scalar_tensor_tensor(gain, ada[:, s], 1.0, wide(vc(g), 2, 9), ALU.add, ALU.mult).then_inc(gain_ready, 1)
                dve.wait_ge(gain_ready, k)

            def by_seq(ap):
                return ap[:, :, TP:T].rearrange("p c (b j) -> p c b j", b=NSEQ)

            def modulate_sample(k, s):
                for q in (0, 4):
                    h = by_seq(hT[:, q:q + 4])
                    dve.wait_ge(xn_ready, 2 * (k - 1) + q // 4 + 1)
                    step(tt(h, h, wide(gain[:, q:q + 4, 1:9], 3, SL), ALU.mult))
                    tt(h, h, wide(ada[:, s, q:q + 4, 1:9], 3, SL), ALU.add).then_inc(hs_ready, 1)

            def normed(k, bank):
                dve.wait_ge(meansq, k)
                inverse_root({1: 1, 2: 4}[k], rstd, ps[:, bank, 0:T], D)
                for q in (0, 4):
                    tt(hT[:, q:q + 4], xT[:, q:q + 4], wide(rstd, 1, 4), ALU.mult).then_inc(xn_ready, 1)

            V.memset(csil, 0.0).then_inc(c_zero, 1)
            dve.wait_ge(ld_x, 16)
            tt(sq, xT, xT, ALU.mult).then_inc(x_sq, 1)
            step(V.memset(dtx, 0.0))
            step(V.memset(ssv, 0.0))
            step(V.memset(ss9, 0.0))
            normed(1, 0)
            ada_rows(SH_M, 1)
            ada_rows(SC_M, 2)
            gains(1, SC_M, "g_mix")
            modulate_sample(1, SH_M)
            for i in range(KC):
                m = (i + 4) % KC
                dve.wait_ge(conv_begun, i + 1)
                c = cacc[:, i % 2, :]
                for k in range(1, TAPS):
                    ins = V.scalar_tensor_tensor(c, line[:, m, k:k + CONVN], conv_w[:, k, m:m + 1], c, ALU.mult, ALU.add)
                    if k < TAPS - 1:
                        step(ins)
                ins.then_inc(conv_done, 1)
            dve.wait_ge(dt_mm, 1)
            dve.wait_ge(ld_row, 16)
            step(tt(dtx[:, 0:2, :], ps[:, 6, 0:2 * H].rearrange("p (t h) -> p t h", t=2), wide(rw("dt_bias"), 1, 2), ALU.add))
            step(tt(dtx[0:TS, 2, :], ps[0:TS, 6, 2 * H:3 * H], rw("dt_bias", TS), ALU.add))
            step(V.tensor_scalar(dtr, dtx, 0.0, None, ALU.max))
            V.scalar_tensor_tensor(dte, dtx, -1.0, dtx, ALU.mult, ALU.max).then_inc(dt_abs, 1)
            dve.wait_ge(ld_con, 16)
            dve.wait_ge(ld_vec, 16)
            dve.wait_ge(dt_exp, 1)
            V.tensor_scalar(dtu, dte, 1.0, None, ALU.add).then_inc(dt_one, 1)
            dve.wait_ge(dt_one, 1)
            step(V.scalar_tensor_tensor(dt, dtu, -1.0, dte, ALU.add, ALU.subtract))
            step(tt(dt, dtr, dt, ALU.subtract))
            dve.wait_ge(dt_ln, 1)
            step(tt(dt, dt, dtx, ALU.add))
            step(V.scalar_tensor_tensor(dta, dt, -1.0, wide(ea, 1, NT), ALU.mult, ALU.mult))
            tt(dseq[0:TS], wide(dta[0:TS, 2, :], 1, NSEQ), wide(cn("seq", TS), 2, H), ALU.mult).then_inc(dta_ready, 1)
            dve.wait_ge(dta_ready, 1)

            def decay_sel(i):
                t = ORDER[i]
                n = TILES[t][1]
                if i:
                    dve.wait_ge(z_silu, NT)
                tt(sel_l[i][0:n, :, 0:n], wide(after(t), 1, H), wide(dta[0:n, t, :], 2, n), ALU.mult).then_inc(sl_ready, 1)

            decay_sel(0)
            dve.wait_ge(rep_mm, 1)
            step(tt(w_sp, w_sp, wide(cn("upto"), 1, AH), ALU.mult))
            for h in range(AH):
                tt(wblk[0:TS, h, :].rearrange("p (b j) -> p b j", b=NSEQ), wide(ps[0:TS, 7, h * SL:(h + 1) * SL], 1, NSEQ),
                   cn("upto_s", TS).rearrange("p (b j) -> p b j", b=NSEQ), ALU.mult)
            for t in range(2):
                V.tensor_copy(bsp[:, t, :], vc("b_sp"))
            V.tensor_copy(bsp[0:TS, 2, :], ps[0:TS, 7, 64:64 + AH]).then_inc(rep_read, 1)
            dve.wait_ge(gelu_done, 3)
            both = slice(0, 2)
            step(tt(vsq[:, both], vg[:, both], vg[:, both], ALU.mult))
            step(tt(vsq[0:TS, 2], vg[0:TS, 2], vg[0:TS, 2], ALU.mult))
            step(V.tensor_reduce(ssv[:, both].rearrange("p t h -> p (t h)"), vsq[:, both].rearrange("p t (h e) -> p (t h) e", h=AH), AX.X, ALU.add))
            step(V.tensor_reduce(ssv[0:TS, 2], vsq[0:TS, 2].rearrange("p (h e) -> p h e", h=AH), AX.X, ALU.add))
            inverse_root(2, ssv, ssv, P)
            for rows, ts, n in ((P, both, 2), (TS, slice(2, 3), 1)):
                v4 = vg[0:rows, ts].rearrange("p t (h e) -> p (t h) e", h=AH)
                step(tt(v4, v4, wide(ssv[0:rows, ts].rearrange("p t h -> p (t h)"), 2, P), ALU.mult))
                ins = tt(vg[0:rows, ts], vg[0:rows, ts], wide(rw("g_v", rows), 1, n), ALU.mult)
                if n == 2:
                    step(ins)
            ins.then_inc(v_ready, 1)

            def scores(i):
                t = ORDER[i]
                n = TILES[t][1]
                dve.wait_ge(g_mm, i + 1)
                if i:
                    dve.wait_ge(m_ready, i)
                tt(gm[0:n, :, 0:n], ps[0:n, 5, 0:G * P].rearrange("p (g l) -> p g l", g=G)[:, :, 0:n], wide(upto(t), 1, G),
                   ALU.mult).then_inc(gm_ready, 1)
                dve.wait_ge(gm_ready, i + 1)
                dve.wait_ge(lx_ready, i + 1)
                if i:
                    dve.wait_ge(y_mm, i)
                for g in range(G):
                    ins = tt(mdec[0:n, 4 * g:4 * g + 4, 0:n], Lx[0:n, 4 * g:4 * g + 4, 0:n], wide(gm[0:n, g, 0:n], 1, 4), ALU.mult)
                ins.then_inc(m_ready, 1)

            def gate_a(t):
                n = TILES[t][1]
                dve.wait_ge(s_mm, t + 1)
                dst = cat[0:n, t, 0:AW]
                tt(dst.rearrange("p (h e) -> p h e", h=AH), ps[0:n, SPATIAL[t], :].rearrange("p (h e) -> p h e", h=AH),
                   wide(bsp[0:n, t, :], 2, P), ALU.add).then_inc(s_read, 1)
                dve.wait_ge(s_read, t + 1)
                tt(dst, dst, ug[0:n, t, :], ALU.mult).then_inc(ga_ready, 1)

            def heads(ap):
                return ap.rearrange("p (h e) -> p h e", h=H)

            def weight_x(t):
                n = TILES[t][1]
                tt(heads(xdt[0:n, t, :]), heads(xs[0:n, t, :]), wide(dt[0:n, t, :], 2, HD), ALU.mult).then_inc(xdt_ready, 1)

            def decay_x(t):
                n = TILES[t][1]
                tt(heads(xw[0:n, t, :]), heads(xdt[0:n, t, :]), wide(dec[0:n, 2 * t * H:(2 * t + 1) * H], 2, HD),
                   ALU.mult).then_inc(xw_ready, 1)

            decay_sel(1)
            decay_sel(2)
            dve.wait_ge(gelu_done, 6)
            gate_a(0)
            gate_a(1)
            dve.wait_ge(xb_tok, NT)
            dve.wait_ge(st_conv, 16)
            for t in ORDER:
                weight_x(t)
            ada_rows(GT_M, 4)
            gate_a(2)
            scores(0)
            dve.wait_ge(decays, 1)
            dve.wait_ge(xdt_ready, NT)
            for t in ORDER:
                decay_x(t)

            def y_out(i):
                t = ORDER[i]
                n = TILES[t][1]
                dve.wait_ge(skip_ready, NT)
                dve.wait_ge(y_mm, i + 1)
                dst = cat[0:n, t, AW:D]
                if t:
                    step(tt(heads(xs[0:n, t, :]), heads(ps[0:n, 2, :]),
                            wide(dec[0:n, (2 * t + 1) * H:(2 * t + 2) * H], 2, HD), ALU.mult))
                    step(tt(dst, dst, xs[0:n, t, :], ALU.add))
                tt(dst, dst, ps[0:n, 1, :], ALU.add).then_inc(y_read, 1)
                dve.wait_ge(y_read, i + 1)
                tt(dst, dst, zs[0:n, t, :], ALU.mult).then_inc(gb_ready, 1)

            scores(1)
            ada_rows(SH_F, 4)
            y_out(0)
            scores(2)
            y_out(1)
            dve.wait_ge(st0_ready, 1)
            step(tt(heads(st1), heads(st0), wide(dec[:, 6 * H:7 * H], 2, HD), ALU.mult))
            y_out(2)
            dve.wait_ge(st_mm, 2)
            tt(st1, st1, ps[:, 0, :], ALU.add).then_inc(st1_ready, 1)
            dve.wait_ge(gb_sq, 1)
            step(V.tensor_scalar(ss9[:, 0, :], ss9[:, 0, :], 0.5, None, ALU.mult))
            inverse_root(3, ss9, ss9, 256)
            for t, (t0, n) in enumerate(TILES):
                V.tensor_scalar(cat[0:n, t, 0:AW], cat[0:n, t, 0:AW], ss9[0:n, 0, t:t + 1], None, ALU.mult)
                for g in range(G):
                    part = cat[0:n, t, AW + g * 256:AW + (g + 1) * 256]
                    ins = V.tensor_scalar(part, part, ss9[0:n, 1 + g, t:t + 1], None, ALU.mult)
                ins.then_inc(cat_ready, 1)
            ada_rows(SC_F, 4)
            for t, (t0, n) in enumerate(TILES):
                dve.wait_ge(cat_tr, t + 1)
                for q in range(2):
                    ins = tt(catT[:, 4 * q:4 * q + 4, t0:t0 + n],
                             ps[:, CATB[t] + q, :].rearrange("p (m l) -> p m l", m=4)[:, :, 0:n],
                             wide(vc("g_cat")[:, 4 * q:4 * q + 4], 2, n), ALU.mult)
                ins.then_inc(catT_ready, 1)
            ada_rows(GT_F, 7)
            gains(2, SC_F, "g_ffn")

            def residual(m, src, gate, done):
                step(V.scalar_tensor_tensor(xT[:, m, 0:TP], src[:, 0:TP], ada[:, gate, m, 0:1], xT[:, m, 0:TP], ALU.mult, ALU.add))
                step(tt(tmp64.rearrange("p (b j) -> p b j", b=NSEQ), src[:, TP:T].rearrange("p (b j) -> p b j", b=NSEQ),
                        wide(ada[:, gate, m, 1:9], 2, SL), ALU.mult))
                tt(xT[:, m, TP:T], xT[:, m, TP:T], tmp64, ALU.add).then_inc(done, 1)

            def add_squares(m):
                dve.wait_ge(x1_sq, m + 1)
                if m > 1:
                    dve.wait_ge(sq_added, m - 1)
                tt(sq[:, 0, :], sq[:, 0, :], sq[:, m, :], ALU.add).then_inc(sq_added, 1)

            for m in range(KC):
                dve.wait_ge(out_mm, m + 1)
                residual(m, ps[:, 6 + m % 2, 0:T], GT_M, x1_ready)
                if m >= 2:
                    add_squares(m - 1)
            add_squares(KC - 1)
            dve.wait_ge(x1_ready, KC)
            normed(2, 2)
            modulate_sample(2, SH_F)
            step(V.memset(logit, 0.0))
            step(V.memset(rank, -1.0))
            step(V.memset(wgt, 0.0))
            dve.wait_ge(router_mm, 1)
            tt(logit[:, 0:2, :], ps[:, 7, 0:2 * NE].rearrange("p (t e) -> p t e", t=2), wide(rw("b_router"), 1, 2), ALU.add)
            step(tt(logit[0:TS, 2, :], ps[0:TS, 7, 2 * NE:3 * NE], rw("b_router", TS), ALU.add))
            for t in range(NT):
                ins = V.max(top[:, t, :], logit[:, t, :])
            step(ins)
            for t in range(NT):
                ins = V.max_index(topi[:, t, :].bitcast(U32), top[:, t, :], logit[:, t, :])
            step(ins)
            step(V.tensor_copy(topf, topi.bitcast(U32)))
            tt(topw[:, :, 0:TOPK], top[:, :, 0:TOPK], top[:, :, 0:1].to_broadcast([P, NT, TOPK]), ALU.subtract).then_inc(soft_in, 1)
            for t in range(NT):
                ins = tt(onehot[:, t * TOPK:(t + 1) * TOPK, :], wide(cn("iota", P, NE), 1, TOPK),
                         wide(topf[:, t, 0:TOPK], 2, NE), ALU.is_equal)
            step(ins)
            V.tensor_reduce(picked, onehot.rearrange("p (t k) e -> p t e k", t=NT), AX.X, ALU.add).then_inc(picks_ready, 1)
            dve.wait_ge(rank_mm, 1)
            dve.wait_ge(picks_ready, 1)
            for rows, a, b in ((P, 0, 2), (TS, 2, 3)):
                r = rank[0:rows, 0:NE, a:b].rearrange("p e t -> p t e")
                ins = V.scalar_tensor_tensor(r, ps[0:rows, 2, a * NE:b * NE].rearrange("p (t e) -> p t e", e=NE), 1.0,
                                             picked[0:rows, a:b, :], ALU.add, ALU.mult)
            ins.then_inc(rank_read, 1)
            dve.wait_ge(rank_read, 1)
            step(V.tensor_scalar(rank[:, 0:NE, 0:2], rank[:, 0:NE, 0:2], -1.0, None, ALU.add))
            step(V.tensor_scalar(rank[0:TS, 0:NE, 2:3], rank[0:TS, 0:NE, 2:3], -1.0, None, ALU.add))
            def blocks(bank):
                return ps[:, bank:bank + 2, :]

            def halves(name):
                return moe[name].rearrange("p (a b) -> p a b", a=2)

            def of(table, q):
                return lambda s, t, r: table[0:r, bass.ds(q * 2 + s, 1), t:t + 1].rearrange("p e t -> p (e t)")

            def select(q, place_of):
                for t, (t0, r) in enumerate(TILES):
                    for s in range(2):
                        ins = V.tensor_scalar(moe["sel"][0:r, t, s * CAP:(s + 1) * CAP], cn("iota", r, CAP),
                                              place_of(s, t, r), None, ALU.is_equal)
                ins.then_inc(sel_ready, 1)

            def select_weighted(q, place_of, weight_of):
                for t, (t0, r) in enumerate(TILES):
                    for s in range(2):
                        ins = V.tensor_scalar(moe["selw"][0:r, t, s * CAP:(s + 1) * CAP], cn("iota", r, CAP),
                                              place_of(s, t, r), weight_of(s, t, r), ALU.is_equal, ALU.mult)
                ins.then_inc(selw_ready, 1)

            def pick_bias(experts):
                for m in range(3):
                    for s in range(2):
                        ins = V.tensor_copy(moe["pick"][:, m, s * CAP:(s + 1) * CAP],
                                            cn("ident")[:, bass.ds(experts(s) + NE * m, 1)].to_broadcast([P, CAP]))
                ins.then_inc(pick_ready, 1)

            def activate(q):
                g, s = moe["g"], moe["s"]
                dve.wait_ge(exp_used, q * PER + 8)
                V.tensor_scalar(halves("g"), blocks(0), LIMIT, None, ALU.min).then_inc(g_ready, 1)
                dve.wait_ge(sig_ready, q + 1)
                step(tt(g, g, s, ALU.mult))
                dve.wait_ge(exp_used, q * PER + 16)
                step(V.tensor_scalar(halves("s"), blocks(2), LIMIT, -LIMIT, ALU.min, ALU.max))
                V.scalar_tensor_tensor(g, s, 1.0, g, ALU.add, ALU.mult).then_inc(act_ready, 1)

            def add_up(q):
                for m in range(KC):
                    dve.wait_ge(comb_mm, q * KC + (m + 1))
                    tt(acc[:, m, :], acc[:, m, :], ps[:, (2, 3, 6)[m % 3], 0:T], ALU.add).then_inc(comb_added, 1)

            OWN = 2
            select(0, of(rank, 0))
            dve.wait_ge(h_tr, NT)
            dve.wait_ge(router_mm, 1)
            pick_bias(lambda s: s)
            dve.wait_ge(soft_out, 1)
            step(V.tensor_reduce(den, topw[:, :, 0:TOPK], AX.X, ALU.add))
            step(V.reciprocal(den, den))
            step(tt(topw[:, :, 0:TOPK], topw[:, :, 0:TOPK], wide(den, 2, TOPK), ALU.mult))
            for t in range(NT):
                ins = tt(onew[:, t * TOPK:(t + 1) * TOPK, :], onehot[:, t * TOPK:(t + 1) * TOPK, :],
                         wide(topw[:, t, 0:TOPK], 2, NE), ALU.mult)
            step(ins)
            step(V.tensor_reduce(wgt[:, 0:NE, :].rearrange("p e t -> p t e"), onew.rearrange("p (t k) e -> p t e k", t=NT), AX.X, ALU.add))
            dve.wait_ge(cnt_mm, 1)
            V.tensor_tensor(flag[0:NE, :], ps[0:NE, 5, 0:1].to_broadcast([NE, PASSES - 1]), cn("thr", NE), ALU.is_gt).then_inc(flag_ready, 1)
            dve.wait_ge(place_mm, 1)
            V.tensor_copy(place[0:NE, :], ps[0:NE, 5, 8:8 + PASSES - 1]).then_inc(place_read, 1)
            dve.wait_ge(place_read, 1)
            dve.wait_ge(flag_ready, 1)
            for p in range(PASSES - 1):
                step(V.tensor_scalar(oh[0:NE, p, :], cn("iota", NE, LW), place[0:NE, p:p + 1], flag[0:NE, p:p + 1],
                                     ALU.is_equal, ALU.mult))
            tt(ohb[0:NE], oh[0:NE], wide(cn("thr", NE), 2, LW), ALU.mult).then_inc(oh_ready, 1)
            dve.wait_ge(more_mm, 1)
            V.tensor_copy(more_f, ps[:, 5, 32:32 + 3 * LW].rearrange("p (q j) -> p q j", q=3)).then_inc(more_read, 1)
            dve.wait_ge(more_read, 1)
            step(V.scalar_tensor_tensor(more_f[:, 1, :], more_f[:, 2, :], -FAR, more_f[:, 1, :], ALU.mult, ALU.add))
            step(V.tensor_scalar(more_f[:, 1, :], more_f[:, 1, :], FAR, None, ALU.add))
            V.tensor_copy(more_i, more_f).then_inc(more_ready, 1)
            V.memset(acc, 0.0).then_inc(moe_zero, 1)
            dve.wait_ge(moe_zero, 1)

            start = step.count

            def select_further(i):
                es = listed(dve, i)
                for s in range(2):
                    step(V.tensor_scalar(rk_more[:, s, :], rank[:, bass.ds(es[s], 1), :].rearrange("p e t -> p (e t)"),
                                         more_f[:, 1, bass.ds(i * 2 + s, 1)], None, ALU.subtract))
                select(i + PAIRS, of_more)

            def of_more(s, t, r):
                return rk_more[0:r, s, t:t + 1]

            def dve_turn(i):
                for j in range(UNROLL):
                    q = i * UNROLL + j
                    first, last = isinstance(q, int) and q == 0, isinstance(q, int) and q == PAIRS - 1
                    step.count, step.n = start + j * OWN + i * (UNROLL * OWN), 0
                    dve.wait_ge(x_mm, q + 1)
                    if last:
                        select_further(0)
                    else:
                        select(q + 1, of(rank, q + 1))
                    wait(dve, selT_tr, q)
                    select_weighted(q, of(rank, q), of(wgt, q))
                    activate(q)
                    if not first:
                        add_up(q - 1)
                    if not last:
                        dve.wait_ge(exp_used, q * PER + 17)
                        pick_bias(lambda s: (q + 1) * 2 + s)
                    assert step.n == (OWN + 2 if last else OWN)

            turns(dve.Fori, dve_turn)
            add_up(PAIRS - 1)
            start = start + PAIRS * OWN + 2

            def more_pair(i):
                straight = isinstance(i, int)
                step.count, step.n = start + (0 if straight else (i - 1) * (OWN + 2) + OWN), 0
                q = i + PAIRS
                dve.wait_ge(comb_mm, q * KC)
                if not straight:
                    select_further(i)
                es = listed(dve, i)
                select_weighted(q, of_more, lambda s, t, r: wgt[0:r, bass.ds(es[s], 1), t:t + 1].rearrange("p e t -> p (e t)"))
                pick_bias(lambda s: es[s])
                activate(q)
                add_up(q)
                assert step.n == (OWN if straight else OWN + 2)

            further_pairs(dve, there, more_pair)
            step = Steps(dve, sem("dve_tail_steps"))
            def prompt_chunk(m):
                return V.scalar_tensor_tensor(xT[:, m, 0:TP], acc[:, m, 0:TP], ada[:, GT_F, m, 0:1], xT[:, m, 0:TP],
                                              ALU.mult, ALU.add)

            step(prompt_chunk(0))
            prompt_chunk(1)
            xs_seq, acc_seq = by_seq(xT), by_seq(acc)
            step(tt(acc_seq, acc_seq, wide(ada[:, GT_F, :, 1:9], 3, SL), ALU.mult))
            tt(xs_seq, xs_seq, acc_seq, ALU.add).then_inc(f_sq_in, 1)
            for m in range(2, KC):
                prompt_chunk(m).then_inc(f_sq_in, 1)
            dve.wait_ge(f_sq_in, KC - 1)
            dve.wait_ge(meansq, 3)
            V.tensor_scalar(rstd, ps[:, 0, 0:T], 1.0 / D, EPS, ALU.mult, ALU.add).then_inc(var_ready, 1)
            dve.wait_ge(root_ready, 5)
            step(V.reciprocal(rstd, rstd))
            for m in range(KC):
                V.scalar_tensor_tensor(hT[:, m, :], xT[:, m, :], vc("g_final")[:, m:m + 1], rstd, ALU.mult, ALU.mult).then_inc(yfin, 1)

        @block.gpsimd
        def _(pool):
            Q = nc.gpsimd
            step = Steps(pool, pool_steps)
            step(Q.memset(line[:, :, 0:PAD], 0.0))
            step(Q.memset(cmask, 0.0))
            pool.wait_ge(ld_vec, 16)
            for m in range(KC):
                ins = Q.tensor_copy(line_seq(m, 0, PAD), prev[:, m * NSEQ:(m + 1) * NSEQ, :])
            ins.then_inc(line_ready, 1)
            pool.wait_ge(xbc_line, KC)
            step(Q.tensor_copy(cnew[:, :, 0:PAD], line[:, :, TP:TP + PAD]))
            for m in range(KC):
                step(Q.tensor_copy(cnew[:, m, PAD:].rearrange("p (b w) -> p b w", w=PAD), line_seq(m, SL, PAD)))
            pool.dma_start(out["convT"].rearrange("(c p) t -> p c t", p=P), cnew).then_inc(st_conv, 16)
            pool.wait_ge(xbc_ready, KC)
            for g in range(G):
                diag = cmask[:, g, :].rearrange("p (b w) -> p b w", w=TS + SL)[:, :, 0:SL]
                ins = Q.tensor_copy(diag, xbcT[:, 6 + g, TP:T].rearrange("p (b w) -> p b w", w=SL))
            ins.then_inc(cmask_ready, 1)
            pool.wait_ge(xb_tok, NT)
            pool.wait_ge(v_ready, 1)
            pool.wait_ge(ld_row, 16)
            for t, (t0, n) in enumerate(TILES):
                Q.tensor_tensor(cat[0:n, t, AW:D].rearrange("p (h e) -> p h e", h=H),
                                xs[0:n, t, :].rearrange("p (h e) -> p h e", h=H),
                                wide(rw("d_skip", n), 2, HD), ALU.mult).then_inc(skip_ready, 1)
            for g in range(G):
                ins = Q.tensor_tensor(bmask[0:TS, g], wide(btok[0:TS, 2, g * P:(g + 1) * P], 1, NSEQ),
                                      wide(cn("seq", TS), 2, P), ALU.mult)
            ins.then_inc(bmask_ready, 1)
            pool.dma_start(out["v"], vg[0:TS, 2, :]).then_inc(st_v, 16)
            pool.wait_ge(y_mm, 1)
            pool.wait_ge(decays, 1)
            s0h = s0T.rearrange("p b (h e) -> p (b h) e", e=HD)
            step(Q.tensor_tensor(s0h, s0h, wide(dec[:, 64:128], 2, HD), ALU.mult))
            pool.wait_ge(st1_ready, 1)
            pool.dma_start(out["ssmpT"], st1).then_inc(st_ssmp, 16)
            for b in range(NSEQ):
                pool.wait_ge(sn_copied, b + 1)
                Q.tensor_tensor(s0T[:, b, :], s0T[:, b, :], snew[:, b % 2, :], ALU.add).then_inc(sn_added, 1)
            pool.wait_ge(sn_added, NSEQ)
            pool.dma_start(out["ssmsT"], s0T).then_inc(st_ssms, 16)
            pool.wait_ge(st_ssms, 16)
            pool.wait_ge(st_ssmp, 16)
            pool.wait_ge(st_v, 16)
            pool.wait_ge(st_conv, 16)


def kernel(**inputs):
    import concourse.bacc as bacc
    from concourse.bass_utils import run_bass_kernel_spmd

    a = {k: np.asarray(v) for k, v in inputs.items()}

    def feat(x):
        x = x.reshape(-1, x.shape[-1] // P, P)
        return x

    def chunk_first(x):
        return feat(x).transpose(2, 1, 0).reshape(P, -1)

    def row_first(x):
        return feat(x).transpose(2, 0, 1).reshape(P, -1)

    x = np.concatenate([a["x_prompt"].reshape(-1, D), a["x_sample"].reshape(-1, D)])
    c = np.concatenate([a["c_prompt"], a["c_sample"]])
    b_sp = a["b_spatial"][0].T
    parts = {
        "c": chunk_first(c), "b_ada": row_first(a["b_ada"]), "g_mix": row_first(a["g_mix"]), "g_ffn": row_first(a["g_ffn"]),
        "g_final": row_first(a["g_final"][None]),
        "g_cat": row_first(np.concatenate([a["g_out_a"], a["g_out_b"]], axis=1)),
        "conv_w": row_first(a["conv_w"][0]), "conv_b": row_first(a["conv_b"]),
        "b_exp": np.concatenate([a["b_gate"][0], a["b_up"][0], a["b_down"][0], np.zeros((P - 3 * NE, D), np.float32)]),
        "w_router": a["w_router"][0].reshape(KC, P, NE).transpose(1, 0, 2).reshape(P, -1),
        "w_dt": a["w_in"][0][:, IN_DIM - H:].reshape(KC, P, H).transpose(1, 0, 2).reshape(P, -1),
        "w_sp": a["w_spatial"][0].transpose(2, 0, 1).reshape(P, -1), "b_sp": b_sp,
        "prev": chunk_first(a["state_conv"][0].reshape(NSEQ * PAD, D)),
    }
    vec = np.concatenate([parts[n] for n in VEC], axis=1)
    row = np.concatenate([a[n].reshape(1, -1) for n in ("g_v_a", "dt_bias", "a_log", "d_skip", "b_router")], axis=1)
    arrays = {
        "xT": x.T, "vec": vec, "row": row, "con": constants(),
        "s0T": a["state_ssm"][0].reshape(NSEQ, AW, P).transpose(2, 0, 1),
        "w_in": a["w_in"][0], "w_ada": a["w_ada"][0], "w_out": a["w_out"][0],
        "w_gate": a["w_gate"][0], "w_up": a["w_up"][0], "w_down": a["w_down"][0],
    }
    arrays = {k: np.ascontiguousarray(v) for k, v in arrays.items()}
    nc = bacc.Bacc("TRN2", target_bir_lowering=False, num_devices=1)
    d = {k: nc.dram_tensor(f"in_{k}", v.shape, F32, kind="ExternalInput").ap() for k, v in arrays.items()}
    shapes = {"yT": (D, T), "convT": (D, PAD * (1 + NSEQ)), "v": (TS, AW), "ssmpT": (P, AW), "ssmsT": (P, NSEQ, AW)}
    out = {k: nc.dram_tensor(f"out_{k}", s, F32, kind="ExternalOutput").ap() for k, s in shapes.items()}
    build(nc, d, out)
    r = run_bass_kernel_spmd(nc, [{f"in_{k}": v for k, v in arrays.items()}], core_ids=[0]).results[0]
    y = r["out_yT"].T
    conv = r["out_convT"].T
    return (
        np.ascontiguousarray(y[:TP]).reshape(1, TP, D),
        np.ascontiguousarray(y[TP:]).reshape(NSEQ, SL, D),
        np.ascontiguousarray(r["out_ssmpT"].T).reshape(1, 1, H, HD, P),
        np.ascontiguousarray(conv[:PAD]).reshape(1, 1, PAD, D),
        np.ascontiguousarray(r["out_ssmsT"].transpose(1, 2, 0)).reshape(1, NSEQ, H, HD, P),
        np.ascontiguousarray(conv[PAD:]).reshape(1, NSEQ, PAD, D),
        np.ascontiguousarray(r["out_v"]).reshape(1, NSEQ, SL, AW),
    )
```
